# Optimizing a Trainium2 kernel written in Bass

```python
import math
import jax, jax.numpy as jnp
from jax import lax
import numpy as np

D_MODEL = 1024
BATCH = 1
SEQ = 512
DEPTH = 1
DEC_BATCH = 8
DEC_SEQ = 4
PAST_LEN = 4096
PAGE_SIZE = 128

RET_HEADS = 4
RET_QK_DIM = D_MODEL // 8
RET_V_DIM = D_MODEL // 4
RET_CHUNK = 128
RET_THETA = 10000.0
RET_QK = RET_HEADS * RET_QK_DIM
RET_V = RET_HEADS * RET_V_DIM
ATT_GROUPS = ((128, 1), (512, 4), (2048, 16))
N_GROUPS = 3
ATT_HEADS = 4
ATT_HEAD_DIM = 64
ROPE_DIM = ATT_HEAD_DIM // 4
ROPE_THETA = 500000.0
BAND_BLOCK = 128
ATT_W = N_GROUPS * ATT_HEADS * ATT_HEAD_DIM
ATT_OUT = ATT_HEADS * ATT_HEAD_DIM
D_FF = 2816
CONV_W = 3
EPS = 1e-6
IN_WIDTHS = (RET_QK, RET_QK, RET_V, RET_V, ATT_W, ATT_W, ATT_W, D_MODEL, D_MODEL)
D_IN = 2 * RET_QK + 2 * RET_V + 3 * ATT_W + 2 * D_MODEL

kernel_name = 'hybrid_retention_dilated_attn_convffn_step'

F32 = jnp.float32

def rms_norm(x, g):
    xf = x.astype(F32)
    y = xf * lax.rsqrt(jnp.mean(xf * xf, axis=-1, keepdims=True) + EPS)
    return (y * g.astype(F32)).astype(x.dtype)

def rotary(x, pos, inv_freq):
    half = inv_freq.shape[0]
    rot = 2 * half
    ang = pos.astype(F32)[:, None] * inv_freq[None, :]
    cos = jnp.cos(ang)[:, None, :]
    sin = jnp.sin(ang)[:, None, :]
    xf = x[..., :rot].astype(F32)
    x1, x2 = xf[..., :half], xf[..., half:]
    r = jnp.concatenate([x1 * cos - x2 * sin, x2 * cos + x1 * sin], axis=-1).astype(x.dtype)
    return jnp.concatenate([r, x[..., rot:]], axis=-1)

def ret_inv_freq():
    return RET_THETA ** (-jnp.linspace(0.0, 1.0, RET_QK_DIM // 2, dtype=F32))

def att_inv_freq():
    half = ROPE_DIM // 2
    return ROPE_THETA ** (-jnp.arange(half, dtype=F32) / half)

def retention_log_decay():
    return jnp.log1p(-jnp.exp2(-5.0 - jnp.arange(RET_HEADS, dtype=F32)))

def split_columns(t, widths):
    out, start = [], 0
    for wd in widths:
        out.append(t[..., start:start + wd])
        start += wd
    return out

def mixer_projections(h, w_in, pos):
    B, T, _ = h.shape
    rq, rk, rv, rg, aq, ak, av, gr, ga = split_columns(h @ w_in, IN_WIDTHS)
    rf = ret_inv_freq()
    rq = rotary(rq.reshape(B, T, RET_HEADS, RET_QK_DIM), pos, rf)
    rk = rotary(rk.reshape(B, T, RET_HEADS, RET_QK_DIM), pos, rf) * RET_QK_DIM ** -0.5
    rv = rv.reshape(B, T, RET_HEADS, RET_V_DIM)
    af = att_inv_freq()
    na = N_GROUPS * ATT_HEADS
    gshape = (B, T, N_GROUPS, ATT_HEADS, ATT_HEAD_DIM)
    aq = rotary(aq.reshape(B, T, na, ATT_HEAD_DIM), pos, af).reshape(gshape) * ATT_HEAD_DIM ** -0.5
    ak = rotary(ak.reshape(B, T, na, ATT_HEAD_DIM), pos, af).reshape(gshape)
    av = av.reshape(gshape)
    return rq, rk, rv, rg, aq, ak, av, gr, ga

def retention_chunk(q, k, v, s0, log_gamma):
    C = q.shape[1]
    qf, kf, vf = q.astype(F32), k.astype(F32), v.astype(F32)
    idx = jnp.arange(C, dtype=F32)
    diff = idx[:, None] - idx[None, :]
    decay = jnp.where(diff[None] >= 0, jnp.exp(log_gamma[:, None, None] * jnp.maximum(diff, 0.0)[None]), 0.0)
    scores = jnp.einsum('bihd,bjhd->bhij', qf, kf) * decay[None]
    o = jnp.einsum('bhij,bjhe->bihe', scores, vf)
    q_dec = jnp.exp(log_gamma[None, :] * (idx[:, None] + 1.0))
    o = o + jnp.einsum('bihd,bhde->bihe', qf, s0) * q_dec[None, :, :, None]
    k_dec = jnp.exp(log_gamma[None, :] * (C - 1.0 - idx)[:, None])
    s1 = s0 * jnp.exp(log_gamma * C)[None, :, None, None] + jnp.einsum('bjhd,bjhe->bhde', kf * k_dec[None, :, :, None], vf)
    return o, s1

def retention_prompt(q, k, v, log_gamma):
    B, S, H, dk = q.shape
    dv = v.shape[-1]
    C = min(RET_CHUNK, S)
    n = S // C

    def chunks(t):
        return t.reshape(B, n, C, H, t.shape[-1]).swapaxes(0, 1)

    def step(s, qkv):
        o, s_new = retention_chunk(qkv[0], qkv[1], qkv[2], s, log_gamma)
        return s_new, o

    s_fin, o = lax.scan(step, jnp.zeros((B, H, dk, dv), F32), (chunks(q), chunks(k), chunks(v)))
    return o.swapaxes(0, 1).reshape(B, S, H, dv), s_fin

def band_attention(q, k, v, span):
    N, L, H, Dh = q.shape
    blk = BAND_BLOCK
    nb = -(-L // blk)
    Lp = nb * blk
    qb = jnp.pad(q.astype(F32), ((0, 0), (0, Lp - L), (0, 0), (0, 0))).reshape(N, nb, blk, H, Dh)

    def kv_blocks(t):
        tp = jnp.pad(t.astype(F32), ((0, 0), (blk, Lp - L), (0, 0), (0, 0))).reshape(N, nb + 1, blk, H, Dh)
        return jnp.concatenate([tp[:, :-1], tp[:, 1:]], axis=2)

    kb, vb = kv_blocks(k), kv_blocks(v)
    s = jnp.einsum('nbqhd,nbkhd->nbhqk', qb, kb)
    qi = jnp.arange(blk)[:, None]
    kj = jnp.arange(2 * blk)[None, :]
    dist = qi - kj + blk
    kpos = jnp.arange(nb)[:, None, None] * blk + kj[None] - blk
    mask = (dist[None] >= 0) & (dist[None] <= span) & (kpos >= 0)
    s = jnp.where(mask[None, :, None], s, -jnp.inf)
    m = jnp.max(s, axis=-1, keepdims=True)
    p = jnp.exp(s - m)
    den = jnp.sum(p, axis=-1, keepdims=True)
    o = jnp.einsum('nbhqk,nbkhd->nbqhd', p / den, vb).reshape(N, Lp, H, Dh)[:, :L]
    lse = (m + jnp.log(den))[..., 0].transpose(0, 1, 3, 2).reshape(N, Lp, H)[:, :L]
    return o, lse

def dilated_prompt(q, k, v, window, dil):
    B, S, H, Dh = q.shape
    L = S // dil

    def split(t):
        return t.reshape(B, L, dil, H, Dh).transpose(0, 2, 1, 3, 4).reshape(B * dil, L, H, Dh)

    o, lse = band_attention(split(q), split(k), split(v), window // dil)
    o = o.reshape(B, dil, L, H, Dh).transpose(0, 2, 1, 3, 4).reshape(B, S, H, Dh)
    lse = lse.reshape(B, dil, L, H).transpose(0, 2, 1, 3).reshape(B, S, H)
    return o, lse

def dilated_sample(q, k_new, v_new, buf, window, dil):
    T = q.shape[1]
    Wb = buf.shape[1]
    buf = buf.astype(k_new.dtype)
    kf = jnp.concatenate([buf[:, :, 0], k_new], axis=1)
    vf = jnp.concatenate([buf[:, :, 1], v_new], axis=1)
    nk = window // dil + 1
    idx = Wb + jnp.arange(T)[:, None] - dil * jnp.arange(nk)[None, :]
    valid = idx >= 0
    idxc = jnp.maximum(idx, 0)
    kg = kf[:, idxc].astype(F32)
    vg = vf[:, idxc].astype(F32)
    s = jnp.einsum('bthd,btkhd->bthk', q.astype(F32), kg)
    s = jnp.where(valid[None, :, None, :], s, -jnp.inf)
    m = jnp.max(s, axis=-1, keepdims=True)
    p = jnp.exp(s - m)
    den = jnp.sum(p, axis=-1, keepdims=True)
    o = jnp.einsum('bthk,btkhd->bthd', p / den, vg)
    lse = (m + jnp.log(den))[..., 0]
    new_buf = jnp.concatenate([buf, jnp.stack([k_new, v_new], axis=2)], axis=1)[:, -Wb:]
    return o, lse, new_buf

def merge_branches(ret_o, ret_gate, att_o, gate_r, gate_a, w_branch_ret, w_branch_attn, w_out, dtype):
    B, T = ret_o.shape[:2]
    of = ret_o.astype(F32)
    on = of * lax.rsqrt(jnp.mean(of * of, axis=-1, keepdims=True) + EPS)
    r = on.reshape(B, T, RET_V).astype(dtype) * jax.nn.silu(ret_gate)
    br = r @ w_branch_ret
    ba = att_o.reshape(B, T, ATT_OUT).astype(dtype) @ w_branch_attn
    mix = jax.nn.sigmoid(gate_r) * br + jax.nn.sigmoid(gate_a) * ba
    return mix @ w_out

def conv_ffn(h, conv_state, w_ffn_up, conv_w, conv_b, w_ffn_down):
    u = h @ w_ffn_up
    T = u.shape[1]
    ext = jnp.concatenate([conv_state.astype(u.dtype), u], axis=1)
    c = conv_b + sum(conv_w[i] * ext[:, i:i + T] for i in range(CONV_W))
    g, val = c[..., :D_FF], c[..., D_FF:]
    f = (jax.nn.gelu(g, approximate=True) * val) @ w_ffn_down
    return f, ext[:, -(CONV_W - 1):]

def trunk_layer(x, pos, state, norm_mix_pre, w_in, w_branch_ret, w_branch_attn, w_out, norm_mix_post,
                norm_ffn_pre, w_ffn_up, conv_w, conv_b, w_ffn_down, norm_ffn_post):
    B, T, _ = x.shape
    h = rms_norm(x, norm_mix_pre)
    rq, rk, rv, rg, aq, ak, av, gr, ga = mixer_projections(h, w_in, pos)
    log_gamma = retention_log_decay()
    if state is None:
        ret_o, ret_state = retention_prompt(rq, rk, rv, log_gamma)
        conv_state = jnp.zeros((B, CONV_W - 1, 2 * D_FF), x.dtype)
        kv_bufs = None
    else:
        kv_bufs = state[:3]
        ret_o, ret_state = retention_chunk(rq, rk, rv, state[3].astype(F32), log_gamma)
        conv_state = state[4]
    outs, lses, new_bufs = [], [], []
    for g, (win, dil) in enumerate(ATT_GROUPS):
        q_g, k_g, v_g = aq[:, :, g], ak[:, :, g], av[:, :, g]
        if state is None:
            o_g, l_g = dilated_prompt(q_g, k_g, v_g, win, dil)
            buf = jnp.stack([k_g, v_g], axis=2)[:, -min(win, T):]
        else:
            o_g, l_g, buf = dilated_sample(q_g, k_g, v_g, kv_bufs[g], win, dil)
        outs.append(o_g)
        lses.append(l_g)
        new_bufs.append(buf)
    wts = jax.nn.softmax(jnp.stack(lses, axis=0), axis=0)
    att_o = jnp.einsum('gbth,gbthd->bthd', wts, jnp.stack(outs, axis=0))
    mix = merge_branches(ret_o, rg, att_o, gr, ga, w_branch_ret, w_branch_attn, w_out, x.dtype)
    x = x + rms_norm(mix, norm_mix_post)
    f, conv_new = conv_ffn(rms_norm(x, norm_ffn_pre), conv_state, w_ffn_up, conv_w, conv_b, w_ffn_down)
    x = x + rms_norm(f, norm_ffn_post)
    return x, (new_bufs[0], new_bufs[1], new_bufs[2], ret_state.astype(x.dtype), conv_new)

def setup_inputs(seed: int = 0) -> dict:
    key = jax.random.key(seed)
    ks = jax.random.split(key, 24)
    nrm = jax.random.normal
    L = DEPTH

    def gain(k):
        return 1.0 + 0.02 * nrm(k, (L, D_MODEL), F32)

    def win_len(w):
        return min(w, PAST_LEN)

    return {
        'x_prompt': nrm(ks[0], (BATCH, SEQ, D_MODEL), F32),
        'x_sample': nrm(ks[1], (DEC_BATCH, DEC_SEQ, D_MODEL), F32),
        'cache_kv_g0': nrm(ks[2], (L, DEC_BATCH, win_len(ATT_GROUPS[0][0]), 2, ATT_HEADS, ATT_HEAD_DIM), F32),
        'cache_kv_g1': nrm(ks[3], (L, DEC_BATCH, win_len(ATT_GROUPS[1][0]), 2, ATT_HEADS, ATT_HEAD_DIM), F32),
        'cache_kv_g2': nrm(ks[4], (L, DEC_BATCH, win_len(ATT_GROUPS[2][0]), 2, ATT_HEADS, ATT_HEAD_DIM), F32),
        'state_ret': 0.5 * nrm(ks[5], (L, DEC_BATCH, RET_HEADS, RET_QK_DIM, RET_V_DIM), F32),
        'state_conv': nrm(ks[6], (L, DEC_BATCH, CONV_W - 1, 2 * D_FF), F32),
        'norm_mix_pre': gain(ks[7]),
        'w_in': nrm(ks[8], (L, D_MODEL, D_IN), F32) * D_MODEL ** -0.5,
        'w_branch_ret': nrm(ks[9], (L, RET_V, D_MODEL), F32) * RET_V ** -0.5,
        'w_branch_attn': nrm(ks[10], (L, ATT_OUT, D_MODEL), F32) * ATT_OUT ** -0.5,
        'w_out': nrm(ks[11], (L, D_MODEL, D_MODEL), F32) * D_MODEL ** -0.5,
        'norm_mix_post': gain(ks[12]),
        'norm_ffn_pre': gain(ks[13]),
        'w_ffn_up': nrm(ks[14], (L, D_MODEL, 2 * D_FF), F32) * D_MODEL ** -0.5,
        'conv_w': nrm(ks[15], (L, CONV_W, 2 * D_FF), F32) * CONV_W ** -0.5,
        'conv_b': 0.02 * nrm(ks[16], (L, 2 * D_FF), F32),
        'w_ffn_down': nrm(ks[17], (L, D_FF, D_MODEL), F32) * D_FF ** -0.5,
        'norm_ffn_post': gain(ks[18]),
    }

def reference(x_prompt, x_sample, cache_kv_g0, cache_kv_g1, cache_kv_g2, state_ret, state_conv,
              norm_mix_pre, w_in, w_branch_ret, w_branch_attn, w_out, norm_mix_post,
              norm_ffn_pre, w_ffn_up, conv_w, conv_b, w_ffn_down, norm_ffn_post):
    pos_p = jnp.arange(x_prompt.shape[1])
    pos_s = PAST_LEN + jnp.arange(x_sample.shape[1])
    hp, hs = x_prompt, x_sample
    new_p = [[], [], [], [], []]
    new_s = [[], [], [], [], []]
    for l in range(DEPTH):
        w = (norm_mix_pre[l], w_in[l], w_branch_ret[l], w_branch_attn[l], w_out[l], norm_mix_post[l],
             norm_ffn_pre[l], w_ffn_up[l], conv_w[l], conv_b[l], w_ffn_down[l], norm_ffn_post[l])
        hp, st_p = trunk_layer(hp, pos_p, None, *w)
        st_in = (cache_kv_g0[l], cache_kv_g1[l], cache_kv_g2[l], state_ret[l], state_conv[l])
        hs, st_s = trunk_layer(hs, pos_s, st_in, *w)
        for lst, a in zip(new_p, st_p):
            lst.append(a)
        for lst, a in zip(new_s, st_s):
            lst.append(a)
    p_kv_g0, p_kv_g1, p_kv_g2, p_ret, p_conv = [jnp.stack(a, axis=0) for a in new_p]
    s_kv_g0, s_kv_g1, s_kv_g2, s_ret, s_conv = [jnp.stack(a, axis=0) for a in new_s]
    return (hp, hs, p_kv_g0, p_kv_g1, p_kv_g2, p_ret, p_conv, s_kv_g0, s_kv_g1, s_kv_g2, s_ret, s_conv)


_drawn_inputs = setup_inputs


def setup_inputs(seed=0):
    import zlib

    import numpy as np

    out = dict(_drawn_inputs(seed))
    spreads = {}
    factors = {'norm_mix_post': 3.51, 'norm_ffn_pre': 2.754, 'conv_b': 3.427, 'norm_ffn_post': 5.004}
    for name, (base, spread) in spreads.items():
        noise = np.random.default_rng([zlib.crc32(name.encode()), seed]).standard_normal(out[name].shape)
        drawn = base * np.exp(spread * noise) if base else spread * noise
        out[name] = __import__('jax').numpy.asarray(drawn.astype(out[name].dtype))
    for name, factor in factors.items():
        out[name] = (out[name] * factor).astype(out[name].dtype)
    return out
```

```python
import math
from contextlib import ExitStack

import numpy as np
import concourse.bass as bass
from concourse import mybir

D = 1024
KT = D // 128
SEQ = 512
NB = 8
DT = 4
TS = NB * DT
NTOK = SEQ + TS
HALF = NTOK // 2
TILES = 5
PAST = 4096
RH, DK, DV, CHUNK = 4, 128, 256, 128
GROUPS = ((128, 1), (512, 4), (2048, 16))
NG, AH, HD = 3, 4, 64
DFF = 2816
FT = DFF // 128
EPS = 1e-6
SLOT = 1024
NEG = -1e30

S_RET, S_ATT, S_RG, S_GB, S_GA, S_BA = 0, 16, 34, 42, 58, 66
S_OUT = S_BA + 8
S_UP = S_OUT + 8
S_DN = S_UP + 2 * FT
NSLOT = S_DN + FT
BA_W = 256

BLOCKS = ([(S_RET + 4 * n, 4, 2, 512) for n in range(4)] + [(S_ATT + 4 * n, 4, 2, 512) for n in range(4)]
          + [(S_ATT + 16, 2, 4, 256)] + [(S_RG + 4 * n, 4, 2, 512) for n in range(2)]
          + [(S_OUT + 4 * n, 4, 2, 512) for n in range(2)] + [(S_DN + 11 * n, 11, 2, 512) for n in range(2)])
BLK_RQ, BLK_RK, BLK_RV, BLK_AQ, BLK_AQK, BLK_AK, BLK_AV, BLK_AV2, BLK_RG, BLK_OUT, BLK_DN = 0, 1, 2, 4, 5, 6, 7, 8, 9, 11, 13
ROPE_BLOCKS = (BLK_RQ, BLK_RK, BLK_AQ, BLK_AQK, BLK_AK)


def rows(i):
    return 128 if i < 4 else TS


def cols(i):
    return slice(128 * i, 128 * i + rows(i))


def attention_blocks(qb):
    return ([(1, kb) for kb in range(qb + 1)] + [(2, kb) for kb in range(qb + 1)]
            + [(0, kb) for kb in range(max(qb - 1, 0), qb + 1)])


def turns(s):
    return -(-len(attention_blocks(s // 4)) // 4)


def psum_uses():
    order = []
    for i in range(TILES):
        for half in range(2):
            order.append((("x", i, half), 5 + (2 * i + half) % 3))
    turned = lambda b: [(("t", b, i), 5 + i % 3) for i in range(TILES)]
    order += turned(BLK_RQ) + turned(BLK_RK)
    for c in range(4):
        order.append((("S", c), 5))
        if c:
            order += turned(BLK_AQ + c - 1)
        order += [(("O", c, 0), 6), (("O", c, 1), 7), (("U", c, 0), 5), (("U", c, 1), 5)]
    order.append((("Ss",), 5))
    for h in range(RH):
        order += [(("Us", h, p), (5, 7)[p % 2]) for p in range(4)] + [(("Os", h), 6)]
    for g in range(2):
        order += [(("r", g, i), 5 + i % 3) for i in range(TILES)]
    order += [(("s", 0, g), 4 + g) for g in range(NG)]
    for st in range(17):
        if st:
            order += [(("pt", st - 1, j), 4 + j) for j in range(turns(st - 1))]
            if st % 2 == 0:
                order.append((("o", st // 2 - 1), 7))
        if st < 15:
            order += [(("s", st + 1, g), 4 + g) for g in range(NG)]
    order += [(("st",), 4), (("sn",), 5), (("sp",), 6), (("spn",), 4), (("sv",), 7), (("so",), 5)]
    for i in range(TILES):
        for half in range(2):
            order.append((("h2", i, half), 5 + (2 * i + half) % 3))
    order += [(("cv", j), 5 + j % 3) for j in range(2 * FT // 4)]
    seen, out = {}, {}
    for key, bank in order:
        out[key] = (bank, seen.get(bank, 0))
        seen[bank] = seen.get(bank, 0) + 1
    return out


USES = psum_uses()
SPLIT_KEYS = [k for k in USES if k[0] in ("x", "r", "h2")]
SPLIT_NO = {k: n for n, k in enumerate(SPLIT_KEYS)}


CA_FIELDS = (("ident", 128), ("acos", TILES * 16), ("asin", TILES * 16), ("mask1", 512), ("mask2", 512),
             ("mask0", 256), ("ms0", 128), ("mnew", NG * 32), ("hsel", 4))
CR_FIELDS = (("rcos", TILES * 64), ("rsin", TILES * 128), ("decT", RH * 128), ("qdec", RH * 128), ("kdec", RH),
             ("decTs", RH * 32), ("qdecs", RH * 32), ("kdecs", RH * NB))


def places(fields):
    out, at = {}, 0
    for name, n in fields:
        out[name] = (at, n)
        at += n
    return out, at


CA_AT, CA_N = places(CA_FIELDS)
CR_AT, CR_N = places(CR_FIELDS)


def constant_tables():
    f32 = np.float32
    ca, cr = np.zeros((128, CA_N), f32), np.zeros((128, CR_N), f32)

    def put(a, at, name, v):
        o, n = at[name]
        v = np.asarray(v, np.float64)
        a[:v.shape[0], o:o + n] = v.reshape(v.shape[0], n).astype(f32)

    pos = np.zeros((TILES, 128), f32)
    pos[:4] = np.arange(SEQ).reshape(4, 128)
    pos[4, :TS] = PAST + np.arange(TS) % DT
    af = (np.float64(500000.0) ** (-(np.arange(8, dtype=f32) / f32(8)).astype(np.float64))).astype(f32)
    ang = (pos[:, :, None] * af).astype(f32).astype(np.float64)
    put(ca, CA_AT, "acos", np.concatenate([np.cos(ang), np.cos(ang)], -1).transpose(1, 0, 2))
    put(ca, CA_AT, "asin", np.concatenate([-np.sin(ang), np.sin(ang)], -1).transpose(1, 0, 2))
    rf = (np.float64(10000.0) ** (-(np.arange(64, dtype=f32) * f32(1 / 63)).astype(np.float64))).astype(f32)
    ang = (pos[:, :, None] * rf).astype(f32).astype(np.float64)
    put(cr, CR_AT, "rcos", np.cos(ang).transpose(1, 0, 2))
    put(cr, CR_AT, "rsin", np.concatenate([-np.sin(ang), np.sin(ang)], -1).transpose(1, 0, 2))
    put(ca, CA_AT, "ident", np.eye(128))
    i, j = np.arange(128)[:, None], np.arange(128)[None, :]
    for name, dil in (("mask1", 4), ("mask2", 16)):
        off = np.where((i - j) % dil == 0, 0.0, NEG)
        diag = np.where(((i - j) % dil == 0) & (j <= i), 0.0, NEG)
        put(ca, CA_AT, name, np.concatenate([off, off, off, diag], 1))
    put(ca, CA_AT, "mask0", np.concatenate([np.where(j >= i, 0.0, NEG), np.where(j <= i, 0.0, NEG)], 1))
    p = np.arange(128)
    b, t, h = p // 16, p // 4 % 4, p % 4
    put(ca, CA_AT, "ms0", np.where(j >= t[:, None], 0.0, NEG))
    kb, kt = np.arange(TS)[None] // 4, np.arange(TS)[None] % 4
    same = kb == b[:, None]
    m0 = np.where(same & (kt <= t[:, None]), 0.0, NEG)
    m1 = np.where(same & (kt == t[:, None]), 0.0, NEG)
    put(ca, CA_AT, "mnew", np.stack([m0, m1, m1], 1))
    put(ca, CA_AT, "hsel", (h[:, None] == np.arange(4)[None]).astype(f32))
    lg = log_decay()
    dec = np.where(j[None] >= i[None], np.exp(lg[:, None, None] * np.maximum(j - i, 0)[None]), 0.0)
    put(cr, CR_AT, "decT", dec.transpose(1, 0, 2))
    put(cr, CR_AT, "qdec", np.broadcast_to(np.exp(lg[:, None] * (np.arange(128) + 1.0))[None], (128, 4, 128)))
    put(cr, CR_AT, "kdec", np.exp(lg[None] * (127.0 - np.arange(128))[:, None]))
    sj, si = np.arange(TS)[:, None], np.arange(TS)[None, :]
    ok = (sj // 4 == si // 4) & (sj <= si)
    dec = np.where(ok[None], np.exp(lg[:, None, None] * np.maximum(si - sj, 0)[None]), 0.0)
    put(cr, CR_AT, "decTs", dec.transpose(1, 0, 2))
    put(cr, CR_AT, "qdecs", np.broadcast_to(np.exp(lg[:, None] * (np.arange(TS) % 4 + 1.0))[None], (128, 4, TS)))
    kd = np.exp(lg[None] * (3.0 - np.arange(TS) % 4)[:, None])
    put(cr, CR_AT, "kdecs", kd[:, :, None] * (np.arange(TS)[:, None, None] // 4 == np.arange(NB)[None, None]))
    return ca, cr


def log_decay():
    return np.log1p(-np.exp2(-5.0 - np.arange(RH)))


GAMMA_CHUNK = [float(x) for x in np.exp(log_decay() * CHUNK)]
GAMMA_STEP = [float(x) for x in np.exp(log_decay() * DT)]


def build_layer(nc, a, o, phases=99):
    F, R = mybir.dt.float32, mybir.dt.float32r
    ALU, ACT, AX = mybir.AluOpType, mybir.ActivationFunctionType, mybir.AxisListType
    ctx = ExitStack()

    base = 16512

    def sb(name, at, shape, dt=F):
        return nc.alloc_sbuf_tensor_at(name, shape, dt, offset=base + 4 * at)

    T1h = sb("T1h", 0, [128, KT, NTOK], R)
    T1l = sb("T1l", 4352, [128, KT, NTOK], R)
    T1s = sb("T1s", 8704, [128, KT, 64], R)
    wraw = sb("wraw", 9216, [128, 2, SLOT])
    whi = sb("whi", 11264, [128, 2, SLOT], R)
    wlo = sb("wlo", 13312, [128, 2, SLOT], R)
    CA0 = 15360
    ca_t = sb("ca", CA0, [128, CA_N])
    CONVP = CA0 + (CA_N + 7) // 8 * 8
    convp = sb("convp", CONVP, [128, 2 * FT, 4])
    STAT = CONVP + 8 * FT
    stat = sb("stat", STAT, [128, 136])
    col = lambda n, w: stat[:, n:n + w]
    ss_x, rt_x, rs_x = (col(5 * k, 5) for k in range(3))
    ss_r, rt_r, rs_r = (col(16 + 20 * k, 20) for k in range(3))
    mx = col(76, 8).rearrange("p (a b) -> p a b", a=2)
    nm, den, rden = col(84, 2), col(86, 2), col(88, 2)
    ss_n, rt_n, rs_n = (col(90 + 15 * k, 15) for k in range(3))
    eps = col(135, 1)
    assert CR_N <= 2304
    X = (STAT + 136 + 7) // 8 * 8
    ATT = X + 17168
    SCR = ATT + 10368
    END = (229368 - base) // 4
    assert SCR + 8200 <= END, (SCR, END)
    cr_t = sb("cr", X, [128, CR_N])
    QT = X + 2304
    qT = sb("qT", QT, [128, RH, NTOK])
    kT = sb("kT", QT + 2176, [128, RH, NTOK])
    RBk = sb("rope_k", QT + 4352, [128, TILES, 512])
    V0 = QT + 6912
    vt = sb("v", V0, [128, 4, D])
    vs = sb("v_s", V0 + 4096, [128, D])
    RBq = sb("rope_q", V0 + 5120, [128, TILES, 512])
    assert V0 + 7680 <= ATT
    aqT = sb("aqT", ATT, [128, 6, NTOK])
    akT = sb("akT", ATT + 3264, [128, 6, NTOK])
    av = sb("av", ATT + 6528, [128, 4, 768])
    avs = sb("av_s", ATT + 9600, [128, 768])
    xin = sb("xin", ATT, [128, TILES, D])
    gpre = sb("gpre", ATT + 5120, [128, D])
    xn = sb("xn", ATT + 6144, [128, 2, D])
    junk = sb("junk", ATT + 8192, [128, D])
    at = SCR
    tmp_s = sb("tmp_s", at, [128, 512]); at += 512
    ropet = sb("ropet", at, [128, 2, 512]); at += 1024
    PT = sb("PT", at, [128, RH, 128]); at += 512
    kd = sb("kd", at, [128, 512]); at += 512
    qd = sb("qd", at, [128, RH, 128]); at += 512
    state = sb("state", at, [128, RH, DV]); at += 1024
    S0 = sb("S0", at, [128, 3, 2, DV]); at += 1536
    qm = sb("qm", at, [128, 2, NB, 32]); at += 512
    km = sb("km", at, [128, NB, 128]); at += 1024
    rjunk = sb("rjunk", at, [128, DV]); at += 256
    PTs = sb("PTs", at, [128, RH, 32]); at += 128
    assert at <= END, (at, END)
    rTh = sb("rTh", X, [128, KT, NTOK], R)
    rTl = sb("rTl", X + 4352, [128, KT, NTOK], R)
    rTs = sb("rTs", X + 8704, [128, KT, 64], R)
    assert X + 9216 <= V0
    etmp = sb("etmp", SCR + 512, [128, 2, 512])
    mixr = sb("mixr", V0, [128, KT, NTOK])
    gexp = sb("gexp", V0 + 5120, [128, 2, NTOK])
    at = SCR
    sc = sb("sc", at, [128, 2, 1280]); at += 2560
    pT = sb("pT", at, [128, 2, 1280]); at += 2560
    qpad = sb("qpad", at, [128, 2, NG, 128]); at += 768
    aoh = sb("aoh", at, [128, 2, NTOK], R); at += 2 * NTOK
    aol = sb("aol", at, [128, 2, NTOK], R); at += 2 * NTOK
    assert at <= END
    sga = sb("sga", X, [128, KT, NTOK])
    qbc = sb("qbc", X + 4352, [128, 2, DT, 256])
    prod = sb("prod", X + 6400, [128, 1024])
    sTk = sb("sTk", X + 7424, [128, NG, 128])
    srow = sb("srow", X + 7808, [128, NG, 160])
    kvr = sb("kvr", ATT + 6528, [128, 3, DT, 256])
    at = SCR
    pad0 = sb("pad0", at, [128, 256]); at += 256
    pad1 = sb("pad1", at, [128, 2, 1024]); at += 2048
    pnew = sb("pnew", at, [128, NG, 128]); at += 384
    qbd = sb("qbd", at, [128, NG, 2, 128]); at += 768
    osel = sb("osel", at, [128, 4, HD]); at += 256
    orow = sb("orow", at, [128, HD]); at += 64
    aosf = sb("aosf", at, [128, 2, 32]); at += 64
    assert at <= SCR + 5888
    MT = ATT
    mTh = sb("mTh", MT, [128, KT, NTOK], R)
    mTl = sb("mTl", MT + 4352, [128, KT, NTOK], R)
    mTs = sb("mTs", MT + 8704, [128, KT, 64], R)
    mtmp = sb("mtmp", SCR, [128, 2, NTOK])
    xo = sb("xo", X, [128, TILES, D])
    xr = sb("xr", X + 5120, [128, TILES, D])
    gpost = sb("gpost", X + 10240, [128, D])
    gffn = sb("gffn", X + 11264, [128, D])
    tmpn = sb("tmpn", SCR + 1200, [128, 2, D])
    hn = sb("hn", SCR + 3248, [128, 2, D])
    njunk = sb("njunk", SCR + 5296, [128, D])
    tmp_s2 = sb("tmp_s2", SCR + 6400, [128, 512])
    fTh = sb("fTh", X + 5120, [128, FT * NTOK], R)
    fTl = sb("fTl", X + 17088, [128, FT * NTOK], R)
    fTs = sb("fTs", X + 29056, [128, FT * 64], R)
    U0 = X + 30464
    UW = 2 + SEQ + NB * 6
    CW = UW - 2
    ub = sb("u", U0, [128, 2, 2, UW])
    cb = sb("c", U0 + 4 * UW, [128, 2, UW])
    cvt = sb("cv_tail", U0 + 3376, [128, 2 * FT * 18])
    cvs = sb("cv_state", U0 + 3376 + 36 * FT, [128, 2 * FT * 16])
    assert U0 + 3376 + 68 * FT <= END
    fo = sb("fo", 0, [128, TILES, D])
    gfin = sb("gfin", 5120, [128, D])
    ytmp = sb("ytmp", 6144, [128, 2, D])
    tmp_s3 = sb("tmp_s3", 8192, [128, 512])
    fjunk = sb("fjunk", U0, [128, D])
    cvrow = sb("cv_row", U0 + 1024, [128, 2, 512])
    assert U0 + 2048 <= U0 + 6 * UW

    def cav(name, *shape):
        off, n = CA_AT[name]
        v = ca_t[:, off:off + n]
        return v.rearrange("p (a b) -> p a b", a=shape[0]) if shape else v

    def crv(name, *shape):
        off, n = CR_AT[name]
        v = cr_t[:, off:off + n]
        return v.rearrange("p (a b) -> p a b", a=shape[0]) if shape else v

    ident = cav("ident")
    P = [ctx.enter_context(nc.psum_tensor(f"bank{n}", [128, 512], F)) for n in range(8)]

    def sem(name):
        return ctx.enter_context(nc.semaphore(name))

    w_raw = [sem(f"w_raw{n}") for n in range(2)]
    w_hi, w_lo, w_used = sem("w_hi"), sem("w_lo"), sem("w_used")
    b_free = [sem(f"b_free{i}") for i in range(TILES)]
    a_free = [sem(f"a_free{n}") for n in range(2)]
    bank_full = {n: sem(f"bank_full{n}") for n in range(4, 8)}
    bank_free = {n: sem(f"bank_free{n}") for n in range(4, 8)}
    split_hi = sem("split_hi")
    x_in = [sem(f"x_in{i}") for i in range(TILES)]
    x_again = [sem(f"x_again{i}") for i in range(TILES)]
    ca_in, cr_in, gpre_in, convp_in = sem("ca_in"), sem("cr_in"), sem("gpre_in"), sem("convp_in")
    g2_in, gfin_in, cvs_in = sem("g2_in"), sem("gfin_in"), sem("cvs_in")
    act_step, dve_step, pool_step = sem("act_step"), sem("dve_step"), sem("pool_step")
    x_sq, x_rt, x_norm = sem("x_sq"), sem("x_rt"), sem("x_norm")
    tmp_ready = sem("tmp_ready")
    rope_done = sem("rope_done")
    cleared = sem("cleared")
    kd_ready, qd_ready, qm_ready, km_ready = sem("kd_ready"), sem("qd_ready"), sem("qm_ready"), sem("km_ready")
    s0_in = [sem(f"s0_in{n}") for n in range(3)]
    s1_out = [sem(f"s1_out{n}") for n in range(3)]
    on_sq, rt_ready = sem("on_sq"), sem("rt_ready")
    e_ready, r_ready = sem("e_ready"), sem("r_ready")
    k_out = sem("k_out")
    qs_out = sem("qs_out")
    av_out = sem("av_out")
    out_done = sem("out_done")
    windows_moved = sem("windows_moved")
    q_padded, maxed, exped, probs = sem("q_padded"), sem("maxed"), sem("exped"), sem("probs")
    o_hi = sem("o_hi")
    kv_in = [sem(f"kv_in{n}") for n in range(3)]
    q_in = [sem(f"q_in{n}") for n in range(2)]
    s_step, pads_ready, qbd_ready, v_used, s_probs = (sem("s_step"), sem("pads_ready"), sem("qbd_ready"),
                                                     sem("v_used"), sem("s_probs"))
    s_max, s_exp, o_row, os_hi, os_lo = (sem(n) for n in ("s_max", "s_exp", "o_row", "os_hi", "os_lo"))
    mix_sum, mix_hi, mix_lo = sem("mix_sum"), sem("mix_hi"), sem("mix_lo")
    n_sq, n_rt, x2_ready, h_ready = sem("n_sq"), sem("n_rt"), sem("x2_ready"), sem("h_ready")
    u_evac = [sem(f"u_evac{n}") for n in range(2)]
    conv_done, tail_done, head_ready, conv_tap = sem("conv_done"), sem("tail_done"), sem("head_ready"), sem("conv_tap")
    gelu_done, f_done, f_hi, f_lo = sem("gelu_done"), sem("f_done"), sem("f_hi"), sem("f_lo")
    y_sq, y_rt, y_ready = sem("y_sq"), sem("y_rt"), sem("y_ready")
    y_out = [sem(f"y_out{n}") for n in range(2)]
    cv_out = [sem(f"cv_out{n}") for n in range(2)]

    def emptied(eng, key):
        bank, n = USES[key]
        eng.wait_ge(bank_free[bank], n + 1)

    def filled(eng, key):
        bank, n = USES[key]
        eng.wait_ge(bank_full[bank], n + 1)
        return P[bank]

    def c_sample(c):
        return c[:, 2 + SEQ:UW].rearrange("p (b t) -> p b t", t=6)[:, :, 0:4]

    def slot_width(s):
        return BA_W if S_BA <= s < S_OUT else SLOT

    w_dram, kv_dram = a["weights"], [a[f"cache_kv_g{g}"] for g in range(NG)]
    qs_dram = nc.dram_tensor("sample_queries", [TS, 768], F).ap()
    up_loop = 2 * FT // 4

    def last_b_free(eng, i, n):
        eng.wait_ge(b_free[i], n)

    block = ctx.enter_context(nc.Block())

    @block.sync
    def _(sp):
        for i in range(TILES):
            r = rows(i)
            sp.dma_start(xin[0:r, i, :], a["x_prompt"][0, 128 * i:128 * i + 128, :] if i < 4 else
                         a["x_sample"].rearrange("b t d -> (b t) d")).then_inc(x_in[i], 16)
            if i == 0:
                sp.dma_start(gpre[:], a["norm_mix_pre"].broadcast_to([128, D])).then_inc(gpre_in, 16)
                sp.dma_start(ca_t[:], a["tables"]).then_inc(ca_in, 16)
            if i < 2:
                sp.dma_start(wraw[:, i, :], w_dram[i]).then_inc(w_raw[i], 16)
        sp.dma_start(cr_t[:], a["tables_ret"]).then_inc(cr_in, 16)
        sp.dma_start(convp[:], a["conv_params"]).then_inc(convp_in, 16)

        def load(slot):
            for j in range(2):
                sp.wait_ge(w_lo, slot + (j - 1))
                src = w_dram[bass.ds(slot + j, 1)].rearrange("a p n -> p (a n)")
                sp.dma_start(wraw[:, j, :], src).then_inc(w_raw[j], 16)

        def move(g, b, piece, pieces):
            n = (GROUPS[g][0] - DT) * 512 // pieces
            inner = {0: 1, 1: 1, 2: 7}[g]
            flat = lambda t: t[0, bass.ds(b, 1)].rearrange("a w c h d -> (a w c h d)")
            cut = lambda t, at_: flat(t)[at_ + n * piece:at_ + n * piece + n].rearrange("(e r c) -> e r c", e=16, r=inner)
            sp.dma_start(cut(o[f"s_kv_g{g}"], 0), cut(kv_dram[g], DT * 512)).then_inc(windows_moved, 16)

        with sp.Fori(0, NB) as b:
            for e in range(8):
                load(b * 16 + (2 + 2 * e))
                move(2, b, e, 8)
                if e % 4 == 1:
                    move(1, b, e // 4, 2)
                if e == 3:
                    move(0, b, 0, 1)
        with sp.Fori(0, (NSLOT - 130) // 2) as it:
            load(it * 2 + 130)
        sp.wait_ge(windows_moved, 16 * NB * (8 + 2 + 1))

    @block.gpsimd
    def _(pool):
        steps = [0]

        def step(ins):
            steps[0] += 1
            ins.then_inc(pool_step, 1)
            pool.wait_ge(pool_step, steps[0])

        stores = [0]

        def store(dst, src):
            stores[0] += 1
            pool.dma_start(dst, src).then_inc(out_done, 16)

        nc.gpsimd.memset(ss_r[:], 1.0).then_inc(cleared, 1)
        nc.gpsimd.memset(eps[:], EPS).then_inc(cleared, 1)
        nc.gpsimd.memset(vs[:], 0.0).then_inc(cleared, 1)
        nc.gpsimd.memset(qm[:], 0.0).then_inc(cleared, 1)
        nc.gpsimd.memset(km[:], 0.0).then_inc(cleared, 1)
        state_in = a["state_ret"]
        state_out = o["s_ret"]

        def load_state(n):
            h, p = n // 4, n % 4
            if n >= 3:
                pool.wait_ge(s1_out[n % 3], 16 * (n // 3))
            pool.dma_start(S0[:, n % 3], state_in[0, 2 * p:2 * p + 2, h].rearrange("b k v -> k b v")
                           ).then_inc(s0_in[n % 3], 16)

        for n in range(3):
            load_state(n)
        pool.wait_ge(cr_in, 16)
        pool.wait_ge(rope_done, 10)
        for c in range(4):
            if c:
                filled(pool, ("U", c - 1, 1))
            nc.gpsimd.tensor_tensor(kd[:].rearrange("p (h d) -> p h d", h=RH),
                                    RBk[:, c, :].rearrange("p (h d) -> p h d", h=RH),
                                    crv("kdec").unsqueeze(2).broadcast_to([128, RH, 128]), ALU.mult
                                    ).then_inc(kd_ready, 1)
            if c >= 1:
                pool.wait_ge(rope_done, 10 + 5 * c)
                if c == 1:
                    pool.dma_start(qs_dram[:, 0:512], RBq[0:TS, 4, :]).then_inc(qs_out, 16)
                elif c == 2:
                    pool.dma_start(qs_dram[:, 512:768], RBq[0:TS, 4, 0:256]).then_inc(qs_out, 16)
                    send = ((0, 256),)
                else:
                    send = ((1, 0), (2, 256))
                if c >= 2:
                    for g, at_ in send:
                        win = min(GROUPS[g][0], SEQ)
                        t0 = 4 - win // 128
                        dst = o[f"p_kv_g{g}"][0, 0, :, 0].rearrange("(n p) h d -> p n (h d)", p=128)
                        pool.dma_start(dst, RBq[:, t0:4, at_:at_ + 256]).then_inc(k_out, 16)
                        W = GROUPS[g][0]
                        for b in range(NB):
                            pool.dma_start(o[f"s_kv_g{g}"][0, b, W - DT:W, 0].rearrange("t h d -> t (h d)"),
                                           RBq[4 * b:4 * b + 4, 4, at_:at_ + 256]).then_inc(k_out, 16)
        for h in range(RH):
            if h:
                filled(pool, ("Us", h - 1, 3))
            nc.gpsimd.tensor_tensor(km[0:TS], RBk[0:TS, 4, 128 * h:128 * h + 128].unsqueeze(1).broadcast_to([TS, NB, 128]),
                                    crv("kdecs", RH)[0:TS, h, :].unsqueeze(2).broadcast_to([TS, NB, 128]), ALU.mult
                                    ).then_inc(km_ready, 1)
            if h == 0:
                emptied(pool, ("U", 3, 1))
                store(o["p_ret"][0, 0].rearrange("h k v -> k h v"), state[:])
            for p in range(4):
                n = 4 * h + p
                emptied(pool, ("Us", h, p))
                pool.dma_start(state_out[0, 2 * p:2 * p + 2, h].rearrange("b k v -> k b v"), S0[:, n % 3]
                               ).then_inc(s1_out[n % 3], 16)
                if n + 3 < 16:
                    load_state(n + 3)
        for i in range(TILES):
            pool.wait_ge(b_free[i], BLK_AV2 + 1)
        for g, (win, _) in enumerate(GROUPS):
            w = min(win, SEQ)
            dst = o[f"p_kv_g{g}"][0, 0, :, 1].rearrange("(n p) h d -> p n (h d)", p=128)
            pool.dma_start(dst, av[:, 4 - w // 128:4, 256 * g:256 * g + 256]).then_inc(av_out, 16)
            for b in range(NB):
                pool.dma_start(o[f"s_kv_g{g}"][0, b, win - DT:win, 1].rearrange("t h d -> t (h d)"),
                               avs[4 * b:4 * b + 4, 256 * g:256 * g + 256]).then_inc(av_out, 16)
        for n in range(3):
            pool.wait_ge(s1_out[n], 16 * (16 // 3 + (n < 16 % 3)))
        emptied(pool, ("r", 0, 4))
        step(nc.gpsimd.memset(qpad[:], 0.0))
        for s in range(16):
            qb, h = s // 4, s % 4
            par, hp = h % 2, h // 2
            if s >= 2:
                filled(pool, ("s", s - 2, 2))
            for g in range(NG):
                last = nc.gpsimd.tensor_copy(qpad[64 * par:64 * par + 64, par, g, :],
                                             aqT[64 * par:64 * par + 64, 2 * g + hp, 128 * qb:128 * qb + 128])
            last.then_inc(q_padded, 1)
        filled(pool, ("o", 7))
        pool.wait_ge(o_hi, 8)
        pool.wait_ge(av_out, 16 * 27)
        pool.wait_ge(qs_out, 32)
        pool.wait_ge(w_used, S_GA)

        def kv_load(which, n):
            b, g = n // NG, n % NG
            m = 24 * which + n
            if m >= 3:
                if m - 3 < 24:
                    pool.wait_ge(s_step, m - 2)
                else:
                    pool.wait_ge(v_used, m - 3 - 24 + 1)
            if g == 0:
                pool.dma_start(kvr[:, m % 3, 0, :], kv_dram[0][0, b, :, which].rearrange("n h d -> n (h d)")
                               ).then_inc(kv_in[m % 3], 16)
            else:
                dil = GROUPS[g][1]
                src = kv_dram[g][0, b].rearrange("(n r) c h d -> n r c (h d)", r=dil)[:, 0:DT, which]
                pool.dma_start(kvr[:, m % 3], src).then_inc(kv_in[m % 3], 16)

        def q_load(n):
            b, g = n // NG, n % NG
            if n >= 2:
                pool.wait_ge(s_step, n - 1)
            src = qs_dram[4 * b:4 * b + 4, 256 * g:256 * g + 256].unsqueeze(0).broadcast_to([128, DT, 256])
            pool.dma_start(qbc[:, n % 2], src).then_inc(q_in[n % 2], 16)

        for t in (pad0, pad1, qbd):
            last = nc.gpsimd.memset(t[:], 0.0)
            step(last)
        kv_load(0, 0)
        q_load(0)
        kv_load(0, 1)
        q_load(1)
        for g in range(NG):
            for hp in range(2):
                for par in range(2):
                    dst = qbd[64 * par:64 * par + 64, g, hp, :].rearrange("p (n h) -> p n h", h=4)[:, :, 2 * hp + par]
                    last = nc.gpsimd.tensor_copy(dst, aqT[64 * par:64 * par + 64, 2 * g + hp, SEQ:NTOK])
        last.then_inc(qbd_ready, 1)
        for n in range(2, 24):
            kv_load(0, n)
            q_load(n)
        for n in range(24):
            kv_load(1, n)
        pool.wait_ge(mix_lo, KT)
        for i in range(TILES):
            r = rows(i)
            pool.dma_start(xr[0:r, i, :], a["x_prompt"][0, 128 * i:128 * i + 128, :] if i < 4 else
                           a["x_sample"].rearrange("b t d -> (b t) d")).then_inc(x_again[i], 16)
        pool.dma_start(gpost[:], a["norm_mix_post"].broadcast_to([128, D])).then_inc(g2_in, 16)
        pool.dma_start(gffn[:], a["norm_ffn_pre"].broadcast_to([128, D])).then_inc(g2_in, 16)
        filled(pool, ("h2", 4, 1))
        emptied(pool, ("h2", 4, 1))
        pool.dma_start(cvs[:], a["conv_state"]).then_inc(cvs_in, 16)
        nc.gpsimd.memset(ub[:], 0.0).then_inc(pool_step, 1)
        steps[0] += 1
        pool.wait_ge(pool_step, steps[0])
        pool.wait_ge(cvs_in, 16)
        pool.sem_inc(tail_done, 4)
        with pool.Fori(0, up_loop) as it:
            for q in range(2):
                for j in range(2):
                    tile = it * 2 + (q + FT * j)
                    u_s = ub[:, q, j, 2 + SEQ:].rearrange("p (b t) -> p b t", t=6)
                    pool.wait_ge(conv_done, it * 4 + (2 * q + j + 1))
                    nc.gpsimd.tensor_copy(u_s[:, :, 0:2], cvs[:, bass.ds(tile * 16, 16)].rearrange("p (b t) -> p b t", t=2)
                                          ).then_inc(head_ready, 1)
                    pool.wait_ge(u_evac[j], it * 2 + (q + 1))
                    nc.gpsimd.tensor_copy(cvt[:, bass.ds(tile * 18, 2)], ub[:, q, j, SEQ:SEQ + 2])
                    nc.gpsimd.tensor_copy(cvt[:, bass.ds(tile * 18 + 2, 16)].rearrange("p (b t) -> p b t", t=2),
                                          u_s[:, :, 4:6]).then_inc(tail_done, 1)
        for j in range(2 * FT // 4):
            emptied(pool, ("cv", j))
            pool.dma_start(o["p_conv"][0, 0, :, 512 * j:512 * j + 512], cvrow[0:2, j % 2, :]).then_inc(cv_out[j % 2], 16)
            pool.dma_start(o["s_conv"][0].rearrange("b t n -> (b t) n")[:, 512 * j:512 * j + 512], cvrow[2:18, j % 2, :]
                           ).then_inc(cv_out[j % 2], 16)
        pool.dma_start(gfin[:], a["norm_ffn_post"].broadcast_to([128, D])).then_inc(gfin_in, 16)
        for i in range(TILES):
            pool.wait_ge(y_ready, i + 1)
            r = rows(i)
            dst = o["y_prompt"][0, 128 * i:128 * i + 128, :] if i < 4 else o["y_sample"].rearrange("b t d -> (b t) d")
            pool.dma_start(dst, ytmp[0:r, i % 2, :]).then_inc(y_out[i % 2], 16)
        pool.wait_ge(out_done, 16 * stores[0])
        pool.wait_ge(k_out, 16 * 27)
        pool.wait_ge(av_out, 16 * 27)
        for n in range(2):
            pool.wait_ge(y_out[n], 16 * (3 - n))
            pool.wait_ge(cv_out[n], 32 * (6 - n))

    @block.scalar
    def _(act):
        steps = [0]

        def step(ins):
            steps[0] += 1
            ins.then_inc(act_step, 1)
            act.wait_ge(act_step, steps[0])

        def w_split(s):
            act.wait_ge(w_raw[s % 2], 16 * (s // 2 + 1))
            if s >= 2:
                act.wait_ge(w_used, s - 1)
            w = slot_width(s)
            nc.scalar.activation(whi[:, s % 2, 0:w], wraw[:, s % 2, 0:w], ACT.Copy).then_inc(w_hi, 1)

        def split_evac(key, Th, Ts, k0, i):
            b = filled(act, key)
            n = rows(i)
            src = b[:, 0:4 * n].rearrange("p (k n) -> p k n", k=4)
            ins = nc.scalar.activation(Th[:, k0:k0 + 4, cols(i)], src, ACT.Copy)
            if i == 4:
                ins = nc.scalar.activation(Ts[:, k0:k0 + 4, 0:32], src, ACT.Copy)
            ins.then_inc(split_hi, 1)

        def block_end(bi):
            first, n = BLOCKS[bi][:2]
            act.wait_ge(w_used, first + n)

        def sample_lo(bi, tmp, width, scales):
            if bi:
                act.wait_ge(b_free[4], bi)
            at_ = 0
            for w, scale in scales:
                ins = nc.scalar.activation(tmp[0:TS, at_:at_ + w], P[4][32:64, at_:at_ + w], ACT.Copy, scale=scale)
                at_ += w
            ins.then_inc(tmp_ready, 1)

        def evac_block(bi, dst, width, scales, tmp=tmp_s):
            block_end(bi)
            sample_lo(bi, tmp, width, scales)
            for i in range(4):
                at_ = 0
                for w, scale in scales:
                    ins = nc.scalar.activation(dst(i)[:, at_:at_ + w], P[i][:, at_:at_ + w], ACT.Copy, scale=scale)
                    at_ += w
                ins.then_inc(b_free[i], 1)

        def turn_evac(bi):
            for i in range(TILES):
                b = filled(act, ("t", bi, i))
                n = rows(i)
                src = b[:, 0:4 * n].rearrange("p (k n) -> p k n", k=4)
                if bi == BLK_RQ:
                    parts = ((qT, 0, 0, 4),)
                elif bi == BLK_RK:
                    parts = ((kT, 0, 0, 4),)
                elif bi == BLK_AQ:
                    parts = ((aqT, 0, 0, 4),)
                elif bi == BLK_AQK:
                    parts = ((aqT, 4, 0, 2), (akT, 0, 2, 2))
                else:
                    parts = ((akT, 2, 0, 4),)
                for dst, d0, s0, k in parts:
                    ins = nc.scalar.activation(dst[:, d0:d0 + k, cols(i)], src[:, s0:s0 + k, :], ACT.Copy)
                ins.then_inc(bank_free[USES[("t", bi, i)][0]], 1)

        w_split(0)
        w_split(1)
        act.wait_ge(cleared, 2)
        for i in range(TILES):
            r = rows(i)
            act.wait_ge(x_in[i], 16)
            nc.scalar.activation(junk[0:r], xin[0:r, i, :], ACT.Square, accum_out=ss_x[0:r, i:i + 1]).then_inc(x_sq, 1)
            act.wait_ge(x_sq, i + 1)
            nc.scalar.activation(rt_x[0:r, i:i + 1], ss_x[0:r, i:i + 1], ACT.Sqrt, scale=1.0 / D,
                                 bias=eps[0:r, 0:1]).then_inc(x_rt, 1)
        for i in range(TILES):
            for half in range(2):
                split_evac(("x", i, half), T1h, T1s, 4 * half, i)

        dests = {
            BLK_RQ: (lambda i: RBq[:, i, :], ((512, 1.0),)),
            BLK_RK: (lambda i: RBk[:, i, :], ((512, DK ** -0.5),)),
            BLK_RV: (lambda i: vt[:, i, 0:512], ((512, 1.0),)),
            BLK_RV + 1: (lambda i: vt[:, i, 512:1024], ((512, 1.0),)),
            BLK_AQ: (lambda i: RBq[:, i, :], ((512, HD ** -0.5),)),
            BLK_AQK: (lambda i: RBq[:, i, :], ((256, HD ** -0.5), (256, 1.0))),
            BLK_AK: (lambda i: RBq[:, i, :], ((512, 1.0),)),
            BLK_AV: (lambda i: av[:, i, 0:512], ((512, 1.0),)),
            BLK_AV2: (lambda i: av[:, i, 512:768], ((256, 1.0),)),
        }

        def outputs_evac(c):
            filled(act, ("U", c, 1))
            for j in range(2):
                key = ("O", c, j)
                b = filled(act, key)
                nc.scalar.activation(vt[:, c, 512 * j:512 * j + 512], b[:, :], ACT.Copy).then_inc(bank_free[USES[key][0]], 1)
            for h in range(RH):
                if h % 2 == 0:
                    emptied(act, ("O", c, h // 2))
                if 4 * c + h:
                    act.wait_ge(on_sq, 4 * c + h)
                nc.scalar.activation(rjunk[:], vt[:, c, DV * h:DV * h + DV], ACT.Square,
                                     accum_out=ss_r[:, 4 * c + h:4 * c + h + 1]).then_inc(on_sq, 1)

        def sample_outputs_evac(h):
            filled(act, ("Us", h, 3))
            b = filled(act, ("Os", h))
            nc.scalar.activation(vs[0:TS, DV * h:DV * h + DV], b[0:TS, 0:DV], ACT.Copy).then_inc(bank_free[6], 1)
            emptied(act, ("Os", h))
            act.wait_ge(on_sq, 16 + h)
            nc.scalar.activation(rjunk[0:TS], vs[0:TS, DV * h:DV * h + DV], ACT.Square,
                                 accum_out=ss_r[0:TS, 16 + h:17 + h]).then_inc(on_sq, 1)

        for bi in range(BLK_RG):
            first, n = BLOCKS[bi][:2]
            for s in range(n - 1):
                w_split(first + s + 2)
                if s == 1 and bi in (1, 2):
                    turn_evac(bi - 1)
                if s == 1 and bi in (5, 6, 7):
                    turn_evac(bi - 1)
                if bi == BLK_AV2:
                    sample_outputs_evac(0)
                    sample_outputs_evac(1)
            if bi in (BLK_AQ, BLK_AQK, BLK_AK):
                prev = {BLK_AQ: BLK_RQ, BLK_AQK: BLK_AQ, BLK_AK: BLK_AQK}[bi]
                filled(act, ("t", prev, 4))
            if bi == BLK_AQK:
                act.wait_ge(qs_out, 16)
            if bi == BLK_AK:
                act.wait_ge(qs_out, 32)
                act.wait_ge(k_out, 16 * 9)
            if bi == BLK_RV:
                act.wait_ge(cleared, 3)
            dst, scales = dests[bi]
            evac_block(bi, dst, BLOCKS[bi][3], scales)
            w_split(first + n + 1)
            if 4 <= bi < 8:
                outputs_evac(bi - 4)
            if bi == BLK_AV2:
                sample_outputs_evac(2)
                sample_outputs_evac(3)
                act.wait_ge(on_sq, 20)
                nc.scalar.activation(rt_r[:], ss_r[:], ACT.Sqrt, scale=1.0 / DV, bias=eps[:, 0:1]).then_inc(rt_ready, 1)
        for g in range(2):
            bi = BLK_RG + g
            first, n = BLOCKS[bi][:2]
            for s in range(n - 1):
                w_split(first + s + 2)
                if g == 1 and s == 2:
                    for i in range(TILES):
                        split_evac(("r", 0, i), rTh, rTs, 0, i)
            block_end(bi)
            act.wait_ge(b_free[4], bi)
            if g:
                act.wait_ge(r_ready, 5)
            nc.scalar.activation(tmp_s[0:TS, :], P[4][32:64, :], ACT.Copy).then_inc(tmp_ready, 1)
            for i in range(4):
                k = 5 * g + i
                if k >= 2:
                    act.wait_ge(r_ready, k - 1 if i >= 2 else 5 * g)
                nc.scalar.activation(etmp[:, i % 2, :], P[i][:, :], ACT.Tanh, scale=0.5).then_inc(e_ready, 1)
            act.wait_ge(b_free[4], bi + 1)
            nc.scalar.activation(tmp_s[0:TS, :], etmp[0:TS, 0, :], ACT.Tanh, scale=0.5).then_inc(e_ready, 1)
            w_split(first + n + 1)

        def turned_probs(s):
            nblk = len(attention_blocks(s // 4))
            if s >= 2:
                filled(act, ("o", s // 2 - 1))
            for j in range(turns(s)):
                key = ("pt", s, j)
                b = filled(act, key)
                k = min(4, nblk - 4 * j)
                nc.scalar.activation(pT[:, s % 2, 512 * j:512 * j + 128 * k], b[:, 0:128 * k], ACT.Copy
                                     ).then_inc(bank_free[USES[key][0]], 1)

        def attended_hi(pair):
            qb, hp = pair // 2, pair % 2
            b = filled(act, ("o", pair))
            nc.scalar.activation(aoh[:, hp, 128 * qb:128 * qb + 128], b[:, 0:128], ACT.Copy).then_inc(o_hi, 1)

        for i in range(TILES):
            split_evac(("r", 1, i), rTh, rTs, 4, i)
        act.wait_ge(k_out, 16 * 27)
        for s in range(17):
            if s < 16:
                w = 128 * len(attention_blocks(s // 4))
                act.wait_ge(maxed, s + 1)
                nc.scalar.activation(sc[:, s % 2, 0:w], sc[:, s % 2, 0:w], ACT.Exp, bias=nm[:, s % 2:s % 2 + 1],
                                     accum_out=den[:, s % 2:s % 2 + 1]).then_inc(exped, 1)
            if s >= 1:
                turned_probs(s - 1)
            if s < 16:
                w_split(S_GB + s + 2)
                if s % 2 == 0:
                    n = s // 2
                    act.wait_ge(w_used, S_GB + s + 1)
                    if n >= 2:
                        act.wait_ge(a_free[1], n - 1)
                    nc.scalar.activation(gexp[:, n % 2, 0:HALF], P[0][:, 0:HALF], ACT.Tanh, scale=0.5)
                    nc.scalar.activation(gexp[:, n % 2, HALF:NTOK], P[1][:, 0:HALF], ACT.Tanh, scale=0.5).then_inc(a_free[0], 1)
            if s >= 2 and s % 2 == 0:
                attended_hi(s // 2 - 1)
        for n in range(KT):
            w_split(S_GA + n + 2)
            act.wait_ge(w_used, S_GA + n + 1)
            p = n % 2
            nc.scalar.activation(sga[:, n, 0:HALF], P[2 * p][:, 0:HALF], ACT.Tanh, scale=0.5)
            nc.scalar.activation(sga[:, n, HALF:NTOK], P[2 * p + 1][:, 0:HALF], ACT.Tanh, scale=0.5).then_inc(a_free[p], 1)
        act.wait_ge(s_max, 1)
        nc.scalar.activation(srow[:], srow[:], ACT.Exp, bias=nm[:, 0:1], accum_out=den[:, 0:1]).then_inc(s_exp, 1)
        b = filled(act, ("sp",))
        q4 = b[:, 0:128].rearrange("p (q r) -> p q r", q=4)
        nc.scalar.activation(pad0[:].rearrange("p (q r) -> p q r", q=4)[:, :, 0:16], q4[:, :, 0:16], ACT.Copy)
        nc.scalar.activation(pad0[:].rearrange("p (q r) -> p q r", q=4)[:, :, 48:64], q4[:, :, 16:32], ACT.Copy)
        for g in range(2):
            src = b[:, 128 * (g + 1):128 * (g + 2)].rearrange("p (q j h) -> p q j h", q=4, j=8)
            dst = pad1[:, g, :].rearrange("p (q r) -> p q r", q=4)
            for j in range(8):
                last = nc.scalar.activation(dst[:, :, 36 * j:36 * j + 4], src[:, :, j, :], ACT.Copy)
        last.then_inc(bank_free[6], 1)
        b = filled(act, ("spn",))
        nc.scalar.activation(pnew[0:TS].rearrange("p g n -> p (g n)"), b[0:TS, 0:384], ACT.Copy).then_inc(bank_free[4], 1)
        b = filled(act, ("so",))
        src = b[0:HD, 0:128].rearrange("p (n h) -> p n h", h=4)
        for h in range(AH):
            last = nc.scalar.activation(aosf[64 * (h % 2):64 * (h % 2) + 64, h // 2, :], src[:, :, h], ACT.Copy)
        last.then_inc(bank_free[USES[("so",)][0]], 1)
        emptied(act, ("so",))
        nc.scalar.activation(aoh[:, :, SEQ:NTOK], aosf[:], ACT.Copy).then_inc(os_hi, 1)
        for n in range(KT):
            w_split(S_BA + n + 2)
            act.wait_ge(mix_sum, n + 1)
            nc.scalar.activation(mTh[:, n, :], mtmp[:, n % 2, :], ACT.Copy, scale=0.5)
            nc.scalar.activation(mTs[:, n, 0:32], mtmp[:, n % 2, SEQ:NTOK], ACT.Copy, scale=0.5).then_inc(mix_hi, 1)
        for nb in range(2):
            bi = BLK_OUT + nb
            first, n = BLOCKS[bi][:2]
            for s in range(n - 1):
                w_split(first + s + 2)
            evac_block(bi, lambda i: xo[:, i, 512 * nb:512 * nb + 512], 512, ((512, 1.0),), tmp_s2)
            w_split(first + n + 1)
        for i in range(TILES):
            r = rows(i)
            act.wait_ge(b_free[i], BLK_OUT + 2)
            nc.scalar.activation(njunk[0:r], xo[0:r, i, :], ACT.Square, accum_out=ss_n[0:r, i:i + 1]).then_inc(n_sq, 1)
            act.wait_ge(n_sq, i + 1)
            nc.scalar.activation(rt_n[0:r, i:i + 1], ss_n[0:r, i:i + 1], ACT.Sqrt, scale=1.0 / D,
                                 bias=eps[0:r, 0:1]).then_inc(n_rt, 1)
        for i in range(TILES + 1):
            if i < TILES:
                r = rows(i)
                act.wait_ge(x2_ready, i + 1)
                nc.scalar.activation(njunk[0:r], xo[0:r, i, :], ACT.Square, accum_out=ss_n[0:r, 5 + i:6 + i]).then_inc(n_sq, 1)
                act.wait_ge(n_sq, TILES + i + 1)
                nc.scalar.activation(rt_n[0:r, 5 + i:6 + i], ss_n[0:r, 5 + i:6 + i], ACT.Sqrt, scale=1.0 / D,
                                     bias=eps[0:r, 0:1]).then_inc(n_rt, 1)
            if i:
                for half in range(2):
                    split_evac(("h2", i - 1, half), T1h, T1s, 4 * half, i - 1)
        with act.Fori(0, up_loop) as it:
            for q in range(2):
                for j in range(2):
                    t1 = 2 * q + j + 1
                    act.wait_ge(w_used, it * 4 + (S_UP + t1))
                    act.wait_ge(conv_done, it * 4 + t1)
                    act.wait_ge(tail_done, it * 4 + t1)
                    nc.scalar.activation(ub[:, q, j, 2:2 + HALF], P[2 * j][:, 0:HALF], ACT.Copy)
                    nc.scalar.activation(ub[:, q, j, 2 + HALF:2 + SEQ], P[2 * j + 1][:, 0:SEQ - HALF], ACT.Copy)
                    u_s = ub[:, q, j, 2 + SEQ:].rearrange("p (b t) -> p b t", t=6)
                    nc.scalar.activation(u_s[:, :, 2:6], P[2 * j + 1][:, SEQ - HALF:HALF].rearrange("p (b t) -> p b t", t=4),
                                         ACT.Copy).then_inc(u_evac[j], 1)
                    act.wait_ge(w_raw[j], it * 32 + (16 * ((S_UP + 2 * q + 2 + j) // 2 + 1)))
                    nc.scalar.activation(whi[:, j, :], wraw[:, j, :], ACT.Copy).then_inc(w_hi, 1)
                    if j == 0:
                        act.wait_ge(conv_done, it * 4 + (t1 + 4))
                        nc.scalar.activation(cb[:, 0, 0:CW], cb[:, 0, 0:CW], ACT.Gelu_apprx_tanh).then_inc(gelu_done, 1)
                act.wait_ge(f_done, it * 2 + (q + 1))
                pair = it * 2 + q
                samp = c_sample(cb[:, 0, :])
                nc.scalar.activation(fTh[:, bass.ds(pair * NTOK, SEQ)], cb[:, 0, 0:SEQ], ACT.Copy)
                nc.scalar.activation(fTh[:, bass.ds(pair * NTOK + SEQ, TS)].rearrange("p (b t) -> p b t", t=4), samp, ACT.Copy)
                nc.scalar.activation(fTs[:, bass.ds(pair * 64, TS)].rearrange("p (b t) -> p b t", t=4), samp, ACT.Copy
                                     ).then_inc(f_hi, 1)
        for nb in range(2):
            bi = BLK_DN + nb
            first, n = BLOCKS[bi][:2]
            for s in range(n - 1):
                if first + s + 2 < NSLOT:
                    w_split(first + s + 2)
            evac_block(bi, lambda i: fo[:, i, 512 * nb:512 * nb + 512], 512, ((512, 1.0),), tmp_s3)
            if first + n + 1 < NSLOT:
                w_split(first + n + 1)
        for i in range(TILES):
            r = rows(i)
            act.wait_ge(b_free[i], BLK_DN + 2)
            nc.scalar.activation(fjunk[0:r], fo[0:r, i, :], ACT.Square, accum_out=ss_n[0:r, 10 + i:11 + i]).then_inc(y_sq, 1)
            act.wait_ge(y_sq, i + 1)
            nc.scalar.activation(rt_n[0:r, 10 + i:11 + i], ss_n[0:r, 10 + i:11 + i], ACT.Sqrt, scale=1.0 / D,
                                 bias=eps[0:r, 0:1]).then_inc(y_rt, 1)

    @block.tensor
    def _(pe):
        mm = nc.tensor.matmul

        def open_bank(key):
            bank, n = USES[key]
            if n:
                pe.wait_ge(bank_free[bank], n)
            return P[bank], bank_full[bank]

        def turn(key, srcs, n, m=128):
            b, full = open_bank(key)
            for k, src in enumerate(srcs):
                last = nc.tensor.transpose(b[0:m, k * n:(k + 1) * n], src, ident[0:n, 0:n])
            last.then_inc(full, 1)

        def b_block(bi, Th, Tl, Ts, between=None, ready=None):
            first, n, per, w = BLOCKS[bi]
            for s in range(n):
                slot = first + s
                pe.wait_ge(w_lo, slot + 1)
                for kk in range(per):
                    k = s * per + kk
                    Wh = whi[:, slot % 2, kk * w:(kk + 1) * w]
                    Wl = wlo[:, slot % 2, kk * w:(kk + 1) * w]
                    st, sp_ = k == 0, k == n * per - 1
                    for i in range(4):
                        if k == 0:
                            if ready:
                                ready(i)
                            if bi:
                                pe.wait_ge(b_free[i], bi)
                        xh, xl = Th(k, cols(i)), Tl(k, cols(i))
                        mm(P[i][:, 0:w], xh, Wh, start=st, stop=False)
                        mm(P[i][:, 0:w], xh, Wl, start=False, stop=False)
                        mm(P[i][:, 0:w], xl, Wh, start=False, stop=sp_)
                    if k == 0:
                        if ready:
                            ready(4)
                        if bi:
                            pe.wait_ge(b_free[4], bi)
                    mm(P[4][0:64, 0:w], Ts(k), Wh, start=st, stop=False)
                    last = mm(P[4][0:64, 0:w], Ts(k), Wl, start=False, stop=sp_)
                last.then_inc(w_used, 1)
                if between:
                    between(s)

        def a_tile(slot, Th, Tl, kt, banks):
            for k in range(kt):
                Wh, Wl = whi[:, slot % 2, 128 * k:128 * k + 128], wlo[:, slot % 2, 128 * k:128 * k + 128]
                for half in range(2):
                    dst = P[banks + half][:, 0:HALF]
                    c = slice(HALF * half, HALF * half + HALF)
                    mm(dst, Wh, Th[:, k, c], start=k == 0, stop=False)
                    mm(dst, Wh, Tl[:, k, c], start=False, stop=False)
                    last = mm(dst, Wl, Th[:, k, c], start=False, stop=k == kt - 1)
            return last

        pe.wait_ge(ca_in, 16)
        for i in range(TILES):
            pe.wait_ge(x_norm, i + 1)
            for half in range(2):
                turn(("x", i, half), [xn[0:rows(i), i % 2, 128 * (4 * half + k):128 * (4 * half + k) + 128] for k in range(4)], rows(i))

        T1 = (lambda k, c: T1h[:, k, c], lambda k, c: T1l[:, k, c], lambda k: T1s[:, k, :])

        def turn_block(bi):
            src = RBk if bi == BLK_RK else RBq
            for i in range(TILES):
                pe.wait_ge(rope_done, 5 * ROPE_BLOCKS.index(bi) + i + 1)
                turn(("t", bi, i), [src[0:rows(i), i, 128 * k:128 * k + 128] for k in range(4)], rows(i))

        def scores(c):
            emptied(pe, ("t", BLK_RK, 4))
            emptied(pe, ("t", BLK_RK, 3))
            emptied(pe, ("t", BLK_RK, 2))
            b, full = open_bank(("S", c))
            for h in range(RH):
                last = mm(b[:, 128 * h:128 * h + 128], kT[:, h, cols(c)], qT[:, h, cols(c)], start=True, stop=True)
            last.then_inc(full, 1)

        def outputs(c):
            emptied(pe, ("S", c))
            if c:
                pe.wait_ge(qd_ready, c)
                emptied(pe, ("U", c - 1, 1))
            for j in range(2):
                b, full = open_bank(("O", c, j))
                for e in range(2):
                    h = 2 * j + e
                    dst = b[:, DV * e:DV * e + DV]
                    last = mm(dst, PT[:, h, :], vt[:, c, DV * h:DV * h + DV], start=True, stop=c == 0)
                    if c:
                        last = mm(dst, qd[:, h, :], state[:, h, :], start=False, stop=True)
                last.then_inc(full, 1)

        def updates(c, j):
            pe.wait_ge(kd_ready, c + 1)
            b, full = open_bank(("U", c, j))
            for e in range(2):
                h = 2 * j + e
                last = mm(b[:, DV * e:DV * e + DV], kd[:, 128 * h:128 * h + 128], vt[:, c, DV * h:DV * h + DV],
                          start=True, stop=True)
            last.then_inc(full, 1)

        def retention_part(c, s):
            if s == 0:
                scores(c)
            elif s == 1:
                if c:
                    turn_block(BLK_AQ + c - 1)
                outputs(c)
            else:
                updates(c, s - 2)

        def sample_head(h):
            if h == 0:
                b, full = open_bank(("Ss",))
                for hh in range(RH):
                    last = mm(b[0:TS, 32 * hh:32 * hh + 32], kT[:, hh, SEQ:NTOK], qT[:, hh, SEQ:NTOK], start=True, stop=True)
                last.then_inc(full, 1)
                emptied(pe, ("Ss",))
            ob, ofull = open_bank(("Os", h))
            mm(ob[0:TS, 0:DV], PTs[0:TS, h, :], vs[0:TS, DV * h:DV * h + DV], start=True, stop=False)
            pe.wait_ge(qm_ready, h + 1)
            pe.wait_ge(km_ready, h + 1)
            for p in range(4):
                n = 4 * h + p
                pe.wait_ge(s0_in[n % 3], 16 * (n // 3 + 1))
                for e in range(2):
                    last = mm(ob[0:TS, 0:DV], qm[:, h % 2, 2 * p + e, :], S0[:, n % 3, e, :], start=False,
                              stop=p == 3 and e == 1)
                if p == 3:
                    last.then_inc(ofull, 1)
                b, full = open_bank(("Us", h, p))
                for e in range(2):
                    last = mm(b[:, DV * e:DV * e + DV], km[:, 2 * p + e, :], vs[:, DV * h:DV * h + DV], start=True, stop=True)
                last.then_inc(full, 1)

        def x_ready(i):
            for half in range(2):
                emptied(pe, ("x", i, half))

        for bi in range(BLK_RG):
            def between(s, bi=bi):
                if bi in (1, 2) and s == 1:
                    turn_block(bi - 1)
                if 4 <= bi < 8:
                    retention_part(bi - 4, s)
                if bi == 8:
                    sample_head(2 * s)
                    sample_head(2 * s + 1)
            b_block(bi, *T1, between=between, ready=x_ready if bi == 0 else None)

        def turn_gated(g):
            for i in range(TILES):
                pe.wait_ge(r_ready, 5 * g + i + 1)
                r = rows(i)
                src = vt[:, i, :] if i < 4 else vs[0:TS, :]
                turn(("r", g, i), [src[:, 128 * (4 * g + k):128 * (4 * g + k) + 128] for k in range(4)], r)

        b_block(BLK_RG, *T1)
        b_block(BLK_RG + 1, *T1, between=lambda s: turn_gated(0) if s == 2 else None)

        def att_scores(s):
            qb, h = s // 4, s % 4
            pe.wait_ge(q_padded, s + 1)
            for g in range(NG):
                gg = (1, 2, 0)[g]
                b, full = open_bank(("s", s, g))
                lo, hi = (0 if gg else 128 * max(qb - 1, 0)), 128 * (qb + 1)
                mm(b[:, 0:hi - lo], qpad[:, h % 2, gg, :], akT[:, 2 * gg + h // 2, lo:hi], start=True, stop=True
                   ).then_inc(full, 1)

        def att_turn(s):
            nblk = len(attention_blocks(s // 4))
            pe.wait_ge(probs, s + 1)
            for j in range(turns(s)):
                ks = range(4 * j, min(4 * j + 4, nblk))
                turn(("pt", s, j), [sc[:, s % 2, 128 * k:128 * k + 128] for k in ks], 128)

        def att_values(s):
            qb, h = s // 4, s % 4
            par = h % 2
            key = ("o", s // 2)
            if par == 0:
                b, full = open_bank(key)
            else:
                b, full = P[7], bank_full[7]
            blocks = attention_blocks(qb)
            for n, (g, kb) in enumerate(blocks):
                if n % 4 == 0:
                    emptied(pe, ("pt", s, n // 4))
                last = mm(b[64 * par:64 * par + 64, 0:128], av[:, kb, 256 * g + 64 * h:256 * g + 64 * h + 64],
                          pT[:, s % 2, 128 * n:128 * n + 128], start=n == 0, stop=n == len(blocks) - 1)
            if par:
                last.then_inc(full, 1)

        for i in range(TILES):
            pe.wait_ge(b_free[i], BLK_AV2 + 1)
        for i in range(4, -1, -1):
            emptied(pe, ("t", BLK_AK, i))
        pe.wait_ge(b_free[4], BLK_RG + 2)
        turn_gated(1)
        att_scores(0)
        for s in range(17):
            if s < 16:
                slot, n = S_GB + s, s // 2
                if s < 2:
                    pe.wait_ge(b_free[2 * s], BLK_RG + 2)
                    pe.wait_ge(b_free[2 * s + 1], BLK_RG + 2)
                if s == 1:
                    for i in (2, 3, 4):
                        emptied(pe, ("r", 1, i))
                pe.wait_ge(w_lo, slot + 1)
                if n:
                    pe.wait_ge(a_free[s % 2], n)
                if s % 2 == 0:
                    a_tile(slot, T1h, T1l, KT, 0).then_inc(w_used, 1)
                else:
                    a_tile(slot, rTh, rTl, KT, 2).then_inc(w_used, 1)
            if s >= 1:
                att_turn(s - 1)
                att_values(s - 1)
            if s < 15:
                att_scores(s + 1)
        for n in range(KT):
            pe.wait_ge(w_lo, S_GA + n + 1)
            pe.wait_ge(a_free[n % 2], 8 + n // 2)
            a_tile(S_GA + n, T1h, T1l, KT, 2 * (n % 2)).then_inc(w_used, 1)
        pe.wait_ge(s_step, 24)
        turn(("st",), [sTk[:, g, :] for g in range(NG)], 128)
        pe.wait_ge(qbd_ready, 1)
        b, full = open_bank(("sn",))
        for g in range(NG):
            for hp in range(2):
                last = mm(b[:, 32 * g:32 * g + 32], qbd[:, g, hp, :], akT[:, 2 * g + hp, SEQ:NTOK], start=hp == 0, stop=hp == 1)
        last.then_inc(full, 1)
        pe.wait_ge(s_probs, 1)
        turn(("sp",), [srow[:, g, 0:128] for g in range(NG)], 128)
        turn(("spn",), [srow[:, g, 128:160] for g in range(NG)], 128, 32)
        emptied(pe, ("sp",))
        emptied(pe, ("spn",))
        b, full = open_bank(("sv",))
        for n in range(24):
            bb, g = n // NG, n % NG
            m = 24 + n
            pe.wait_ge(kv_in[m % 3], 16 * (m // 3 + 1))
            q = bb // 2
            dst = b[32 * q:32 * q + 32, 0:256]
            if g == 0:
                last = mm(dst, pad0[:, 32 * bb:32 * bb + 32], kvr[:, m % 3, 0, :], start=bb % 2 == 0, stop=False)
            else:
                for t in range(DT):
                    last = mm(dst, pad1[:, g - 1, 32 * (4 * bb + t):32 * (4 * bb + t) + 32], kvr[:, m % 3, t, :],
                              start=False, stop=False)
            last.then_inc(v_used, 1)
            if g == 2 and bb % 2 == 1:
                for gg in range(NG):
                    last = mm(dst, pnew[0:TS, gg, 32 * q:32 * q + 32], avs[0:TS, 256 * gg:256 * gg + 256], start=False,
                              stop=gg == 2)
        last.then_inc(full, 1)
        pe.wait_ge(o_row, 1)
        turn(("so",), [orow[:, :]], 128, HD)
        pe.wait_ge(os_lo, 1)
        for n in range(KT):
            pe.wait_ge(w_lo, S_BA + n + 1)
            pe.wait_ge(a_free[n % 2], 12 + n // 2)
            a_tile(S_BA + n, aoh, aol, 2, 2 * (n % 2)).then_inc(w_used, 1)
        pe.wait_ge(mix_lo, KT)
        pe.wait_ge(a_free[0], 16)
        pe.wait_ge(a_free[1], 16)
        for nb in range(2):
            b_block(BLK_OUT + nb, lambda k, c: mTh[:, k, c], lambda k, c: mTl[:, k, c], lambda k: mTs[:, k, :])
        for i in range(TILES):
            pe.wait_ge(h_ready, i + 1)
            for half in range(2):
                turn(("h2", i, half), [hn[0:rows(i), i % 2, 128 * (4 * half + k):128 * (4 * half + k) + 128] for k in range(4)], rows(i))
        for i in range(TILES):
            pe.wait_ge(b_free[i], BLK_OUT + 2)
            for half in range(2):
                emptied(pe, ("h2", i, half))
        with pe.Fori(0, up_loop) as it:
            for q in range(2):
                for j in range(2):
                    pe.wait_ge(w_lo, it * 4 + (S_UP + 2 * q + j + 1))
                    pe.wait_ge(u_evac[j], it * 2 + q)
                    a_tile(j, T1h, T1l, KT, 2 * j).then_inc(w_used, 1)
        pe.wait_ge(f_lo, FT)
        pe.wait_ge(u_evac[0], FT)
        pe.wait_ge(u_evac[1], FT)
        pe.wait_ge(tail_done, 2 * FT + 4)
        tile = lambda t: t[:].rearrange("p (k n) -> p k n", k=FT)
        fh, fl, fs = tile(fTh), tile(fTl), tile(fTs)

        def conv_tail(s):
            if s < 11:
                turn18(s)

        def turn18(j):
            b, full = open_bank(("cv", j))
            for k in range(4):
                last = nc.tensor.transpose(b[0:18, 128 * k:128 * k + 128], cvt[:, 18 * (4 * j + k):18 * (4 * j + k) + 18], ident)
            last.then_inc(full, 1)

        b_block(BLK_DN, lambda k, c: fh[:, k, c], lambda k, c: fl[:, k, c], lambda k: fs[:, k, :], between=conv_tail)
        b_block(BLK_DN + 1, lambda k, c: fh[:, k, c], lambda k, c: fl[:, k, c], lambda k: fs[:, k, :])

    @block.vector
    def _(dve):
        v = nc.vector
        steps = [0]

        def step(ins):
            steps[0] += 1
            ins.then_inc(dve_step, 1)
            dve.wait_ge(dve_step, steps[0])

        def w_split(s):
            dve.wait_ge(w_hi, s + 1)
            w = slot_width(s)
            v.tensor_tensor(wlo[:, s % 2, 0:w], wraw[:, s % 2, 0:w], whi[:, s % 2, 0:w].bitcast(F), ALU.subtract
                            ).then_inc(w_lo, 1)

        def split_evac(key, Th, Tl, Ts, k0, i):
            b = filled(dve, key)
            n = rows(i)
            dve.wait_ge(split_hi, SPLIT_NO[key] + 1)
            src = b[:, 0:4 * n].rearrange("p (k n) -> p k n", k=4)
            hi = Th[:, k0:k0 + 4, cols(i)].bitcast(F)
            ins = v.tensor_tensor(Tl[:, k0:k0 + 4, cols(i)], src, hi, ALU.subtract)
            if i == 4:
                ins = v.tensor_tensor(Ts[:, k0:k0 + 4, 32:64], src, hi, ALU.subtract)
            ins.then_inc(bank_free[USES[key][0]], 1)

        def norm_scale(out, x, root, rs, gain):
            step(v.reciprocal(rs, root))
            return v.scalar_tensor_tensor(out, x, rs, gain, ALU.mult, ALU.mult)

        def sample_sum(bi, dst, scales, tmp=tmp_s):
            first, n = BLOCKS[bi][:2]
            dve.wait_ge(w_used, first + n)
            dve.wait_ge(tmp_ready, bi + 1)
            at_ = 0
            for w, scale in scales:
                ins = v.scalar_tensor_tensor(dst[:, at_:at_ + w], P[4][0:TS, at_:at_ + w], scale, tmp[0:TS, at_:at_ + w],
                                             ALU.mult, ALU.add)
                at_ += w
            ins.then_inc(b_free[4], 1)

        rope_tiles = [0]

        def rope(bi):
            buf = RBk if bi == BLK_RK else RBq
            for i in range(TILES):
                r = rows(i)
                dve.wait_ge(b_free[i], bi + 1)
                if rope_tiles[0]:
                    dve.wait_ge(rope_done, rope_tiles[0])
                rope_tiles[0] += 1
                if bi in (BLK_RQ, BLK_RK):
                    x = buf[0:r, i, :].rearrange("p (h s d) -> p h s d", h=RH, s=2)
                    tc = ropet[0:r, 0, :].rearrange("p (h s d) -> p h s d", h=RH, s=2)
                    tn = ropet[0:r, 1, :].rearrange("p (h s d) -> p h s d", h=RH, s=2)
                    cos = crv("rcos", TILES)[0:r, i, :].unsqueeze(1).broadcast_to([r, 8, 64])
                    sin = crv("rsin", TILES)[0:r, i, :].rearrange("p (s d) -> p s d", s=2)
                    v.tensor_tensor(ropet[0:r, 0, :].rearrange("p (k d) -> p k d", k=8),
                                    buf[0:r, i, :].rearrange("p (k d) -> p k d", k=8), cos, ALU.mult)
                    for side in range(2):
                        last = v.tensor_tensor(tn[:, :, side, :], x[:, :, 1 - side, :],
                                               sin[:, side, :].unsqueeze(1).broadcast_to([r, RH, 64]), ALU.mult)
                    step(last)
                    v.tensor_tensor(buf[0:r, i, :], ropet[0:r, 0, :], ropet[0:r, 1, :], ALU.add).then_inc(rope_done, 1)
                else:
                    x = buf[0:r, i, :].rearrange("p (h d) -> p h d", h=8)[:, :, 0:16]
                    tc = ropet[0:r, 0, 0:128].rearrange("p (h d) -> p h d", h=8)
                    tn = ropet[0:r, 1, 0:128].rearrange("p (h d) -> p h d", h=8)
                    cos = cav("acos", TILES)[0:r, i, :].unsqueeze(1).broadcast_to([r, 8, 16])
                    sin = cav("asin", TILES)[0:r, i, :]
                    v.tensor_tensor(tc, x, cos, ALU.mult)
                    for side in range(2):
                        last = v.tensor_tensor(tn[:, :, 8 * side:8 * side + 8], x[:, :, 8 - 8 * side:16 - 8 * side],
                                               sin[:, 8 * side:8 * side + 8].unsqueeze(1).broadcast_to([r, 8, 8]), ALU.mult)
                    step(last)
                    v.tensor_tensor(x, tc, tn, ALU.add).then_inc(rope_done, 1)

        w_split(0)
        w_split(1)
        dve.wait_ge(gpre_in, 16)
        for i in range(TILES):
            r = rows(i)
            dve.wait_ge(x_rt, i + 1)
            if i >= 2:
                filled(dve, ("x", i - 2, 1))
            norm_scale(xn[0:r, i % 2, :], xin[0:r, i, :], rt_x[0:r, i:i + 1], rs_x[0:r, i:i + 1], gpre[0:r]).then_inc(x_norm, 1)
            if i >= 1:
                for half in range(2):
                    split_evac(("x", i - 1, half), T1h, T1l, T1s, 4 * half, i - 1)
        for half in range(2):
            split_evac(("x", 4, half), T1h, T1l, T1s, 4 * half, 4)
        dve.wait_ge(cr_in, 16)
        dve.wait_ge(cleared, 4)

        sample_dst = {
            BLK_RQ: (RBq[0:TS, 4, :], ((512, 1.0),)), BLK_RK: (RBk[0:TS, 4, :], ((512, DK ** -0.5),)),
            BLK_RV: (vs[0:TS, 0:512], ((512, 1.0),)), BLK_RV + 1: (vs[0:TS, 512:1024], ((512, 1.0),)),
            BLK_AQ: (RBq[0:TS, 4, :], ((512, HD ** -0.5),)), BLK_AQK: (RBq[0:TS, 4, :], ((256, HD ** -0.5), (256, 1.0))),
            BLK_AK: (RBq[0:TS, 4, :], ((512, 1.0),)), BLK_AV: (avs[0:TS, 0:512], ((512, 1.0),)),
            BLK_AV2: (avs[0:TS, 512:768], ((256, 1.0),)),
        }

        def decayed(c):
            key = ("S", c)
            b = filled(dve, key)
            if c:
                filled(dve, ("O", c - 1, 1))
                v.tensor_tensor(qd[:], qT[:, :, cols(c)], crv("qdec", RH), ALU.mult).then_inc(qd_ready, 1)
            v.tensor_tensor(PT[:], b[:, :].rearrange("p (h n) -> p h n", h=RH), crv("decT", RH), ALU.mult
                            ).then_inc(bank_free[USES[key][0]], 1)

        def state_update(c, j):
            key = ("U", c, j)
            b = filled(dve, key)
            for e in range(2):
                h = 2 * j + e
                src = b[:, DV * e:DV * e + DV]
                if c == 0:
                    ins = v.tensor_copy(state[:, h, :], src)
                else:
                    ins = v.scalar_tensor_tensor(state[:, h, :], state[:, h, :], GAMMA_CHUNK[h], src, ALU.mult, ALU.add)
            ins.then_inc(bank_free[USES[key][0]], 1)

        def sample_queries(h):
            if h >= 2:
                filled(dve, ("Os", h - 2))
            dst = bass.AP(qm, (h % 2) * 256, [[512, 128], [36, NB], [1, DT]])
            v.tensor_tensor(dst, qT[:, h, SEQ:NTOK].rearrange("p (b t) -> p b t", t=DT),
                            crv("qdecs", RH)[:, h, :].rearrange("p (b t) -> p b t", t=DT), ALU.mult).then_inc(qm_ready, 1)

        for bi in range(BLK_RG):
            first, n = BLOCKS[bi][:2]
            for s in range(n - 1):
                w_split(first + s + 2)
                if 4 <= bi < 8:
                    if s == 0:
                        decayed(bi - 4)
                    if s == 2:
                        state_update(bi - 4, 0)
            dst, scales = sample_dst[bi]
            if bi == BLK_AQ:
                filled(dve, ("t", BLK_RQ, 4))
            if bi == BLK_AQK:
                filled(dve, ("t", BLK_AQ, 4))
                dve.wait_ge(qs_out, 16)
            if bi == BLK_AK:
                filled(dve, ("t", BLK_AQK, 4))
                dve.wait_ge(qs_out, 32)
                dve.wait_ge(k_out, 16 * 9)
            sample_sum_first = bi != BLK_AV2
            if sample_sum_first:
                sample_sum(bi, dst, scales)
                w_split(first + n + 1)
            if bi in ROPE_BLOCKS:
                rope(bi)
            if 4 <= bi < 8:
                state_update(bi - 4, 1)
            if bi == BLK_AV2:
                def sample_half(hs):
                    for h in hs:
                        for p in range(4):
                            key = ("Us", h, p)
                            b = filled(dve, key)
                            m = (4 * h + p) % 3
                            v.scalar_tensor_tensor(S0[:, m], S0[:, m], GAMMA_STEP[h],
                                                   b[:, :].rearrange("p (e n) -> p e n", e=2), ALU.mult, ALU.add
                                                   ).then_inc(bank_free[USES[key][0]], 1)
                        if h + 2 < RH:
                            sample_queries(h + 2)
                b = filled(dve, ("Ss",))
                v.tensor_tensor(PTs[0:TS], b[0:TS, 0:128].rearrange("p (h n) -> p h n", h=RH), crv("decTs", RH)[0:TS], ALU.mult
                                ).then_inc(bank_free[5], 1)
                sample_queries(0)
                sample_queries(1)
                sample_half((0, 1))
                sample_sum(bi, dst, scales)
                w_split(first + n + 1)
                sample_half((2, 3))
                dve.wait_ge(rt_ready, 1)
                step(v.reciprocal(rs_r[:], rt_r[:]))
                step(v.tensor_scalar(rs_r[:], rs_r[:], 0.5, None, ALU.mult))

        def gate_tile(g, i):
            k = 5 * g + i
            dve.wait_ge(e_ready, k + 1)
            if i < 4:
                t, e, x, out, r = etmp[:, i % 2, :], etmp[:, i % 2, :], P[i][:, :], vt[:, i, :], 128
                v.scalar_tensor_tensor(t, e, 1.0, x, ALU.add, ALU.mult).then_inc(b_free[i], 1)
                dve.wait_ge(b_free[i], BLK_RG + g + 1)
            else:
                t, e, x, out, r = etmp[0:TS, 0, :], tmp_s[0:TS, :], etmp[0:TS, 0, :], vs[0:TS, :], TS
                step(v.scalar_tensor_tensor(t, e, 1.0, x, ALU.add, ALU.mult))
            for hh in range(2):
                h = 2 * g + hh
                o_ = out[:, DV * h:DV * h + DV]
                last = v.scalar_tensor_tensor(o_, o_, rs_r[0:r, 4 * i + h:4 * i + h + 1], t[:, DV * hh:DV * hh + DV],
                                              ALU.mult, ALU.mult)
            last.then_inc(r_ready, 1)

        for g in range(2):
            bi = BLK_RG + g
            first, n = BLOCKS[bi][:2]
            for s in range(n - 1):
                w_split(first + s + 2)
                if g == 1 and s == 2:
                    for i in range(TILES):
                        split_evac(("r", 0, i), rTh, rTl, rTs, 0, i)
            dve.wait_ge(tmp_ready, bi + 1)
            for i in range(4):
                gate_tile(g, i)
            v.tensor_tensor(etmp[0:TS, 0, :], P[4][0:TS, :], tmp_s[0:TS, :], ALU.add).then_inc(b_free[4], 1)
            dve.wait_ge(b_free[4], bi + 1)
            gate_tile(g, 4)
            w_split(first + n + 1)

        masks = {1: cav("mask1"), 2: cav("mask2"), 0: cav("mask0")}

        def score_max(s):
            qb = s // 4
            at_ = 0
            for g in range(NG):
                gg = (1, 2, 0)[g]
                key = ("s", s, g)
                b = filled(dve, key)
                w = 128 * (qb + 1) if gg else 128 * min(qb + 1, 2)
                m = masks[gg]
                full_w = 512 if gg else 256
                last = v.tensor_tensor_reduce(out=sc[:, s % 2, at_:at_ + w], in0=b[:, 0:w], in1=m[:, full_w - w:full_w],
                                              scale=1.0, scalar=NEG, op0=ALU.add, op1=ALU.max,
                                              accum_out=mx[:, s % 2, g:g + 1])
                last.then_inc(bank_free[USES[key][0]], 1)
                at_ += w
            emptied(dve, ("s", s, 0))
            emptied(dve, ("s", s, 1))
            emptied(dve, ("s", s, 2))
            step(v.tensor_reduce(rden[:, s % 2:s % 2 + 1], mx[:, s % 2, 0:3], AX.X, ALU.max))
            v.tensor_scalar(nm[:, s % 2:s % 2 + 1], rden[:, s % 2:s % 2 + 1], -1.0, None, ALU.mult).then_inc(maxed, 1)

        def normalise(s):
            w = 128 * len(attention_blocks(s // 4))
            dve.wait_ge(exped, s + 1)
            step(v.reciprocal(rden[:, s % 2:s % 2 + 1], den[:, s % 2:s % 2 + 1]))
            v.tensor_scalar(sc[:, s % 2, 0:w], sc[:, s % 2, 0:w], rden[:, s % 2:s % 2 + 1], None, ALU.mult
                            ).then_inc(probs, 1)

        def gated(n, gate, src, out, frees):
            for half in range(2):
                c = slice(HALF * half, HALF * half + HALF)
                last = v.scalar_tensor_tensor(out[:, c], gate[:, c], 1.0, P[src + half][:, 0:HALF], ALU.add, ALU.mult)
            last.then_inc(frees, 1)

        def attended_lo(pair):
            qb, hp = pair // 2, pair % 2
            b = filled(dve, ("o", pair))
            dve.wait_ge(o_hi, pair + 1)
            c = slice(128 * qb, 128 * qb + 128)
            v.tensor_tensor(aol[:, hp, c], b[:, 0:128], aoh[:, hp, c].bitcast(F), ALU.subtract).then_inc(bank_free[7], 1)

        for s in range(17):
            if s < 16:
                if s >= 2:
                    filled(dve, ("pt", s - 2, turns(s - 2) - 1))
                if s == 0:
                    for i in range(TILES):
                        split_evac(("r", 1, i), rTh, rTl, rTs, 4, i)
                score_max(s)
                normalise(s)
                w_split(S_GB + s + 2)
                if s % 2:
                    n = s // 2
                    dve.wait_ge(w_used, S_GB + s + 1)
                    dve.wait_ge(a_free[0], n + 1)
                    gated(n, gexp[:, n % 2, :], 2, mixr[:, n, :], a_free[1])
            if s >= 2 and s % 2 == 0:
                attended_lo(s // 2 - 1)

        for n in range(24):
            if n % 3 == 0:
                w_split(S_GA + n // 3 + 2)
            b, g = n // NG, n % NG
            dve.wait_ge(kv_in[n % 3], 16 * (n // 3 + 1))
            dve.wait_ge(q_in[n % 2], 16 * (n // 2 + 1))
            if n:
                dve.wait_ge(s_step, n)
            keys = kvr[:, n % 3, 0, :].unsqueeze(1).broadcast_to([128, DT, 256]) if g == 0 else kvr[:, n % 3]
            step(v.tensor_tensor(prod[:].rearrange("p (t n) -> p t n", t=DT), keys, qbc[:, n % 2], ALU.mult))
            v.tensor_reduce(sTk[:, g, 16 * b:16 * b + 16], prod[:].rearrange("p (k d) -> p k d", d=HD), AX.X, ALU.add
                            ).then_inc(s_step, 1)
        b = filled(dve, ("st",))
        v.tensor_tensor(srow[:, 0, 0:128], b[:, 0:128], cav("ms0"), ALU.add)
        v.tensor_copy(srow[:, 1:3, 0:128], b[:, 128:384].rearrange("p (g n) -> p g n", g=2)).then_inc(bank_free[4], 1)
        b = filled(dve, ("sn",))
        v.tensor_tensor(srow[:, :, 128:160], b[:, 0:96].rearrange("p (g n) -> p g n", g=NG), cav("mnew", NG), ALU.add
                        ).then_inc(bank_free[5], 1)
        emptied(dve, ("sn",))
        step(v.tensor_reduce(rden[:, 0:1], srow[:], AX.XY, ALU.max))
        v.tensor_scalar(nm[:, 0:1], rden[:, 0:1], -1.0, None, ALU.mult).then_inc(s_max, 1)
        dve.wait_ge(s_exp, 1)
        step(v.reciprocal(rden[:, 1:2], den[:, 0:1]))
        v.tensor_scalar(srow[:], srow[:], rden[:, 1:2], None, ALU.mult).then_inc(s_probs, 1)
        b = filled(dve, ("sv",))
        v.tensor_tensor(osel[:], b[:, 0:256].rearrange("p (h d) -> p h d", h=AH),
                        cav("hsel").unsqueeze(2).broadcast_to([128, AH, HD]), ALU.mult).then_inc(bank_free[7], 1)
        emptied(dve, ("sv",))
        v.tensor_reduce(orow[:], osel[:].rearrange("p h d -> p d h"), AX.X, ALU.add).then_inc(o_row, 1)
        dve.wait_ge(os_hi, 1)
        v.tensor_tensor(aol[:, :, SEQ:NTOK], aosf[:], aoh[:, :, SEQ:NTOK].bitcast(F), ALU.subtract).then_inc(os_lo, 1)

        for n in range(KT):
            w_split(S_BA + n + 2)
            dve.wait_ge(w_used, S_BA + n + 1)
            p = n % 2
            if n >= 2:
                dve.wait_ge(mix_lo, n - 1)
            gated(n, sga[:, n, :], 2 * p, mtmp[:, p, :], a_free[p])
            dve.wait_ge(a_free[p], 13 + n // 2)
            v.tensor_tensor(mtmp[:, p, :], mtmp[:, p, :], mixr[:, n, :], ALU.add).then_inc(mix_sum, 1)
            dve.wait_ge(mix_hi, n + 1)
            v.scalar_tensor_tensor(mTl[:, n, :], mtmp[:, p, :], 0.5, mTh[:, n, :].bitcast(F), ALU.mult, ALU.subtract)
            v.scalar_tensor_tensor(mTs[:, n, 32:64], mtmp[:, p, SEQ:NTOK], 0.5, mTh[:, n, SEQ:NTOK].bitcast(F), ALU.mult, ALU.subtract
                            ).then_inc(mix_lo, 1)
        for nb in range(2):
            bi = BLK_OUT + nb
            first, n = BLOCKS[bi][:2]
            for s in range(n - 1):
                w_split(first + s + 2)
            sample_sum(bi, xo[0:TS, 4, 512 * nb:512 * nb + 512], ((512, 1.0),), tmp_s2)
            w_split(first + n + 1)
        dve.wait_ge(g2_in, 32)
        for i in range(TILES + 1):
            if i < TILES:
                r = rows(i)
                dve.wait_ge(x_again[i], 16)
                dve.wait_ge(n_rt, i + 1)
                step(norm_scale(tmpn[0:r, i % 2, :], xo[0:r, i, :], rt_n[0:r, i:i + 1], rs_n[0:r, i:i + 1], gpost[0:r]))
                v.tensor_tensor(xo[0:r, i, :], tmpn[0:r, i % 2, :], xr[0:r, i, :], ALU.add).then_inc(x2_ready, 1)
            if i:
                k = i - 1
                r = rows(k)
                dve.wait_ge(n_rt, TILES + k + 1)
                if k >= 2:
                    filled(dve, ("h2", k - 2, 1))
                norm_scale(hn[0:r, k % 2, :], xo[0:r, k, :], rt_n[0:r, 5 + k:6 + k], rs_n[0:r, 5 + k:6 + k], gffn[0:r]
                           ).then_inc(h_ready, 1)
            if i >= 2:
                for half in range(2):
                    split_evac(("h2", i - 2, half), T1h, T1l, T1s, 4 * half, i - 2)
        for half in range(2):
            split_evac(("h2", 4, half), T1h, T1l, T1s, 4 * half, 4)
        dve.wait_ge(convp_in, 16)
        dve.sem_inc(conv_done, 4)
        with dve.Fori(0, up_loop) as it:
            for q in range(2):
                for j in range(2):
                    t1 = 2 * q + j + 1
                    dve.wait_ge(w_hi, it * 4 + (S_UP + t1 + 2))
                    v.tensor_tensor(wlo[:, j, :], wraw[:, j, :], whi[:, j, :].bitcast(F), ALU.subtract).then_inc(w_lo, 1)
                    tile = it * 2 + (q + FT * j)
                    cp = convp[:].rearrange("p n c -> p (n c)")
                    tap = lambda k: cp[:, bass.ds(tile * 4 + k, 1)]
                    dve.wait_ge(u_evac[j], it * 2 + (q + 1))
                    dve.wait_ge(head_ready, it * 4 + t1)
                    if j == 0:
                        dve.wait_ge(f_lo, it * 2 + q)
                    v.tensor_scalar(cb[:, j, 0:CW], ub[:, q, j, 2:UW], tap(2), tap(3), ALU.mult, ALU.add).then_inc(conv_tap, 1)
                    dve.wait_ge(conv_tap, it * 8 + (2 * t1 - 1))
                    v.scalar_tensor_tensor(cb[:, j, 0:CW], ub[:, q, j, 1:UW - 1], tap(1), cb[:, j, 0:CW], ALU.mult, ALU.add
                                           ).then_inc(conv_tap, 1)
                    dve.wait_ge(conv_tap, it * 8 + 2 * t1)
                    v.scalar_tensor_tensor(cb[:, j, 0:CW], ub[:, q, j, 0:UW - 2], tap(0), cb[:, j, 0:CW], ALU.mult, ALU.add
                                           ).then_inc(conv_done, 1)
                pair = it * 2 + q
                dve.wait_ge(gelu_done, it * 2 + (q + 1))
                dve.wait_ge(conv_done, it * 4 + (2 * q + 6))
                v.tensor_tensor(cb[:, 0, 0:CW], cb[:, 0, 0:CW], cb[:, 1, 0:CW], ALU.mult).then_inc(f_done, 1)
                dve.wait_ge(f_hi, it * 2 + (q + 1))
                four = lambda t: t.rearrange("p (b t) -> p b t", t=4)
                hi_s = four(fTh[:, bass.ds(pair * NTOK + SEQ, TS)].bitcast(F))
                v.tensor_tensor(fTl[:, bass.ds(pair * NTOK, SEQ)], cb[:, 0, 0:SEQ], fTh[:, bass.ds(pair * NTOK, SEQ)].bitcast(F),
                                ALU.subtract)
                v.tensor_tensor(four(fTl[:, bass.ds(pair * NTOK + SEQ, TS)]), c_sample(cb[:, 0, :]), hi_s, ALU.subtract)
                v.tensor_tensor(four(fTs[:, bass.ds(pair * 64 + 32, TS)]), c_sample(cb[:, 0, :]), hi_s, ALU.subtract
                                ).then_inc(f_lo, 1)
        def conv_rows(j):
            key = ("cv", j)
            b = filled(dve, key)
            if j >= 2:
                dve.wait_ge(cv_out[j % 2], 32 * (j // 2))
            v.tensor_copy(cvrow[0:18, j % 2, :], b[0:18, :]).then_inc(bank_free[USES[key][0]], 1)

        for nb in range(2):
            bi = BLK_DN + nb
            first, n = BLOCKS[bi][:2]
            for s in range(n - 1):
                if first + s + 2 < NSLOT:
                    w_split(first + s + 2)
                if nb == 0:
                    conv_rows(s)
            if nb == 0:
                conv_rows(10)
            sample_sum(bi, fo[0:TS, 4, 512 * nb:512 * nb + 512], ((512, 1.0),), tmp_s3)
            if first + n + 1 < NSLOT:
                w_split(first + n + 1)
        dve.wait_ge(gfin_in, 16)
        for i in range(TILES):
            r = rows(i)
            dve.wait_ge(y_rt, i + 1)
            if i >= 2:
                dve.wait_ge(y_out[i % 2], 16 * (i // 2))
            step(norm_scale(ytmp[0:r, i % 2, :], fo[0:r, i, :], rt_n[0:r, 10 + i:11 + i], rs_n[0:r, 10 + i:11 + i], gfin[0:r]))
            v.tensor_tensor(ytmp[0:r, i % 2, :], ytmp[0:r, i % 2, :], xo[0:r, i, :], ALU.add).then_inc(y_ready, 1)

    ctx.close()


_INS = ("x_prompt", "x_sample", "cache_kv_g0", "cache_kv_g1", "cache_kv_g2", "state_ret", "norm_mix_pre",
        "norm_mix_post", "norm_ffn_pre", "norm_ffn_post")
_OUTS = (("y_prompt", (1, SEQ, D)), ("y_sample", (NB, DT, D)),
         ("p_kv_g0", (1, 1, 128, 2, AH, HD)), ("p_kv_g1", (1, 1, 512, 2, AH, HD)), ("p_kv_g2", (1, 1, 512, 2, AH, HD)),
         ("p_ret", (1, 1, RH, DK, DV)), ("p_conv", (1, 1, 2, 2 * DFF)),
         ("s_kv_g0", (1, NB, 128, 2, AH, HD)), ("s_kv_g1", (1, NB, 512, 2, AH, HD)), ("s_kv_g2", (1, NB, 2048, 2, AH, HD)),
         ("s_ret", (1, NB, RH, DK, DV)), ("s_conv", (1, NB, 2, 2 * DFF)))


def weight_stream(w_in, w_branch_ret, w_branch_attn, w_out, w_ffn_up, w_ffn_down):
    def b_slots(w, per):
        k, n = w.shape
        return w.reshape(k // (128 * per), per, 128, n).transpose(0, 2, 1, 3).reshape(-1, 128, per * n)

    def a_slots(w):
        k, n = w.shape
        return w.reshape(k // 128, 128, n // 128, 128).transpose(2, 1, 0, 3).reshape(n // 128, 128, k)

    rq, rk, rv, rg, aq, ak, av, gr, ga = np.split(w_in, np.cumsum([512, 512, 1024, 1024, 768, 768, 768, 1024])[:8], axis=1)
    ret = np.concatenate([rq, rk, rv], 1)
    att = np.concatenate([aq, ak, av], 1)
    parts = [b_slots(ret[:, 512 * n:512 * n + 512], 2) for n in range(4)]
    parts += [b_slots(att[:, 512 * n:512 * n + 512], 2) for n in range(4)]
    parts.append(b_slots(att[:, 2048:], 4))
    parts += [b_slots(rg[:, 512 * n:512 * n + 512], 2) for n in range(2)]
    parts.append(np.stack([a_slots(gr), a_slots(w_branch_ret)], 1).reshape(-1, 128, SLOT))
    parts.append(a_slots(ga))
    parts.append(np.pad(a_slots(w_branch_attn), ((0, 0), (0, 0), (0, SLOT - BA_W))))
    parts += [b_slots(w_out[:, 512 * n:512 * n + 512], 2) for n in range(2)]
    up = a_slots(w_ffn_up)
    parts.append(np.stack([up[:FT], up[FT:]], 1).reshape(-1, 128, SLOT))
    parts += [b_slots(w_ffn_down[:, 512 * n:512 * n + 512], 2) for n in range(2)]
    return np.concatenate(parts, 0)


def kernel(**inputs):
    import concourse.bacc as bacc
    from concourse.bass_utils import run_bass_kernel_spmd

    inp = {k: np.asarray(x) for k, x in inputs.items()}
    tables, tables_ret = constant_tables()
    arrays = {k: np.ascontiguousarray(inp[k]) for k in _INS}
    arrays["weights"] = weight_stream(*(inp[k][0] for k in ("w_in", "w_branch_ret", "w_branch_attn", "w_out", "w_ffn_up",
                                                            "w_ffn_down")))
    cw = np.concatenate([inp["conv_w"][0], inp["conv_b"]], 0)
    arrays["conv_params"] = np.ascontiguousarray(cw.reshape(4, 2 * FT, 128).transpose(2, 1, 0))
    arrays["conv_state"] = np.ascontiguousarray(
        inp["state_conv"][0].reshape(NB * 2, 2 * FT, 128).transpose(2, 1, 0).reshape(128, -1))
    arrays["tables"], arrays["tables_ret"] = tables, tables_ret

    nc = bacc.Bacc("TRN2", target_bir_lowering=False, num_devices=1)
    f32 = mybir.dt.float32
    a = {k: nc.dram_tensor(f"in_{k}", x.shape, f32, kind="ExternalInput").ap() for k, x in arrays.items()}
    o = {k: nc.dram_tensor(f"out_{k}", shape, f32, kind="ExternalOutput").ap() for k, shape in _OUTS}
    build_layer(nc, a, o)
    r = run_bass_kernel_spmd(nc, [{f"in_{k}": x for k, x in arrays.items()}], core_ids=[0])
    return tuple(r.results[0][f"out_{k}"] for k, _ in _OUTS)
```

```python
import math
from contextlib import ExitStack

import numpy as np
import concourse.bass as bass
from concourse import mybir

D = 1024
KT = D // 128
SEQ = 512
NB = 8
DT = 4
TS = NB * DT
NTOK = SEQ + TS
HALF = NTOK // 2
TILES = 5
PAST = 4096
RH, DK, DV, CHUNK = 4, 128, 256, 128
GROUPS = ((128, 1), (512, 4), (2048, 16))
NG, AH, HD = 3, 4, 64
DFF = 2816
FT = DFF // 128
EPS = 1e-6
SLOT = 1024
NEG = -1e30

S_RET, S_ATT, S_RG, S_GB, S_GA, S_BA = 0, 16, 34, 42, 58, 66
S_OUT = S_BA + 8
S_UP = S_OUT + 8
S_DN = S_UP + 2 * FT
NSLOT = S_DN + FT
BA_W = 256

BLOCKS = ([(S_RET + 4 * n, 4, 2, 512) for n in range(4)] + [(S_ATT + 4 * n, 4, 2, 512) for n in range(4)]
          + [(S_ATT + 16, 2, 4, 256)] + [(S_RG + 4 * n, 4, 2, 512) for n in range(2)]
          + [(S_OUT + 4 * n, 4, 2, 512) for n in range(2)] + [(S_DN + 11 * n, 11, 2, 512) for n in range(2)])
BLK_RQ, BLK_RK, BLK_RV, BLK_AQ, BLK_AQK, BLK_AK, BLK_AV, BLK_AV2, BLK_RG, BLK_OUT, BLK_DN = 0, 1, 2, 4, 5, 6, 7, 8, 9, 11, 13
ROPE_BLOCKS = (BLK_RQ, BLK_RK, BLK_AQ, BLK_AQK, BLK_AK)


def rows(i):
    return 128 if i < 4 else TS


def cols(i):
    return slice(128 * i, 128 * i + rows(i))


def attention_blocks(qb):
    return ([(1, kb) for kb in range(qb + 1)] + [(2, kb) for kb in range(qb + 1)]
            + [(0, kb) for kb in range(max(qb - 1, 0), qb + 1)])


def turns(s):
    return -(-len(attention_blocks(s // 4)) // 4)


def psum_uses():
    order = []
    for i in range(TILES):
        for half in range(2):
            order.append((("x", i, half), 5 + (2 * i + half) % 3))
    turned = lambda b: [(("t", b, i), 5 + i % 3) for i in range(TILES)]
    order += turned(BLK_RQ) + turned(BLK_RK)
    for c in range(4):
        order.append((("S", c), 5))
        if c == 0:
            order.append((("Ss",), 6))
        else:
            order += turned(BLK_AQ + c - 1)
        order += [(("O", c, 0), 6), (("O", c, 1), 7), (("U", c, 0), 5), (("U", c, 1), 5)]
        order += [(("Os", c), 6)] + [(("Us", c, p), (7, 5)[p % 2]) for p in range(4)]
    for g in range(2):
        order += [(("r", g, i), 5 + i % 3) for i in range(TILES)]
    order += [(("s", 0, g), 4 + g) for g in range(NG)]
    for st in range(17):
        if st:
            order += [(("pt", st - 1, j), 4 + j) for j in range(turns(st - 1))]
            if st % 2 == 0:
                order.append((("o", st // 2 - 1), 7))
        if st < 15:
            order += [(("s", st + 1, g), 4 + g) for g in range(NG)]
    order += [(("st",), 4), (("sn",), 5), (("sp",), 6), (("spn",), 4), (("sv",), 7), (("so",), 5)]
    for i in range(TILES):
        for half in range(2):
            order.append((("h2", i, half), 5 + (2 * i + half) % 3))
    order += [(("cv", j), 5 + j % 3) for j in range(2 * FT // 4)]
    seen, out = {}, {}
    for key, bank in order:
        out[key] = (bank, seen.get(bank, 0))
        seen[bank] = seen.get(bank, 0) + 1
    return out


USES = psum_uses()
SPLIT_KEYS = [k for k in USES if k[0] in ("x", "r", "h2")]
SPLIT_NO = {k: n for n, k in enumerate(SPLIT_KEYS)}


CA_FIELDS = (("ident", 128), ("acos", TILES * 16), ("asin", TILES * 16), ("mask1", 512), ("mask2", 512),
             ("mask0", 256), ("ms0", 128), ("mnew", NG * 32), ("hsel", 4))
CR_FIELDS = (("rcos", TILES * 64), ("rsin", TILES * 128), ("decT", RH * 128), ("qdec", RH * 128), ("kdec", RH),
             ("decTs", RH * 32), ("qdecs", RH * 32), ("kdecs", RH * NB))


def places(fields):
    out, at = {}, 0
    for name, n in fields:
        out[name] = (at, n)
        at += n
    return out, at


CA_AT, CA_N = places(CA_FIELDS)
CR_AT, CR_N = places(CR_FIELDS)


def constant_tables():
    f32 = np.float32
    ca, cr = np.zeros((128, CA_N), f32), np.zeros((128, CR_N), f32)

    def put(a, at, name, v):
        o, n = at[name]
        v = np.asarray(v, np.float64)
        a[:v.shape[0], o:o + n] = v.reshape(v.shape[0], n).astype(f32)

    pos = np.zeros((TILES, 128), f32)
    pos[:4] = np.arange(SEQ).reshape(4, 128)
    pos[4, :TS] = PAST + np.arange(TS) % DT
    af = (np.float64(500000.0) ** (-(np.arange(8, dtype=f32) / f32(8)).astype(np.float64))).astype(f32)
    ang = (pos[:, :, None] * af).astype(f32).astype(np.float64)
    put(ca, CA_AT, "acos", np.concatenate([np.cos(ang), np.cos(ang)], -1).transpose(1, 0, 2))
    put(ca, CA_AT, "asin", np.concatenate([-np.sin(ang), np.sin(ang)], -1).transpose(1, 0, 2))
    rf = (np.float64(10000.0) ** (-(np.arange(64, dtype=f32) * f32(1 / 63)).astype(np.float64))).astype(f32)
    ang = (pos[:, :, None] * rf).astype(f32).astype(np.float64)
    put(cr, CR_AT, "rcos", np.cos(ang).transpose(1, 0, 2))
    put(cr, CR_AT, "rsin", np.concatenate([-np.sin(ang), np.sin(ang)], -1).transpose(1, 0, 2))
    put(ca, CA_AT, "ident", np.eye(128))
    i, j = np.arange(128)[:, None], np.arange(128)[None, :]
    for name, dil in (("mask1", 4), ("mask2", 16)):
        off = np.where((i - j) % dil == 0, 0.0, NEG)
        diag = np.where(((i - j) % dil == 0) & (j <= i), 0.0, NEG)
        put(ca, CA_AT, name, np.concatenate([off, off, off, diag], 1))
    put(ca, CA_AT, "mask0", np.concatenate([np.where(j >= i, 0.0, NEG), np.where(j <= i, 0.0, NEG)], 1))
    p = np.arange(128)
    b, t, h = p // 16, p // 4 % 4, p % 4
    put(ca, CA_AT, "ms0", np.where(j >= t[:, None], 0.0, NEG))
    kb, kt = np.arange(TS)[None] // 4, np.arange(TS)[None] % 4
    same = kb == b[:, None]
    m0 = np.where(same & (kt <= t[:, None]), 0.0, NEG)
    m1 = np.where(same & (kt == t[:, None]), 0.0, NEG)
    put(ca, CA_AT, "mnew", np.stack([m0, m1, m1], 1))
    put(ca, CA_AT, "hsel", (h[:, None] == np.arange(4)[None]).astype(f32))
    lg = log_decay()
    dec = np.where(j[None] >= i[None], np.exp(lg[:, None, None] * np.maximum(j - i, 0)[None]), 0.0)
    put(cr, CR_AT, "decT", dec.transpose(1, 0, 2))
    put(cr, CR_AT, "qdec", np.broadcast_to(np.exp(lg[:, None] * (np.arange(128) + 1.0))[None], (128, 4, 128)))
    put(cr, CR_AT, "kdec", np.exp(lg[None] * (127.0 - np.arange(128))[:, None]))
    sj, si = np.arange(TS)[:, None], np.arange(TS)[None, :]
    ok = (sj // 4 == si // 4) & (sj <= si)
    dec = np.where(ok[None], np.exp(lg[:, None, None] * np.maximum(si - sj, 0)[None]), 0.0)
    put(cr, CR_AT, "decTs", dec.transpose(1, 0, 2))
    put(cr, CR_AT, "qdecs", np.broadcast_to(np.exp(lg[:, None] * (np.arange(TS) % 4 + 1.0))[None], (128, 4, TS)))
    kd = np.exp(lg[None] * (3.0 - np.arange(TS) % 4)[:, None])
    put(cr, CR_AT, "kdecs", kd[:, :, None] * (np.arange(TS)[:, None, None] // 4 == np.arange(NB)[None, None]))
    return ca, cr


def log_decay():
    return np.log1p(-np.exp2(-5.0 - np.arange(RH)))


GAMMA_CHUNK = [float(x) for x in np.exp(log_decay() * CHUNK)]
GAMMA_STEP = [float(x) for x in np.exp(log_decay() * DT)]


def build_layer(nc, a, o, phases=99):
    F, R = mybir.dt.float32, mybir.dt.float32r
    ALU, ACT, AX = mybir.AluOpType, mybir.ActivationFunctionType, mybir.AxisListType
    ctx = ExitStack()

    base = 16512

    def sb(name, at, shape, dt=F):
        return nc.alloc_sbuf_tensor_at(name, shape, dt, offset=base + 4 * at)

    T1h = sb("T1h", 0, [128, KT, NTOK], R)
    T1l = sb("T1l", 4352, [128, KT, NTOK], R)
    T1s = sb("T1s", 8704, [128, KT, 64], R)
    wraw = sb("wraw", 9216, [128, 2, SLOT])
    whi = sb("whi", 11264, [128, 2, SLOT], R)
    wlo = sb("wlo", 13312, [128, 2, SLOT], R)
    CA0 = 15360
    ca_t = sb("ca", CA0, [128, CA_N])
    CONVP = CA0 + (CA_N + 7) // 8 * 8
    convp = sb("convp", CONVP, [128, 2 * FT, 4])
    STAT = CONVP + 8 * FT
    stat = sb("stat", STAT, [128, 136])
    col = lambda n, w: stat[:, n:n + w]
    ss_x, rt_x, rs_x = (col(5 * k, 5) for k in range(3))
    ss_r, rt_r, rs_r = (col(16 + 20 * k, 20) for k in range(3))
    mx = col(76, 8).rearrange("p (a b) -> p a b", a=2)
    nm, den, rden = col(84, 2), col(86, 2), col(88, 2)
    ss_n, rt_n, rs_n = (col(90 + 15 * k, 15) for k in range(3))
    eps = col(135, 1)
    assert CR_N <= 2304
    X = (STAT + 136 + 7) // 8 * 8
    ATT = X + 17168
    SCR = ATT + 10368
    END = (229368 - base) // 4
    assert SCR + 8200 <= END, (SCR, END)
    cr_t = sb("cr", X, [128, CR_N])
    QT = X + 2304
    qT = sb("qT", QT, [128, RH, NTOK])
    kT = sb("kT", QT + 2176, [128, RH, NTOK])
    RBk = sb("rope_k", QT + 4352, [128, TILES, 512])
    V0 = QT + 6912
    vt = sb("v", V0, [128, 4, D])
    vs = sb("v_s", V0 + 4096, [128, D])
    RBq = sb("rope_q", V0 + 5120, [128, TILES, 512])
    assert V0 + 7680 <= ATT
    aqT = sb("aqT", ATT, [128, 6, NTOK])
    akT = sb("akT", ATT + 3264, [128, 6, NTOK])
    av = sb("av", ATT + 6528, [128, 4, 768])
    avs = sb("av_s", ATT + 9600, [128, 768])
    xin = sb("xin", ATT, [128, TILES, D])
    gpre = sb("gpre", ATT + 5120, [128, D])
    xn = sb("xn", ATT + 6144, [128, 2, D])
    junk = sb("junk", ATT + 8192, [128, D])
    at = SCR
    tmp_s = sb("tmp_s", at, [128, 512]); at += 512
    ropet = sb("ropet", at, [128, 2, 512]); at += 1024
    PT = sb("PT", at, [128, RH, 128]); at += 512
    kd = sb("kd", at, [128, 512]); at += 512
    qd = sb("qd", at, [128, RH, 128]); at += 512
    state = sb("state", at, [128, RH, DV]); at += 1024
    S0 = sb("S0", at, [128, 4, 2, DV]); at += 2048
    qm = sb("qm", at, [128, 2, NB, 32]); at += 512
    km = sb("km", at, [128, NB, 128]); at += 1024
    rjunk = sb("rjunk", at, [128, DV]); at += 256
    PTs = sb("PTs", at, [128, RH, 32]); at += 128
    assert at <= END, (at, END)
    rTh = sb("rTh", X, [128, KT, NTOK], R)
    rTl = sb("rTl", X + 4352, [128, KT, NTOK], R)
    rTs = sb("rTs", X + 8704, [128, KT, 64], R)
    assert X + 9216 <= V0
    etmp = sb("etmp", SCR + 512, [128, 2, 512])
    mixr = sb("mixr", V0, [128, KT, NTOK])
    gexp = sb("gexp", V0 + 5120, [128, NTOK])
    at = SCR
    sc = sb("sc", at, [128, 2, 1280]); at += 2560
    pT = sb("pT", at, [128, 1280]); at += 1280
    qpad = sb("qpad", at, [128, 2, NG, 128]); at += 768
    aoh = sb("aoh", at, [128, 2, NTOK], R); at += 2 * NTOK
    aol = sb("aol", at, [128, 2, NTOK], R); at += 2 * NTOK
    qbc = [sb("qbc0", at, [128, 2, 256]), sb("qbc1", at + 512, [128, 2, 256])]; at += 1024
    sTk = sb("sTk", at, [128, NG, 128]); at += 384
    assert at <= END
    kvk = sb("kvk", V0 + 5664, [128, 3, 2, 256])
    prod = sb("prod", V0 + 7200, [128, 512])
    qbc.append(sb("qbc2", V0 + 4352, [128, 2, 256]))
    assert V0 + 7712 <= ATT
    sga = sb("sga", X, [128, KT, NTOK])
    kvv = (sb("kvv0", ATT + 6528, [128, 3, DT, 256]), sb("kvv1", X + 4352, [128, 3, DT, 256]))
    srow = sb("srow", X + 7808, [128, NG, 160])
    at = SCR
    pad0 = sb("pad0", at, [128, 256]); at += 256
    pad1 = sb("pad1", at, [128, 2, 1024]); at += 2048
    pnew = sb("pnew", at, [128, NG, 128]); at += 384
    qbd = sb("qbd", at, [128, NG, 2, 128]); at += 768
    osel = sb("osel", at, [128, 4, HD]); at += 256
    orow = sb("orow", at, [128, HD]); at += 64
    aosf = sb("aosf", at, [128, 2, 32]); at += 64
    assert at <= SCR + 3840
    MT = ATT
    mTh = sb("mTh", MT, [128, KT, NTOK], R)
    mTl = sb("mTl", MT + 4352, [128, KT, NTOK], R)
    mTs = sb("mTs", MT + 8704, [128, KT, 64], R)
    mtmp = sb("mtmp", SCR, [128, 2, NTOK])
    xo = sb("xo", X, [128, TILES, D])
    xr = sb("xr", X + 5120, [128, TILES, D])
    gpost = sb("gpost", X + 10240, [128, D])
    gffn = sb("gffn", X + 11264, [128, D])
    tmpn = sb("tmpn", SCR + 1200, [128, 2, D])
    hn = sb("hn", SCR + 3248, [128, 2, D])
    njunk = sb("njunk", SCR + 5296, [128, D])
    tmp_s2 = sb("tmp_s2", SCR + 6400, [128, 512])
    fTh = sb("fTh", X + 5120, [128, FT * NTOK], R)
    fTl = sb("fTl", X + 17088, [128, FT * NTOK], R)
    fTs = sb("fTs", X + 29056, [128, FT * 64], R)
    U0 = X + 30464
    UW = 2 + SEQ + NB * 6
    CW = UW - 2
    ub = sb("u", U0, [128, 2, 2, UW])
    cb = sb("c", U0 + 4 * UW, [128, 2, UW])
    cvt = sb("cv_tail", U0 + 3376, [128, 2 * FT * 18])
    cvs = sb("cv_state", U0 + 3376 + 36 * FT, [128, 2 * FT * 16])
    assert U0 + 3376 + 68 * FT <= END
    fo = sb("fo", 0, [128, TILES, D])
    gfin = sb("gfin", 5120, [128, D])
    ytmp = sb("ytmp", 6144, [128, 2, D])
    tmp_s3 = sb("tmp_s3", 8192, [128, 512])
    fjunk = sb("fjunk", U0, [128, D])
    cvrow = sb("cv_row", U0 + 1024, [128, 2, 512])
    assert U0 + 2048 <= U0 + 6 * UW

    def cav(name, *shape):
        off, n = CA_AT[name]
        v = ca_t[:, off:off + n]
        return v.rearrange("p (a b) -> p a b", a=shape[0]) if shape else v

    def crv(name, *shape):
        off, n = CR_AT[name]
        v = cr_t[:, off:off + n]
        return v.rearrange("p (a b) -> p a b", a=shape[0]) if shape else v

    ident = cav("ident")
    P = [ctx.enter_context(nc.psum_tensor(f"bank{n}", [128, 512], F)) for n in range(8)]

    def sem(name):
        return ctx.enter_context(nc.semaphore(name))

    w_raw = [sem(f"w_raw{n}") for n in range(2)]
    w_hi, w_lo, w_used = sem("w_hi"), sem("w_lo"), sem("w_used")
    b_free = [sem(f"b_free{i}") for i in range(TILES)]
    a_free = [sem(f"a_free{n}") for n in range(2)]
    bank_full = {n: sem(f"bank_full{n}") for n in range(4, 8)}
    bank_free = {n: sem(f"bank_free{n}") for n in range(4, 8)}
    split_hi = sem("split_hi")
    x_in = [sem(f"x_in{i}") for i in range(TILES)]
    x_again = [sem(f"x_again{i}") for i in range(TILES)]
    ca_in, cr_in, gpre_in, convp_in = sem("ca_in"), sem("cr_in"), sem("gpre_in"), sem("convp_in")
    g2_in, gfin_in, cvs_in = sem("g2_in"), sem("gfin_in"), sem("cvs_in")
    act_step, dve_step, pool_step = sem("act_step"), sem("dve_step"), sem("pool_step")
    x_sq, x_rt, x_norm = sem("x_sq"), sem("x_rt"), sem("x_norm")
    tmp_ready = sem("tmp_ready")
    rope_done = sem("rope_done")
    cleared = sem("cleared")
    kd_ready, qd_ready, qm_ready, km_ready = sem("kd_ready"), sem("qd_ready"), sem("qm_ready"), sem("km_ready")
    s0_in = [sem(f"s0_in{n}") for n in range(4)]
    s1_out = [sem(f"s1_out{n}") for n in range(4)]
    on_sq, rt_ready = sem("on_sq"), sem("rt_ready")
    e_ready, r_ready = sem("e_ready"), sem("r_ready")
    k_out = sem("k_out")
    qs_out = sem("qs_out")
    av_out = sem("av_out")
    out_done = sem("out_done")
    windows_moved = sem("windows_moved")
    q_padded, maxed, exped, probs = sem("q_padded"), sem("maxed"), sem("exped"), sem("probs")
    o_hi = sem("o_hi")
    kk_in = [sem(f"kk_in{n}") for n in range(3)]
    kv_in = [sem(f"kv_in{n}") for n in range(6)]
    q_in = [sem(f"q_in{n}") for n in range(3)]
    s_step, pads_ready, qbd_ready, v_used, s_probs = (sem("s_step"), sem("pads_ready"), sem("qbd_ready"),
                                                     sem("v_used"), sem("s_probs"))
    s_max, s_exp, o_row, os_hi, os_lo = (sem(n) for n in ("s_max", "s_exp", "o_row", "os_hi", "os_lo"))
    mix_sum, mix_hi, mix_lo = sem("mix_sum"), sem("mix_hi"), sem("mix_lo")
    n_sq, n_rt, x2_ready, h_ready = sem("n_sq"), sem("n_rt"), sem("x2_ready"), sem("h_ready")
    u_evac = [sem(f"u_evac{n}") for n in range(2)]
    conv_done, tail_done, head_ready, conv_tap = sem("conv_done"), sem("tail_done"), sem("head_ready"), sem("conv_tap")
    gelu_done, f_done, f_hi, f_lo = sem("gelu_done"), sem("f_done"), sem("f_hi"), sem("f_lo")
    y_sq, y_rt, y_ready = sem("y_sq"), sem("y_rt"), sem("y_ready")
    y_out = [sem(f"y_out{n}") for n in range(2)]
    cv_out = [sem(f"cv_out{n}") for n in range(2)]

    def emptied(eng, key):
        bank, n = USES[key]
        eng.wait_ge(bank_free[bank], n + 1)

    def filled(eng, key):
        bank, n = USES[key]
        eng.wait_ge(bank_full[bank], n + 1)
        return P[bank]

    def c_sample(c):
        return c[:, 2 + SEQ:UW].rearrange("p (b t) -> p b t", t=6)[:, :, 0:4]

    def slot_width(s):
        return BA_W if S_BA <= s < S_OUT else SLOT

    w_dram, kv_dram = a["weights"], [a[f"cache_kv_g{g}"] for g in range(NG)]
    qs_dram = nc.dram_tensor("sample_queries", [TS, 768], F).ap()
    new_kv_dram = nc.dram_tensor("sample_keys_values", [TS, 2, 768], F).ap()
    up_loop = 2 * FT // 4

    def last_b_free(eng, i, n):
        eng.wait_ge(b_free[i], n)

    block = ctx.enter_context(nc.Block())

    @block.sync
    def _(sp):
        for i in range(TILES):
            r = rows(i)
            sp.dma_start(xin[0:r, i, :], a["x_prompt"][0, 128 * i:128 * i + 128, :] if i < 4 else
                         a["x_sample"].rearrange("b t d -> (b t) d")).then_inc(x_in[i], 16)
            if i == 0:
                sp.dma_start(gpre[:], a["norm_mix_pre"].broadcast_to([128, D])).then_inc(gpre_in, 16)
                sp.dma_start(ca_t[:], a["tables"]).then_inc(ca_in, 16)
            if i < 2:
                sp.dma_start(wraw[:, i, :], w_dram[i]).then_inc(w_raw[i], 16)
        sp.dma_start(cr_t[:], a["tables_ret"]).then_inc(cr_in, 16)
        sp.dma_start(convp[:], a["conv_params"]).then_inc(convp_in, 16)

        def load(slot):
            for j in range(2):
                sp.wait_ge(w_lo, slot + (j - 1))
                src = w_dram[bass.ds(slot + j, 1)].rearrange("a p n -> p (a n)")
                sp.dma_start(wraw[:, j, :], src).then_inc(w_raw[j], 16)

        def move(g, b, piece, pieces):
            n = (GROUPS[g][0] - DT) * 512 // pieces
            inner = {0: 1, 1: 1, 2: 7}[g]
            flat = lambda t: t[0, bass.ds(b, 1)].rearrange("a w c h d -> (a w c h d)")
            cut = lambda t, at_: flat(t)[at_ + n * piece:at_ + n * piece + n].rearrange("(e r c) -> e r c", e=16, r=inner)
            sp.dma_start(cut(o[f"s_kv_g{g}"], 0), cut(kv_dram[g], DT * 512)).then_inc(windows_moved, 16)

        with sp.Fori(0, NB) as b:
            for e in range(8):
                load(b * 16 + (2 + 2 * e))
                move(2, b, e, 8)
                if e % 4 == 1:
                    move(1, b, e // 4, 2)
                if e == 3:
                    move(0, b, 0, 1)
        with sp.Fori(0, (NSLOT - 130) // 2) as it:
            load(it * 2 + 130)
        sp.wait_ge(k_out, 16 * (NG + 2))
        sp.wait_ge(av_out, 16 * (NG + 1))
        for g in range(NG):
            W = GROUPS[g][0]
            for which in range(2):
                sp.dma_start(o[f"s_kv_g{g}"][0, :, W - DT:W, which].rearrange("b t h d -> b t (h d)"),
                             new_kv_dram[:, which, 256 * g:256 * g + 256].rearrange("(b t) n -> b t n", b=NB)
                             ).then_inc(windows_moved, 16)
        sp.wait_ge(windows_moved, 16 * (NB * (8 + 2 + 1) + 2 * NG))

    @block.gpsimd
    def _(pool):
        steps = [0]

        def step(ins):
            steps[0] += 1
            ins.then_inc(pool_step, 1)
            pool.wait_ge(pool_step, steps[0])

        stores = [0]

        def store(dst, src):
            stores[0] += 1
            pool.dma_start(dst, src).then_inc(out_done, 16)

        nc.gpsimd.memset(ss_r[:], 1.0).then_inc(cleared, 1)
        nc.gpsimd.memset(eps[:], EPS).then_inc(cleared, 1)
        nc.gpsimd.memset(vs[:], 0.0).then_inc(cleared, 1)
        nc.gpsimd.memset(qm[:], 0.0).then_inc(cleared, 1)
        nc.gpsimd.memset(km[:], 0.0).then_inc(cleared, 1)
        state_in = a["state_ret"]
        state_out = o["s_ret"]

        def load_state(h, p):
            if h:
                pool.wait_ge(s1_out[p], 16 * h)
            pool.dma_start(S0[:, p], state_in[0, 2 * p:2 * p + 2, h].rearrange("b k v -> k b v")
                           ).then_inc(s0_in[p], 16)

        def store_prompt(which, g, prompt, signal):
            dst = o[f"p_kv_g{g}"][0, 0, :, which].rearrange("(n p) h d -> p n (h d)", p=128)
            pool.dma_start(dst, prompt[:, 4 - min(GROUPS[g][0], SEQ) // 128:4]).then_inc(signal, 16)

        pool.wait_ge(w_used, 2)
        for q in range(4):
            load_state(0, q)
        pool.wait_ge(cr_in, 16)
        pool.wait_ge(cleared, 5)
        pool.wait_ge(rope_done, 10)
        for c in range(4):
            if c:
                filled(pool, ("U", c - 1, 1))
            nc.gpsimd.tensor_tensor(kd[:].rearrange("p (h d) -> p h d", h=RH),
                                    RBk[:, c, :].rearrange("p (h d) -> p h d", h=RH),
                                    crv("kdec").unsqueeze(2).broadcast_to([128, RH, 128]), ALU.mult
                                    ).then_inc(kd_ready, 1)
            if c:
                filled(pool, ("Us", c - 1, 3))
            nc.gpsimd.tensor_tensor(km[0:TS], RBk[0:TS, 4, 128 * c:128 * c + 128].unsqueeze(1).broadcast_to([TS, NB, 128]),
                                    crv("kdecs", RH)[0:TS, c, :].unsqueeze(2).broadcast_to([TS, NB, 128]), ALU.mult
                                    ).then_inc(km_ready, 1)
            if c >= 1:
                pool.wait_ge(rope_done, 10 + 5 * c)
                if c == 1:
                    pool.dma_start(qs_dram[:, 0:512], RBq[0:TS, 4, :]).then_inc(qs_out, 16)
                elif c == 2:
                    pool.dma_start(qs_dram[:, 512:768], RBq[0:TS, 4, 0:256]).then_inc(qs_out, 16)
                    store_prompt(0, 0, RBq[:, 0:4, 256:512], k_out)
                    pool.dma_start(new_kv_dram[:, 0, 0:256], RBq[0:TS, 4, 256:512]).then_inc(k_out, 16)
                else:
                    for g in (1, 2):
                        store_prompt(0, g, RBq[:, 0:4, 256 * (g - 1):256 * g], k_out)
                    pool.dma_start(new_kv_dram[:, 0, 256:768], RBq[0:TS, 4, :]).then_inc(k_out, 16)
            for q in range(4):
                emptied(pool, ("Us", c, q))
                pool.dma_start(state_out[0, 2 * q:2 * q + 2, c].rearrange("b k v -> k b v"), S0[:, q]
                               ).then_inc(s1_out[q], 16)
            if c < 3:
                for q in range(4):
                    load_state(c + 1, q)
        store(o["p_ret"][0, 0].rearrange("h k v -> k h v"), state[:])
        for i in range(TILES):
            pool.wait_ge(b_free[i], BLK_AV2 + 1)
        for g in range(NG):
            store_prompt(1, g, av[:, 0:4, 256 * g:256 * g + 256], av_out)
        pool.dma_start(new_kv_dram[:, 1, :], avs[0:TS, :]).then_inc(av_out, 16)
        for q in range(4):
            pool.wait_ge(s1_out[q], 16 * RH)
        emptied(pool, ("r", 0, 4))
        pool.wait_ge(out_done, 16)
        step(nc.gpsimd.memset(qpad[:], 0.0))

        def pad_queries(s):
            qb, h = s // 4, s % 4
            par, hp = h % 2, h // 2
            if s >= 2:
                filled(pool, ("s", s - 2, 2))
            for g in range(NG):
                last = nc.gpsimd.tensor_copy(qpad[64 * par:64 * par + 64, par, g, :],
                                             aqT[64 * par:64 * par + 64, 2 * g + hp, 128 * qb:128 * qb + 128])
            last.then_inc(q_padded, 1)

        def load_piece(n):
            b, g, t = n // 6, n // 2 % NG, 2 * (n % 2)
            if n >= 3:
                pool.wait_ge(s_step, n - 2)
            if g == 0:
                pool.dma_start(kvk[:, n % 3, 0, :], kv_dram[0][0, b, :, 0].rearrange("n h d -> n (h d)")
                               ).then_inc(kk_in[n % 3], 16)
            else:
                src = kv_dram[g][0, b].rearrange("(n r) c h d -> n r c (h d)", r=GROUPS[g][1])[:, t:t + 2, 0]
                pool.dma_start(kvk[:, n % 3], src).then_inc(kk_in[n % 3], 16)
            src = qs_dram[4 * b + t:4 * b + t + 2, 256 * g:256 * g + 256].unsqueeze(0).broadcast_to([128, 2, 256])
            pool.dma_start(qbc[n % 3][:], src).then_inc(q_in[n % 3], 16)

        pool.wait_ge(qs_out, 32)
        pool.wait_ge(k_out, 16 * (NG + 2))
        filled(pool, ("t", BLK_AK, 4))
        filled(pool, ("r", 1, 4))
        pad_queries(0)
        for s in range(16):
            if s < 15:
                pad_queries(s + 1)
            for n in range(3 * s, 3 * s + 3):
                load_piece(n)
        filled(pool, ("o", 7))
        pool.wait_ge(o_hi, 8)
        step(nc.gpsimd.memset(qbd[:], 0.0))
        for g in range(NG):
            for hp in range(2):
                for par in range(2):
                    dst = qbd[64 * par:64 * par + 64, g, hp, :].rearrange("p (n h) -> p n h", h=4)[:, :, 2 * hp + par]
                    last = nc.gpsimd.tensor_copy(dst, aqT[64 * par:64 * par + 64, 2 * g + hp, SEQ:NTOK])
        last.then_inc(qbd_ready, 1)
        pool.wait_ge(av_out, 16 * (NG + 1))
        pool.wait_ge(w_used, S_GA)

        def load_values(n):
            b, g = n // NG, n % NG
            if n >= 6:
                pool.wait_ge(v_used, n - 5)
            place = kvv[n % 6 // 3][:, n % 3]
            if g == 0:
                pool.dma_start(place[:, 0, :], kv_dram[0][0, b, :, 1].rearrange("n h d -> n (h d)")
                               ).then_inc(kv_in[n % 6], 16)
            else:
                src = kv_dram[g][0, b].rearrange("(n r) c h d -> n r c (h d)", r=GROUPS[g][1])[:, 0:DT, 1]
                pool.dma_start(place, src).then_inc(kv_in[n % 6], 16)

        for n in range(6):
            load_values(n)
        pool.wait_ge(qbd_ready, 1)
        nc.gpsimd.memset(pad0[:], 0.0).then_inc(pads_ready, 1)
        nc.gpsimd.memset(pad1[:], 0.0).then_inc(pads_ready, 1)
        for n in range(6, 24):
            load_values(n)
        pool.wait_ge(mix_lo, KT)
        for i in range(TILES):
            r = rows(i)
            pool.dma_start(xr[0:r, i, :], a["x_prompt"][0, 128 * i:128 * i + 128, :] if i < 4 else
                           a["x_sample"].rearrange("b t d -> (b t) d")).then_inc(x_again[i], 16)
        pool.dma_start(gpost[:], a["norm_mix_post"].broadcast_to([128, D])).then_inc(g2_in, 16)
        pool.dma_start(gffn[:], a["norm_ffn_pre"].broadcast_to([128, D])).then_inc(g2_in, 16)
        filled(pool, ("h2", 4, 1))
        emptied(pool, ("h2", 4, 1))
        pool.dma_start(cvs[:], a["conv_state"]).then_inc(cvs_in, 16)
        nc.gpsimd.memset(ub[:], 0.0).then_inc(pool_step, 1)
        steps[0] += 1
        pool.wait_ge(pool_step, steps[0])
        pool.wait_ge(cvs_in, 16)
        pool.sem_inc(tail_done, 4)
        with pool.Fori(0, up_loop) as it:
            for q in range(2):
                for j in range(2):
                    tile = it * 2 + (q + FT * j)
                    u_s = ub[:, q, j, 2 + SEQ:].rearrange("p (b t) -> p b t", t=6)
                    pool.wait_ge(conv_done, it * 4 + (2 * q + j + 1))
                    nc.gpsimd.tensor_copy(u_s[:, :, 0:2], cvs[:, bass.ds(tile * 16, 16)].rearrange("p (b t) -> p b t", t=2)
                                          ).then_inc(head_ready, 1)
                    pool.wait_ge(u_evac[j], it * 2 + (q + 2))
                    nc.gpsimd.tensor_copy(cvt[:, bass.ds(tile * 18, 2)], ub[:, q, j, SEQ:SEQ + 2])
                    nc.gpsimd.tensor_copy(cvt[:, bass.ds(tile * 18 + 2, 16)].rearrange("p (b t) -> p b t", t=2),
                                          u_s[:, :, 4:6]).then_inc(tail_done, 1)
        for j in range(2 * FT // 4):
            emptied(pool, ("cv", j))
            pool.dma_start(o["p_conv"][0, 0, :, 512 * j:512 * j + 512], cvrow[0:2, j % 2, :]).then_inc(cv_out[j % 2], 16)
            pool.dma_start(o["s_conv"][0].rearrange("b t n -> (b t) n")[:, 512 * j:512 * j + 512], cvrow[2:18, j % 2, :]
                           ).then_inc(cv_out[j % 2], 16)
        pool.dma_start(gfin[:], a["norm_ffn_post"].broadcast_to([128, D])).then_inc(gfin_in, 16)
        for i in range(TILES):
            pool.wait_ge(y_ready, i + 1)
            r = rows(i)
            dst = o["y_prompt"][0, 128 * i:128 * i + 128, :] if i < 4 else o["y_sample"].rearrange("b t d -> (b t) d")
            pool.dma_start(dst, ytmp[0:r, i % 2, :]).then_inc(y_out[i % 2], 16)
        pool.wait_ge(out_done, 16 * stores[0])
        pool.wait_ge(k_out, 16 * (NG + 2))
        pool.wait_ge(av_out, 16 * (NG + 1))
        for n in range(2):
            pool.wait_ge(y_out[n], 16 * (3 - n))
            pool.wait_ge(cv_out[n], 32 * (6 - n))

    @block.scalar
    def _(act):
        steps = [0]

        def step(ins):
            steps[0] += 1
            ins.then_inc(act_step, 1)
            act.wait_ge(act_step, steps[0])

        def w_split(s):
            act.wait_ge(w_raw[s % 2], 16 * (s // 2 + 1))
            if s >= 2:
                act.wait_ge(w_used, s - 1)
            w = slot_width(s)
            nc.scalar.activation(whi[:, s % 2, 0:w], wraw[:, s % 2, 0:w], ACT.Copy).then_inc(w_hi, 1)

        def split_evac(key, Th, Ts, k0, i):
            b = filled(act, key)
            n = rows(i)
            src = b[:, 0:4 * n].rearrange("p (k n) -> p k n", k=4)
            ins = nc.scalar.activation(Th[:, k0:k0 + 4, cols(i)], src, ACT.Copy)
            if i == 4:
                ins = nc.scalar.activation(Ts[:, k0:k0 + 4, 0:32], src, ACT.Copy)
            ins.then_inc(split_hi, 1)

        def block_end(bi):
            first, n = BLOCKS[bi][:2]
            act.wait_ge(w_used, first + n)

        def sample_lo(bi, tmp, width, scales):
            if bi:
                act.wait_ge(b_free[4], bi)
            at_ = 0
            for w, scale in scales:
                ins = nc.scalar.activation(tmp[0:TS, at_:at_ + w], P[4][32:64, at_:at_ + w], ACT.Copy, scale=scale)
                at_ += w
            ins.then_inc(tmp_ready, 1)

        def evac_block(bi, dst, width, scales, tmp=tmp_s):
            block_end(bi)
            sample_lo(bi, tmp, width, scales)
            for i in range(4):
                at_ = 0
                for w, scale in scales:
                    ins = nc.scalar.activation(dst(i)[:, at_:at_ + w], P[i][:, at_:at_ + w], ACT.Copy, scale=scale)
                    at_ += w
                ins.then_inc(b_free[i], 1)

        def turn_evac(bi):
            for i in range(TILES):
                b = filled(act, ("t", bi, i))
                n = rows(i)
                src = b[:, 0:4 * n].rearrange("p (k n) -> p k n", k=4)
                if bi == BLK_RQ:
                    parts = ((qT, 0, 0, 4),)
                elif bi == BLK_RK:
                    parts = ((kT, 0, 0, 4),)
                elif bi == BLK_AQ:
                    parts = ((aqT, 0, 0, 4),)
                elif bi == BLK_AQK:
                    parts = ((aqT, 4, 0, 2), (akT, 0, 2, 2))
                else:
                    parts = ((akT, 2, 0, 4),)
                for dst, d0, s0, k in parts:
                    ins = nc.scalar.activation(dst[:, d0:d0 + k, cols(i)], src[:, s0:s0 + k, :], ACT.Copy)
                ins.then_inc(bank_free[USES[("t", bi, i)][0]], 1)

        w_split(0)
        w_split(1)
        act.wait_ge(cleared, 2)
        for i in range(TILES):
            r = rows(i)
            act.wait_ge(x_in[i], 16)
            nc.scalar.activation(junk[0:r], xin[0:r, i, :], ACT.Square, accum_out=ss_x[0:r, i:i + 1]).then_inc(x_sq, 1)
            act.wait_ge(x_sq, i + 1)
            nc.scalar.activation(rt_x[0:r, i:i + 1], ss_x[0:r, i:i + 1], ACT.Sqrt, scale=1.0 / D,
                                 bias=eps[0:r, 0:1]).then_inc(x_rt, 1)
        for i in range(TILES):
            for half in range(2):
                split_evac(("x", i, half), T1h, T1s, 4 * half, i)

        dests = {
            BLK_RQ: (lambda i: RBq[:, i, :], ((512, 1.0),)),
            BLK_RK: (lambda i: RBk[:, i, :], ((512, DK ** -0.5),)),
            BLK_RV: (lambda i: vt[:, i, 0:512], ((512, 1.0),)),
            BLK_RV + 1: (lambda i: vt[:, i, 512:1024], ((512, 1.0),)),
            BLK_AQ: (lambda i: RBq[:, i, :], ((512, HD ** -0.5),)),
            BLK_AQK: (lambda i: RBq[:, i, :], ((256, HD ** -0.5), (256, 1.0))),
            BLK_AK: (lambda i: RBq[:, i, :], ((512, 1.0),)),
            BLK_AV: (lambda i: av[:, i, 0:512], ((512, 1.0),)),
            BLK_AV2: (lambda i: av[:, i, 512:768], ((256, 1.0),)),
        }

        def outputs_evac(c):
            filled(act, ("U", c, 1))
            for j in range(2):
                key = ("O", c, j)
                b = filled(act, key)
                nc.scalar.activation(vt[:, c, 512 * j:512 * j + 512], b[:, :], ACT.Copy).then_inc(bank_free[USES[key][0]], 1)
            for h in range(RH):
                if h % 2 == 0:
                    emptied(act, ("O", c, h // 2))
                if 5 * c + h:
                    act.wait_ge(on_sq, 5 * c + h)
                nc.scalar.activation(rjunk[:], vt[:, c, DV * h:DV * h + DV], ACT.Square,
                                     accum_out=ss_r[:, 4 * c + h:4 * c + h + 1]).then_inc(on_sq, 1)

        def sample_outputs_evac(h):
            filled(act, ("Us", h, 3))
            b = filled(act, ("Os", h))
            nc.scalar.activation(vs[0:TS, DV * h:DV * h + DV], b[0:TS, 0:DV], ACT.Copy).then_inc(bank_free[6], 1)
            emptied(act, ("Os", h))
            act.wait_ge(on_sq, 5 * h + 4)
            nc.scalar.activation(rjunk[0:TS], vs[0:TS, DV * h:DV * h + DV], ACT.Square,
                                 accum_out=ss_r[0:TS, 16 + h:17 + h]).then_inc(on_sq, 1)

        for bi in range(BLK_RG):
            first, n = BLOCKS[bi][:2]
            for s in range(n - 1):
                w_split(first + s + 2)
                if s == 1 and bi in (1, 2):
                    turn_evac(bi - 1)
                if s == 1 and bi in (5, 6, 7):
                    turn_evac(bi - 1)
                if s == 2 and 4 <= bi < 8:
                    outputs_evac(bi - 4)
            if bi in (BLK_AQ, BLK_AQK, BLK_AK):
                prev = {BLK_AQ: BLK_RQ, BLK_AQK: BLK_AQ, BLK_AK: BLK_AQK}[bi]
                filled(act, ("t", prev, 4))
            if bi == BLK_AQK:
                act.wait_ge(qs_out, 16)
            if bi == BLK_AK:
                act.wait_ge(qs_out, 32)
                act.wait_ge(k_out, 32)
            if bi == BLK_RV:
                act.wait_ge(cleared, 3)
            dst, scales = dests[bi]
            evac_block(bi, dst, BLOCKS[bi][3], scales)
            w_split(first + n + 1)
            if 4 <= bi < 8:
                sample_outputs_evac(bi - 4)
            if bi == BLK_AV2:
                act.wait_ge(on_sq, 20)
                nc.scalar.activation(rt_r[:], ss_r[:], ACT.Sqrt, scale=1.0 / DV, bias=eps[:, 0:1]).then_inc(rt_ready, 1)
        for g in range(2):
            bi = BLK_RG + g
            first, n = BLOCKS[bi][:2]
            for s in range(n - 1):
                w_split(first + s + 2)
                if g == 1 and s == 2:
                    for i in range(TILES):
                        split_evac(("r", 0, i), rTh, rTs, 0, i)
            block_end(bi)
            act.wait_ge(b_free[4], bi)
            if g:
                act.wait_ge(r_ready, 5)
            nc.scalar.activation(tmp_s[0:TS, :], P[4][32:64, :], ACT.Copy).then_inc(tmp_ready, 1)
            for i in range(4):
                k = 5 * g + i
                if k >= 2:
                    act.wait_ge(r_ready, k - 1 if i >= 2 else 5 * g)
                nc.scalar.activation(etmp[:, i % 2, :], P[i][:, :], ACT.Tanh, scale=0.5).then_inc(e_ready, 1)
            act.wait_ge(b_free[4], bi + 1)
            nc.scalar.activation(tmp_s[0:TS, :], etmp[0:TS, 0, :], ACT.Tanh, scale=0.5).then_inc(e_ready, 1)
            w_split(first + n + 1)

        def turned_probs(s):
            nblk = len(attention_blocks(s // 4))
            for j in range(turns(s)):
                key = ("pt", s, j)
                b = filled(act, key)
                k = min(4, nblk - 4 * j)
                nc.scalar.activation(pT[:, 512 * j:512 * j + 128 * k], b[:, 0:128 * k], ACT.Copy
                                     ).then_inc(bank_free[USES[key][0]], 1)

        def attended_hi(pair):
            qb, hp = pair // 2, pair % 2
            b = filled(act, ("o", pair))
            nc.scalar.activation(aoh[:, hp, 128 * qb:128 * qb + 128], b[:, 0:128], ACT.Copy).then_inc(o_hi, 1)

        for i in range(TILES):
            split_evac(("r", 1, i), rTh, rTs, 4, i)
        act.wait_ge(k_out, 16 * (NG + 2))
        for s in range(17):
            if s < 16:
                w = 128 * len(attention_blocks(s // 4))
                act.wait_ge(maxed, s + 1)
                nc.scalar.activation(sc[:, s % 2, 0:w], sc[:, s % 2, 0:w], ACT.Exp, bias=nm[:, s % 2:s % 2 + 1],
                                     accum_out=den[:, s % 2:s % 2 + 1]).then_inc(exped, 1)
            if s >= 1:
                turned_probs(s - 1)
            if s < 16:
                w_split(S_GB + s + 2)
                if s % 2 == 0:
                    n = s // 2
                    act.wait_ge(w_used, S_GB + s + 1)
                    if n:
                        act.wait_ge(a_free[1], n)
                    nc.scalar.activation(gexp[:, 0:HALF], P[0][:, 0:HALF], ACT.Tanh, scale=0.5)
                    nc.scalar.activation(gexp[:, HALF:NTOK], P[1][:, 0:HALF], ACT.Tanh, scale=0.5).then_inc(a_free[0], 1)
            if s >= 2 and s % 2 == 0:
                attended_hi(s // 2 - 1)
        def sample_exp():
            act.wait_ge(s_max, 1)
            nc.scalar.activation(srow[:], srow[:], ACT.Exp, bias=nm[:, 0:1], accum_out=den[:, 0:1]).then_inc(s_exp, 1)

        def sample_turned():
            act.wait_ge(pads_ready, 2)
            b = filled(act, ("sp",))
            q4 = b[:, 0:128].rearrange("p (q r) -> p q r", q=4)
            nc.scalar.activation(pad0[:].rearrange("p (q r) -> p q r", q=4)[:, :, 0:16], q4[:, :, 0:16], ACT.Copy)
            nc.scalar.activation(pad0[:].rearrange("p (q r) -> p q r", q=4)[:, :, 48:64], q4[:, :, 16:32], ACT.Copy)
            for g in range(2):
                src = b[:, 128 * (g + 1):128 * (g + 2)].rearrange("p (q j h) -> p q j h", q=4, j=8)
                dst = pad1[:, g, :].rearrange("p (q r) -> p q r", q=4)
                for j in range(8):
                    last = nc.scalar.activation(dst[:, :, 36 * j:36 * j + 4], src[:, :, j, :], ACT.Copy)
            last.then_inc(bank_free[6], 1)
            b = filled(act, ("spn",))
            nc.scalar.activation(pnew[0:TS].rearrange("p g n -> p (g n)"), b[0:TS, 0:384], ACT.Copy).then_inc(bank_free[4], 1)

        def sample_attended():
            b = filled(act, ("so",))
            src = b[0:HD, 0:128].rearrange("p (n h) -> p n h", h=4)
            for h in range(AH):
                last = nc.scalar.activation(aosf[64 * (h % 2):64 * (h % 2) + 64, h // 2, :], src[:, :, h], ACT.Copy)
            last.then_inc(bank_free[USES[("so",)][0]], 1)
            emptied(act, ("so",))
            nc.scalar.activation(aoh[:, :, SEQ:NTOK], aosf[:], ACT.Copy).then_inc(os_hi, 1)

        for n in range(KT):
            w_split(S_GA + n + 2)
            act.wait_ge(w_used, S_GA + n + 1)
            p = n % 2
            nc.scalar.activation(sga[:, n, 0:HALF], P[2 * p][:, 0:HALF], ACT.Tanh, scale=0.5)
            nc.scalar.activation(sga[:, n, HALF:NTOK], P[2 * p + 1][:, 0:HALF], ACT.Tanh, scale=0.5).then_inc(a_free[p], 1)
            if n in (0, 1, 6):
                {0: sample_exp, 1: sample_turned, 6: sample_attended}[n]()
        for n in range(KT):
            w_split(S_BA + n + 2)
            act.wait_ge(mix_sum, n + 1)
            nc.scalar.activation(mTh[:, n, :], mtmp[:, n % 2, :], ACT.Copy, scale=0.5)
            nc.scalar.activation(mTs[:, n, 0:32], mtmp[:, n % 2, SEQ:NTOK], ACT.Copy, scale=0.5).then_inc(mix_hi, 1)
        for nb in range(2):
            bi = BLK_OUT + nb
            first, n = BLOCKS[bi][:2]
            for s in range(n - 1):
                w_split(first + s + 2)
            evac_block(bi, lambda i: xo[:, i, 512 * nb:512 * nb + 512], 512, ((512, 1.0),), tmp_s2)
            w_split(first + n + 1)
        for i in range(TILES):
            r = rows(i)
            act.wait_ge(b_free[i], BLK_OUT + 2)
            nc.scalar.activation(njunk[0:r], xo[0:r, i, :], ACT.Square, accum_out=ss_n[0:r, i:i + 1]).then_inc(n_sq, 1)
            act.wait_ge(n_sq, i + 1)
            nc.scalar.activation(rt_n[0:r, i:i + 1], ss_n[0:r, i:i + 1], ACT.Sqrt, scale=1.0 / D,
                                 bias=eps[0:r, 0:1]).then_inc(n_rt, 1)
        for i in range(TILES + 1):
            if i < TILES:
                r = rows(i)
                act.wait_ge(x2_ready, i + 1)
                nc.scalar.activation(njunk[0:r], xo[0:r, i, :], ACT.Square, accum_out=ss_n[0:r, 5 + i:6 + i]).then_inc(n_sq, 1)
                act.wait_ge(n_sq, TILES + i + 1)
                nc.scalar.activation(rt_n[0:r, 5 + i:6 + i], ss_n[0:r, 5 + i:6 + i], ACT.Sqrt, scale=1.0 / D,
                                     bias=eps[0:r, 0:1]).then_inc(n_rt, 1)
            if i:
                for half in range(2):
                    split_evac(("h2", i - 1, half), T1h, T1s, 4 * half, i - 1)
        def columns(at, n, j):
            q, t1 = n % 2, 2 * n + j + 1
            act.wait_ge(w_used, at * 2 + (S_UP + t1))
            act.wait_ge(conv_done, at * 2 + t1)
            act.wait_ge(tail_done, at * 2 + t1)
            nc.scalar.activation(ub[:, q, j, 2:2 + HALF], P[2 * j][:, 0:HALF], ACT.Copy)
            nc.scalar.activation(ub[:, q, j, 2 + HALF:2 + SEQ], P[2 * j + 1][:, 0:SEQ - HALF], ACT.Copy)
            u_s = ub[:, q, j, 2 + SEQ:].rearrange("p (b t) -> p b t", t=6)
            nc.scalar.activation(u_s[:, :, 2:6], P[2 * j + 1][:, SEQ - HALF:HALF].rearrange("p (b t) -> p b t", t=4),
                                 ACT.Copy).then_inc(u_evac[j], 1)

        def up_split(at, n, j):
            act.wait_ge(w_raw[j], at * 16 + 16 * ((S_UP + 2 * n + 2 + j) // 2 + 1))
            nc.scalar.activation(whi[:, j, :], wraw[:, j, :], ACT.Copy).then_inc(w_hi, 1)

        def gelu(at, n):
            act.wait_ge(conv_done, at * 2 + (2 * n + 5))
            nc.scalar.activation(cb[:, 0, 0:CW], cb[:, 0, 0:CW], ACT.Gelu_apprx_tanh).then_inc(gelu_done, 1)

        def product_hi(at, n):
            act.wait_ge(f_done, at + (n + 1))
            samp = c_sample(cb[:, 0, :])
            at_f, at_s = (at + n) * NTOK, (at + n) * 64
            place = (lambda x, w: bass.ds(x, w)) if not isinstance(at, int) else (lambda x, w: slice(x, x + w))
            nc.scalar.activation(fTh[:, place(at_f, SEQ)], cb[:, 0, 0:SEQ], ACT.Copy)
            nc.scalar.activation(fTh[:, place(at_f + SEQ, TS)].rearrange("p (b t) -> p b t", t=4), samp, ACT.Copy)
            nc.scalar.activation(fTs[:, place(at_s, TS)].rearrange("p (b t) -> p b t", t=4), samp, ACT.Copy
                                 ).then_inc(f_hi, 1)

        def pair_round(at, n):
            gelu(at, n)
            columns(at, n + 1, 0)
            product_hi(at, n)
            up_split(at, n + 1, 0)
            columns(at, n + 1, 1)
            up_split(at, n + 1, 1)

        for j in range(2):
            act.sem_inc(u_evac[j], 1)
        for j in range(2):
            columns(0, 0, j)
            up_split(0, 0, j)
        with act.Fori(0, up_loop - 1) as it:
            for q in range(2):
                pair_round(it * 2, q)
        pair_round(0, FT - 2)
        gelu(0, FT - 1)
        product_hi(0, FT - 1)
        for nb in range(2):
            bi = BLK_DN + nb
            first, n = BLOCKS[bi][:2]
            for s in range(n - 1):
                if first + s + 2 < NSLOT:
                    w_split(first + s + 2)
            evac_block(bi, lambda i: fo[:, i, 512 * nb:512 * nb + 512], 512, ((512, 1.0),), tmp_s3)
            if first + n + 1 < NSLOT:
                w_split(first + n + 1)
        for i in range(TILES):
            r = rows(i)
            act.wait_ge(b_free[i], BLK_DN + 2)
            nc.scalar.activation(fjunk[0:r], fo[0:r, i, :], ACT.Square, accum_out=ss_n[0:r, 10 + i:11 + i]).then_inc(y_sq, 1)
            act.wait_ge(y_sq, i + 1)
            nc.scalar.activation(rt_n[0:r, 10 + i:11 + i], ss_n[0:r, 10 + i:11 + i], ACT.Sqrt, scale=1.0 / D,
                                 bias=eps[0:r, 0:1]).then_inc(y_rt, 1)

    @block.tensor
    def _(pe):
        mm = nc.tensor.matmul

        def open_bank(key):
            bank, n = USES[key]
            if n:
                pe.wait_ge(bank_free[bank], n)
            return P[bank], bank_full[bank]

        def turn(key, srcs, n, m=128):
            b, full = open_bank(key)
            for k, src in enumerate(srcs):
                last = nc.tensor.transpose(b[0:m, k * n:(k + 1) * n], src, ident[0:n, 0:n])
            last.then_inc(full, 1)

        def b_block(bi, Th, Tl, Ts, between=None, ready=None):
            first, n, per, w = BLOCKS[bi]
            for s in range(n):
                slot = first + s
                pe.wait_ge(w_lo, slot + 1)
                for kk in range(per):
                    k = s * per + kk
                    Wh = whi[:, slot % 2, kk * w:(kk + 1) * w]
                    Wl = wlo[:, slot % 2, kk * w:(kk + 1) * w]
                    st, sp_ = k == 0, k == n * per - 1
                    for i in range(4):
                        if k == 0:
                            if ready:
                                ready(i)
                            if bi:
                                pe.wait_ge(b_free[i], bi)
                        xh, xl = Th(k, cols(i)), Tl(k, cols(i))
                        mm(P[i][:, 0:w], xh, Wh, start=st, stop=False)
                        mm(P[i][:, 0:w], xh, Wl, start=False, stop=False)
                        mm(P[i][:, 0:w], xl, Wh, start=False, stop=sp_)
                    if k == 0:
                        if ready:
                            ready(4)
                        if bi:
                            pe.wait_ge(b_free[4], bi)
                    mm(P[4][0:64, 0:w], Ts(k), Wh, start=st, stop=False)
                    last = mm(P[4][0:64, 0:w], Ts(k), Wl, start=False, stop=sp_)
                last.then_inc(w_used, 1)
                if between:
                    between(s)

        def a_tile(slot, Th, Tl, kt, banks):
            for k in range(kt):
                Wh, Wl = whi[:, slot % 2, 128 * k:128 * k + 128], wlo[:, slot % 2, 128 * k:128 * k + 128]
                for half in range(2):
                    dst = P[banks + half][:, 0:HALF]
                    c = slice(HALF * half, HALF * half + HALF)
                    mm(dst, Wh, Th[:, k, c], start=k == 0, stop=False)
                    mm(dst, Wh, Tl[:, k, c], start=False, stop=False)
                    last = mm(dst, Wl, Th[:, k, c], start=False, stop=k == kt - 1)
            return last

        pe.wait_ge(ca_in, 16)
        for i in range(TILES):
            pe.wait_ge(x_norm, i + 1)
            for half in range(2):
                turn(("x", i, half), [xn[0:rows(i), i % 2, 128 * (4 * half + k):128 * (4 * half + k) + 128] for k in range(4)], rows(i))

        T1 = (lambda k, c: T1h[:, k, c], lambda k, c: T1l[:, k, c], lambda k: T1s[:, k, :])

        def turn_block(bi):
            src = RBk if bi == BLK_RK else RBq
            for i in range(TILES):
                pe.wait_ge(rope_done, 5 * ROPE_BLOCKS.index(bi) + i + 1)
                turn(("t", bi, i), [src[0:rows(i), i, 128 * k:128 * k + 128] for k in range(4)], rows(i))

        def scores(c):
            emptied(pe, ("t", BLK_RK, 4))
            emptied(pe, ("t", BLK_RK, 3))
            emptied(pe, ("t", BLK_RK, 2))
            b, full = open_bank(("S", c))
            for h in range(RH):
                last = mm(b[:, 128 * h:128 * h + 128], kT[:, h, cols(c)], qT[:, h, cols(c)], start=True, stop=True)
            last.then_inc(full, 1)
            if c == 0:
                b, full = open_bank(("Ss",))
                for h in range(RH):
                    last = mm(b[0:TS, 32 * h:32 * h + 32], kT[:, h, SEQ:NTOK], qT[:, h, SEQ:NTOK], start=True, stop=True)
                last.then_inc(full, 1)

        def outputs(c):
            emptied(pe, ("S", c))
            if c:
                pe.wait_ge(qd_ready, c)
                emptied(pe, ("U", c - 1, 1))
            for j in range(2):
                b, full = open_bank(("O", c, j))
                for e in range(2):
                    h = 2 * j + e
                    dst = b[:, DV * e:DV * e + DV]
                    last = mm(dst, PT[:, h, :], vt[:, c, DV * h:DV * h + DV], start=True, stop=c == 0)
                    if c:
                        last = mm(dst, qd[:, h, :], state[:, h, :], start=False, stop=True)
                last.then_inc(full, 1)

        def updates(c, j):
            pe.wait_ge(kd_ready, c + 1)
            b, full = open_bank(("U", c, j))
            for e in range(2):
                h = 2 * j + e
                last = mm(b[:, DV * e:DV * e + DV], kd[:, 128 * h:128 * h + 128], vt[:, c, DV * h:DV * h + DV],
                          start=True, stop=True)
            last.then_inc(full, 1)

        def retention_part(c, s):
            if s == 0:
                scores(c)
            elif s == 1:
                if c:
                    turn_block(BLK_AQ + c - 1)
                outputs(c)
                updates(c, 0)
            elif s == 2:
                updates(c, 1)
            else:
                sample_head(c)

        def sample_head(h):
            emptied(pe, ("Ss",))
            ob, ofull = open_bank(("Os", h))
            mm(ob[0:TS, 0:DV], PTs[0:TS, h, :], vs[0:TS, DV * h:DV * h + DV], start=True, stop=False)
            pe.wait_ge(qm_ready, h + 1)
            pe.wait_ge(km_ready, h + 1)
            for p in range(4):
                pe.wait_ge(s0_in[p], 16 * (h + 1))
                for e in range(2):
                    last = mm(ob[0:TS, 0:DV], qm[:, h % 2, 2 * p + e, :], S0[:, p, e, :], start=False,
                              stop=p == 3 and e == 1)
                if p == 3:
                    last.then_inc(ofull, 1)
                b, full = open_bank(("Us", h, p))
                for e in range(2):
                    last = mm(b[:, DV * e:DV * e + DV], km[:, 2 * p + e, :], vs[:, DV * h:DV * h + DV], start=True, stop=True)
                last.then_inc(full, 1)

        def x_ready(i):
            for half in range(2):
                emptied(pe, ("x", i, half))

        for bi in range(BLK_RG):
            def between(s, bi=bi):
                if bi in (1, 2) and s == 1:
                    turn_block(bi - 1)
                if 4 <= bi < 8:
                    retention_part(bi - 4, s)
            b_block(bi, *T1, between=between, ready=x_ready if bi == 0 else None)

        def turn_gated(g):
            for i in range(TILES):
                pe.wait_ge(r_ready, 5 * g + i + 1)
                r = rows(i)
                src = vt[:, i, :] if i < 4 else vs[0:TS, :]
                turn(("r", g, i), [src[:, 128 * (4 * g + k):128 * (4 * g + k) + 128] for k in range(4)], r)

        b_block(BLK_RG, *T1)
        b_block(BLK_RG + 1, *T1, between=lambda s: turn_gated(0) if s == 2 else None)

        def att_scores(s):
            qb, h = s // 4, s % 4
            pe.wait_ge(q_padded, s + 1)
            for g in range(NG):
                gg = (1, 2, 0)[g]
                b, full = open_bank(("s", s, g))
                lo, hi = (0 if gg else 128 * max(qb - 1, 0)), 128 * (qb + 1)
                mm(b[:, 0:hi - lo], qpad[:, h % 2, gg, :], akT[:, 2 * gg + h // 2, lo:hi], start=True, stop=True
                   ).then_inc(full, 1)

        def att_turn(s):
            nblk = len(attention_blocks(s // 4))
            pe.wait_ge(probs, s + 1)
            for j in range(turns(s)):
                ks = range(4 * j, min(4 * j + 4, nblk))
                turn(("pt", s, j), [sc[:, s % 2, 128 * k:128 * k + 128] for k in ks], 128)

        def att_values(s):
            qb, h = s // 4, s % 4
            par = h % 2
            key = ("o", s // 2)
            if par == 0:
                b, full = open_bank(key)
            else:
                b, full = P[7], bank_full[7]
            blocks = attention_blocks(qb)
            for n, (g, kb) in enumerate(blocks):
                if n % 4 == 0:
                    emptied(pe, ("pt", s, n // 4))
                last = mm(b[64 * par:64 * par + 64, 0:128], av[:, kb, 256 * g + 64 * h:256 * g + 64 * h + 64],
                          pT[:, 128 * n:128 * n + 128], start=n == 0, stop=n == len(blocks) - 1)
            if par:
                last.then_inc(full, 1)

        for i in range(TILES):
            pe.wait_ge(b_free[i], BLK_AV2 + 1)
        for i in range(4, -1, -1):
            emptied(pe, ("t", BLK_AK, i))
        pe.wait_ge(b_free[4], BLK_RG + 2)
        turn_gated(1)
        att_scores(0)
        for s in range(17):
            if s < 16:
                slot, n = S_GB + s, s // 2
                if s < 2:
                    pe.wait_ge(b_free[2 * s], BLK_RG + 2)
                    pe.wait_ge(b_free[2 * s + 1], BLK_RG + 2)
                if s == 1:
                    for i in (2, 3, 4):
                        emptied(pe, ("r", 1, i))
                pe.wait_ge(w_lo, slot + 1)
                if n:
                    pe.wait_ge(a_free[s % 2], n)
                if s % 2 == 0:
                    a_tile(slot, T1h, T1l, KT, 0).then_inc(w_used, 1)
                else:
                    a_tile(slot, rTh, rTl, KT, 2).then_inc(w_used, 1)
            if s >= 1:
                att_turn(s - 1)
                att_values(s - 1)
            if s < 15:
                att_scores(s + 1)
        def sample_scores():
            pe.wait_ge(s_step, 48)
            turn(("st",), [sTk[:, g, :] for g in range(NG)], 128)
            pe.wait_ge(qbd_ready, 1)
            b, full = open_bank(("sn",))
            for g in range(NG):
                for hp in range(2):
                    last = mm(b[:, 32 * g:32 * g + 32], qbd[:, g, hp, :], akT[:, 2 * g + hp, SEQ:NTOK], start=hp == 0, stop=hp == 1)
            last.then_inc(full, 1)

        def sample_turn():
            pe.wait_ge(s_probs, 1)
            turn(("sp",), [srow[:, g, 0:128] for g in range(NG)], 128)
            turn(("spn",), [srow[:, g, 128:160] for g in range(NG)], 128, 32)

        def sample_values(batches):
            if 0 in batches:
                emptied(pe, ("sp",))
                emptied(pe, ("spn",))
                open_bank(("sv",))
            b, full = P[7], bank_full[7]
            for bb in batches:
                q = bb // 2
                dst = b[32 * q:32 * q + 32, 0:256]
                for g in range(NG):
                    n = NG * bb + g
                    pe.wait_ge(kv_in[n % 6], 16 * (n // 6 + 1))
                    place = kvv[n % 6 // 3][:, n % 3]
                    if g == 0:
                        last = mm(dst, pad0[:, 32 * bb:32 * bb + 32], place[:, 0, :], start=bb % 2 == 0, stop=False)
                    else:
                        for t in range(DT):
                            last = mm(dst, pad1[:, g - 1, 32 * (4 * bb + t):32 * (4 * bb + t) + 32], place[:, t, :],
                                      start=False, stop=False)
                    last.then_inc(v_used, 1)
                if bb % 2 == 1:
                    for g in range(NG):
                        last = mm(dst, pnew[0:TS, g, 32 * q:32 * q + 32], avs[0:TS, 256 * g:256 * g + 256], start=False,
                                  stop=g == 2)
                if bb == NB - 1:
                    last.then_inc(full, 1)

        for n in range(KT):
            pe.wait_ge(w_lo, S_GA + n + 1)
            pe.wait_ge(a_free[n % 2], 8 + n // 2)
            a_tile(S_GA + n, T1h, T1l, KT, 2 * (n % 2)).then_inc(w_used, 1)
            if n == 0:
                sample_scores()
            elif n == 1:
                sample_turn()
            elif n < 6:
                sample_values(((0,), (1, 2), (3, 4, 5), (6, 7))[n - 2])
            elif n == 6:
                pe.wait_ge(o_row, 1)
                turn(("so",), [orow[:, :]], 128, HD)
        pe.wait_ge(os_lo, 1)
        for n in range(KT):
            pe.wait_ge(w_lo, S_BA + n + 1)
            pe.wait_ge(a_free[n % 2], 12 + n // 2)
            a_tile(S_BA + n, aoh, aol, 2, 2 * (n % 2)).then_inc(w_used, 1)
        pe.wait_ge(mix_lo, KT)
        pe.wait_ge(a_free[0], 16)
        pe.wait_ge(a_free[1], 16)
        for nb in range(2):
            b_block(BLK_OUT + nb, lambda k, c: mTh[:, k, c], lambda k, c: mTl[:, k, c], lambda k: mTs[:, k, :])
        for i in range(TILES):
            pe.wait_ge(h_ready, i + 1)
            for half in range(2):
                turn(("h2", i, half), [hn[0:rows(i), i % 2, 128 * (4 * half + k):128 * (4 * half + k) + 128] for k in range(4)], rows(i))
        for i in range(TILES):
            pe.wait_ge(b_free[i], BLK_OUT + 2)
            for half in range(2):
                emptied(pe, ("h2", i, half))
        with pe.Fori(0, up_loop) as it:
            for q in range(2):
                for j in range(2):
                    pe.wait_ge(w_lo, it * 4 + (S_UP + 2 * q + j + 1))
                    pe.wait_ge(u_evac[j], it * 2 + (q + 1))
                    a_tile(j, T1h, T1l, KT, 2 * j).then_inc(w_used, 1)
        pe.wait_ge(f_lo, FT + 1)
        pe.wait_ge(u_evac[0], FT + 1)
        pe.wait_ge(u_evac[1], FT + 1)
        pe.wait_ge(tail_done, 2 * FT + 4)
        tile = lambda t: t[:].rearrange("p (k n) -> p k n", k=FT)
        fh, fl, fs = tile(fTh), tile(fTl), tile(fTs)

        def conv_tail(s):
            if s < 11:
                turn18(s)

        def turn18(j):
            b, full = open_bank(("cv", j))
            for k in range(4):
                last = nc.tensor.transpose(b[0:18, 128 * k:128 * k + 128], cvt[:, 18 * (4 * j + k):18 * (4 * j + k) + 18], ident)
            last.then_inc(full, 1)

        b_block(BLK_DN, lambda k, c: fh[:, k, c], lambda k, c: fl[:, k, c], lambda k: fs[:, k, :], between=conv_tail)
        b_block(BLK_DN + 1, lambda k, c: fh[:, k, c], lambda k, c: fl[:, k, c], lambda k: fs[:, k, :])

    @block.vector
    def _(dve):
        v = nc.vector
        steps = [0]

        def step(ins):
            steps[0] += 1
            ins.then_inc(dve_step, 1)
            dve.wait_ge(dve_step, steps[0])

        def w_split(s):
            dve.wait_ge(w_hi, s + 1)
            w = slot_width(s)
            v.tensor_tensor(wlo[:, s % 2, 0:w], wraw[:, s % 2, 0:w], whi[:, s % 2, 0:w].bitcast(F), ALU.subtract
                            ).then_inc(w_lo, 1)

        def split_evac(key, Th, Tl, Ts, k0, i):
            b = filled(dve, key)
            n = rows(i)
            dve.wait_ge(split_hi, SPLIT_NO[key] + 1)
            src = b[:, 0:4 * n].rearrange("p (k n) -> p k n", k=4)
            hi = Th[:, k0:k0 + 4, cols(i)].bitcast(F)
            ins = v.tensor_tensor(Tl[:, k0:k0 + 4, cols(i)], src, hi, ALU.subtract)
            if i == 4:
                ins = v.tensor_tensor(Ts[:, k0:k0 + 4, 32:64], src, hi, ALU.subtract)
            ins.then_inc(bank_free[USES[key][0]], 1)

        def norm_scale(out, x, root, rs, gain):
            step(v.reciprocal(rs, root))
            return v.scalar_tensor_tensor(out, x, rs, gain, ALU.mult, ALU.mult)

        def sample_sum(bi, dst, scales, tmp=tmp_s):
            first, n = BLOCKS[bi][:2]
            dve.wait_ge(w_used, first + n)
            dve.wait_ge(tmp_ready, bi + 1)
            at_ = 0
            for w, scale in scales:
                ins = v.scalar_tensor_tensor(dst[:, at_:at_ + w], P[4][0:TS, at_:at_ + w], scale, tmp[0:TS, at_:at_ + w],
                                             ALU.mult, ALU.add)
                at_ += w
            ins.then_inc(b_free[4], 1)

        rope_tiles = [0]

        def rope(bi):
            buf = RBk if bi == BLK_RK else RBq
            for i in range(TILES):
                r = rows(i)
                dve.wait_ge(b_free[i], bi + 1)
                if rope_tiles[0]:
                    dve.wait_ge(rope_done, rope_tiles[0])
                rope_tiles[0] += 1
                if bi in (BLK_RQ, BLK_RK):
                    x = buf[0:r, i, :].rearrange("p (h s d) -> p h s d", h=RH, s=2)
                    tc = ropet[0:r, 0, :].rearrange("p (h s d) -> p h s d", h=RH, s=2)
                    tn = ropet[0:r, 1, :].rearrange("p (h s d) -> p h s d", h=RH, s=2)
                    cos = crv("rcos", TILES)[0:r, i, :].unsqueeze(1).broadcast_to([r, 8, 64])
                    sin = crv("rsin", TILES)[0:r, i, :].rearrange("p (s d) -> p s d", s=2)
                    v.tensor_tensor(ropet[0:r, 0, :].rearrange("p (k d) -> p k d", k=8),
                                    buf[0:r, i, :].rearrange("p (k d) -> p k d", k=8), cos, ALU.mult)
                    for side in range(2):
                        last = v.tensor_tensor(tn[:, :, side, :], x[:, :, 1 - side, :],
                                               sin[:, side, :].unsqueeze(1).broadcast_to([r, RH, 64]), ALU.mult)
                    step(last)
                    v.tensor_tensor(buf[0:r, i, :], ropet[0:r, 0, :], ropet[0:r, 1, :], ALU.add).then_inc(rope_done, 1)
                else:
                    x = buf[0:r, i, :].rearrange("p (h d) -> p h d", h=8)[:, :, 0:16]
                    tc = ropet[0:r, 0, 0:128].rearrange("p (h d) -> p h d", h=8)
                    tn = ropet[0:r, 1, 0:128].rearrange("p (h d) -> p h d", h=8)
                    cos = cav("acos", TILES)[0:r, i, :].unsqueeze(1).broadcast_to([r, 8, 16])
                    sin = cav("asin", TILES)[0:r, i, :]
                    v.tensor_tensor(tc, x, cos, ALU.mult)
                    for side in range(2):
                        last = v.tensor_tensor(tn[:, :, 8 * side:8 * side + 8], x[:, :, 8 - 8 * side:16 - 8 * side],
                                               sin[:, 8 * side:8 * side + 8].unsqueeze(1).broadcast_to([r, 8, 8]), ALU.mult)
                    step(last)
                    v.tensor_tensor(x, tc, tn, ALU.add).then_inc(rope_done, 1)

        w_split(0)
        w_split(1)
        dve.wait_ge(gpre_in, 16)
        for i in range(TILES):
            r = rows(i)
            dve.wait_ge(x_rt, i + 1)
            if i >= 2:
                filled(dve, ("x", i - 2, 1))
            norm_scale(xn[0:r, i % 2, :], xin[0:r, i, :], rt_x[0:r, i:i + 1], rs_x[0:r, i:i + 1], gpre[0:r]).then_inc(x_norm, 1)
            if i >= 1:
                for half in range(2):
                    split_evac(("x", i - 1, half), T1h, T1l, T1s, 4 * half, i - 1)
        for half in range(2):
            split_evac(("x", 4, half), T1h, T1l, T1s, 4 * half, 4)
        dve.wait_ge(cr_in, 16)
        dve.wait_ge(cleared, 4)

        sample_dst = {
            BLK_RQ: (RBq[0:TS, 4, :], ((512, 1.0),)), BLK_RK: (RBk[0:TS, 4, :], ((512, DK ** -0.5),)),
            BLK_RV: (vs[0:TS, 0:512], ((512, 1.0),)), BLK_RV + 1: (vs[0:TS, 512:1024], ((512, 1.0),)),
            BLK_AQ: (RBq[0:TS, 4, :], ((512, HD ** -0.5),)), BLK_AQK: (RBq[0:TS, 4, :], ((256, HD ** -0.5), (256, 1.0))),
            BLK_AK: (RBq[0:TS, 4, :], ((512, 1.0),)), BLK_AV: (avs[0:TS, 0:512], ((512, 1.0),)),
            BLK_AV2: (avs[0:TS, 512:768], ((256, 1.0),)),
        }

        def decayed(c):
            key = ("S", c)
            b = filled(dve, key)
            if c:
                filled(dve, ("O", c - 1, 1))
                v.tensor_tensor(qd[:], qT[:, :, cols(c)], crv("qdec", RH), ALU.mult).then_inc(qd_ready, 1)
            v.tensor_tensor(PT[:], b[:, :].rearrange("p (h n) -> p h n", h=RH), crv("decT", RH), ALU.mult
                            ).then_inc(bank_free[USES[key][0]], 1)
            if c == 0:
                b = filled(dve, ("Ss",))
                v.tensor_tensor(PTs[0:TS], b[0:TS, 0:128].rearrange("p (h n) -> p h n", h=RH), crv("decTs", RH)[0:TS], ALU.mult
                                ).then_inc(bank_free[USES[("Ss",)][0]], 1)
                sample_queries(0)
                sample_queries(1)

        def state_update(c, j):
            key = ("U", c, j)
            b = filled(dve, key)
            for e in range(2):
                h = 2 * j + e
                src = b[:, DV * e:DV * e + DV]
                if c == 0:
                    ins = v.tensor_copy(state[:, h, :], src)
                else:
                    ins = v.scalar_tensor_tensor(state[:, h, :], state[:, h, :], GAMMA_CHUNK[h], src, ALU.mult, ALU.add)
            ins.then_inc(bank_free[USES[key][0]], 1)

        def sample_queries(h):
            if h >= 2:
                filled(dve, ("Os", h - 2))
            dst = bass.AP(qm, (h % 2) * 256, [[512, 128], [36, NB], [1, DT]])
            v.tensor_tensor(dst, qT[:, h, SEQ:NTOK].rearrange("p (b t) -> p b t", t=DT),
                            crv("qdecs", RH)[:, h, :].rearrange("p (b t) -> p b t", t=DT), ALU.mult).then_inc(qm_ready, 1)

        def new_sample_states(h):
            for p in range(4):
                key = ("Us", h, p)
                b = filled(dve, key)
                v.scalar_tensor_tensor(S0[:, p], S0[:, p], GAMMA_STEP[h], b[:, :].rearrange("p (e n) -> p e n", e=2),
                                       ALU.mult, ALU.add).then_inc(bank_free[USES[key][0]], 1)
            if h + 2 < RH:
                sample_queries(h + 2)

        for bi in range(BLK_RG):
            first, n = BLOCKS[bi][:2]
            for s in range(n - 1):
                w_split(first + s + 2)
                if 4 <= bi < 8:
                    if s == 0:
                        decayed(bi - 4)
                    else:
                        state_update(bi - 4, s - 1)
            dst, scales = sample_dst[bi]
            if bi == BLK_AQ:
                filled(dve, ("t", BLK_RQ, 4))
            if bi == BLK_AQK:
                filled(dve, ("t", BLK_AQ, 4))
                dve.wait_ge(qs_out, 16)
            if bi == BLK_AK:
                filled(dve, ("t", BLK_AQK, 4))
                dve.wait_ge(qs_out, 32)
                dve.wait_ge(k_out, 32)
            sample_sum(bi, dst, scales)
            w_split(first + n + 1)
            if 4 <= bi < 8:
                new_sample_states(bi - 4)
            if bi in ROPE_BLOCKS:
                rope(bi)
            if bi == BLK_AV2:
                dve.wait_ge(rt_ready, 1)
                step(v.reciprocal(rs_r[:], rt_r[:]))
                step(v.tensor_scalar(rs_r[:], rs_r[:], 0.5, None, ALU.mult))

        def gate_tile(g, i):
            k = 5 * g + i
            dve.wait_ge(e_ready, k + 1)
            if i < 4:
                t, e, x, out, r = etmp[:, i % 2, :], etmp[:, i % 2, :], P[i][:, :], vt[:, i, :], 128
                v.scalar_tensor_tensor(t, e, 1.0, x, ALU.add, ALU.mult).then_inc(b_free[i], 1)
                dve.wait_ge(b_free[i], BLK_RG + g + 1)
            else:
                t, e, x, out, r = etmp[0:TS, 0, :], tmp_s[0:TS, :], etmp[0:TS, 0, :], vs[0:TS, :], TS
                step(v.scalar_tensor_tensor(t, e, 1.0, x, ALU.add, ALU.mult))
            for hh in range(2):
                h = 2 * g + hh
                o_ = out[:, DV * h:DV * h + DV]
                last = v.scalar_tensor_tensor(o_, o_, rs_r[0:r, 4 * i + h:4 * i + h + 1], t[:, DV * hh:DV * hh + DV],
                                              ALU.mult, ALU.mult)
            last.then_inc(r_ready, 1)

        for g in range(2):
            bi = BLK_RG + g
            first, n = BLOCKS[bi][:2]
            for s in range(n - 1):
                w_split(first + s + 2)
                if g == 1 and s == 2:
                    for i in range(TILES):
                        split_evac(("r", 0, i), rTh, rTl, rTs, 0, i)
            dve.wait_ge(tmp_ready, bi + 1)
            for i in range(4):
                gate_tile(g, i)
            v.tensor_tensor(etmp[0:TS, 0, :], P[4][0:TS, :], tmp_s[0:TS, :], ALU.add).then_inc(b_free[4], 1)
            dve.wait_ge(b_free[4], bi + 1)
            gate_tile(g, 4)
            w_split(first + n + 1)

        masks = {1: cav("mask1"), 2: cav("mask2"), 0: cav("mask0")}

        def score_max(s):
            qb = s // 4
            at_ = 0
            for g in range(NG):
                gg = (1, 2, 0)[g]
                key = ("s", s, g)
                b = filled(dve, key)
                w = 128 * (qb + 1) if gg else 128 * min(qb + 1, 2)
                m = masks[gg]
                full_w = 512 if gg else 256
                last = v.tensor_tensor_reduce(out=sc[:, s % 2, at_:at_ + w], in0=b[:, 0:w], in1=m[:, full_w - w:full_w],
                                              scale=1.0, scalar=NEG, op0=ALU.add, op1=ALU.max,
                                              accum_out=mx[:, s % 2, g:g + 1])
                last.then_inc(bank_free[USES[key][0]], 1)
                at_ += w
            emptied(dve, ("s", s, 0))
            emptied(dve, ("s", s, 1))
            emptied(dve, ("s", s, 2))
            step(v.tensor_reduce(rden[:, s % 2:s % 2 + 1], mx[:, s % 2, 0:3], AX.X, ALU.max))
            v.tensor_scalar(nm[:, s % 2:s % 2 + 1], rden[:, s % 2:s % 2 + 1], -1.0, None, ALU.mult).then_inc(maxed, 1)

        def normalise(s):
            w = 128 * len(attention_blocks(s // 4))
            dve.wait_ge(exped, s + 1)
            step(v.reciprocal(rden[:, s % 2:s % 2 + 1], den[:, s % 2:s % 2 + 1]))
            v.tensor_scalar(sc[:, s % 2, 0:w], sc[:, s % 2, 0:w], rden[:, s % 2:s % 2 + 1], None, ALU.mult
                            ).then_inc(probs, 1)

        def gated(n, gate, src, out, frees):
            for half in range(2):
                c = slice(HALF * half, HALF * half + HALF)
                last = v.scalar_tensor_tensor(out[:, c], gate[:, c], 1.0, P[src + half][:, 0:HALF], ALU.add, ALU.mult)
            last.then_inc(frees, 1)

        def attended_lo(pair):
            qb, hp = pair // 2, pair % 2
            b = filled(dve, ("o", pair))
            dve.wait_ge(o_hi, pair + 1)
            c = slice(128 * qb, 128 * qb + 128)
            v.tensor_tensor(aol[:, hp, c], b[:, 0:128], aoh[:, hp, c].bitcast(F), ALU.subtract).then_inc(bank_free[7], 1)

        def sample_piece(n):
            b, g, t = n // 6, n // 2 % NG, 2 * (n % 2)
            dve.wait_ge(kk_in[n % 3], 16 * (n // 3 + 1))
            dve.wait_ge(q_in[n % 3], 16 * (n // 3 + 1))
            if n:
                dve.wait_ge(s_step, n)
            keys = kvk[:, n % 3, 0, :].unsqueeze(1).broadcast_to([128, 2, 256]) if g == 0 else kvk[:, n % 3]
            step(v.tensor_tensor(prod[:].rearrange("p (t n) -> p t n", t=2), keys, qbc[n % 3][:], ALU.mult))
            v.tensor_reduce(sTk[:, g, 16 * b + 4 * t:16 * b + 4 * t + 8], prod[:].rearrange("p (k d) -> p k d", d=HD), AX.X,
                            ALU.add).then_inc(s_step, 1)

        for s in range(17):
            if s < 16:
                if s >= 2:
                    filled(dve, ("pt", s - 2, turns(s - 2) - 1))
                if s == 0:
                    for i in range(TILES):
                        split_evac(("r", 1, i), rTh, rTl, rTs, 4, i)
                score_max(s)
                normalise(s)
                w_split(S_GB + s + 2)
                sample_piece(3 * s)
                if s % 2:
                    n = s // 2
                    dve.wait_ge(w_used, S_GB + s + 1)
                    dve.wait_ge(a_free[0], n + 1)
                    gated(n, gexp[:], 2, mixr[:, n, :], a_free[1])
                sample_piece(3 * s + 1)
            if s >= 2 and s % 2 == 0:
                attended_lo(s // 2 - 1)
            if s < 16:
                sample_piece(3 * s + 2)

        def sample_softmax():
            b = filled(dve, ("st",))
            v.tensor_tensor(srow[:, 0, 0:128], b[:, 0:128], cav("ms0"), ALU.add)
            v.tensor_copy(srow[:, 1:3, 0:128], b[:, 128:384].rearrange("p (g n) -> p g n", g=2)).then_inc(bank_free[4], 1)
            b = filled(dve, ("sn",))
            v.tensor_tensor(srow[:, :, 128:160], b[:, 0:96].rearrange("p (g n) -> p g n", g=NG), cav("mnew", NG), ALU.add
                            ).then_inc(bank_free[5], 1)
            emptied(dve, ("sn",))
            step(v.tensor_reduce(rden[:, 0:1], srow[:], AX.XY, ALU.max))
            v.tensor_scalar(nm[:, 0:1], rden[:, 0:1], -1.0, None, ALU.mult).then_inc(s_max, 1)
            dve.wait_ge(s_exp, 1)
            step(v.reciprocal(rden[:, 1:2], den[:, 0:1]))
            v.tensor_scalar(srow[:], srow[:], rden[:, 1:2], None, ALU.mult).then_inc(s_probs, 1)

        def sample_own_head():
            b = filled(dve, ("sv",))
            v.tensor_tensor(osel[:], b[:, 0:256].rearrange("p (h d) -> p h d", h=AH),
                            cav("hsel").unsqueeze(2).broadcast_to([128, AH, HD]), ALU.mult).then_inc(bank_free[7], 1)
            emptied(dve, ("sv",))
            v.tensor_reduce(orow[:], osel[:].rearrange("p h d -> p d h"), AX.X, ALU.add).then_inc(o_row, 1)

        def sample_attended_lo():
            dve.wait_ge(os_hi, 1)
            v.tensor_tensor(aol[:, :, SEQ:NTOK], aosf[:], aoh[:, :, SEQ:NTOK].bitcast(F), ALU.subtract).then_inc(os_lo, 1)

        for n in range(KT):
            w_split(S_GA + n + 2)
            if n in (0, 5, 6):
                {0: sample_softmax, 5: sample_own_head, 6: sample_attended_lo}[n]()

        for n in range(KT):
            w_split(S_BA + n + 2)
            dve.wait_ge(w_used, S_BA + n + 1)
            p = n % 2
            if n >= 2:
                dve.wait_ge(mix_lo, n - 1)
            gated(n, sga[:, n, :], 2 * p, mtmp[:, p, :], a_free[p])
            dve.wait_ge(a_free[p], 13 + n // 2)
            v.tensor_tensor(mtmp[:, p, :], mtmp[:, p, :], mixr[:, n, :], ALU.add).then_inc(mix_sum, 1)
            dve.wait_ge(mix_hi, n + 1)
            v.scalar_tensor_tensor(mTl[:, n, :], mtmp[:, p, :], 0.5, mTh[:, n, :].bitcast(F), ALU.mult, ALU.subtract)
            v.scalar_tensor_tensor(mTs[:, n, 32:64], mtmp[:, p, SEQ:NTOK], 0.5, mTh[:, n, SEQ:NTOK].bitcast(F), ALU.mult, ALU.subtract
                            ).then_inc(mix_lo, 1)
        for nb in range(2):
            bi = BLK_OUT + nb
            first, n = BLOCKS[bi][:2]
            for s in range(n - 1):
                w_split(first + s + 2)
            sample_sum(bi, xo[0:TS, 4, 512 * nb:512 * nb + 512], ((512, 1.0),), tmp_s2)
            w_split(first + n + 1)
        dve.wait_ge(g2_in, 32)
        for i in range(TILES + 1):
            if i < TILES:
                r = rows(i)
                dve.wait_ge(x_again[i], 16)
                dve.wait_ge(n_rt, i + 1)
                step(norm_scale(tmpn[0:r, i % 2, :], xo[0:r, i, :], rt_n[0:r, i:i + 1], rs_n[0:r, i:i + 1], gpost[0:r]))
                v.tensor_tensor(xo[0:r, i, :], tmpn[0:r, i % 2, :], xr[0:r, i, :], ALU.add).then_inc(x2_ready, 1)
            if i:
                k = i - 1
                r = rows(k)
                dve.wait_ge(n_rt, TILES + k + 1)
                if k >= 2:
                    filled(dve, ("h2", k - 2, 1))
                norm_scale(hn[0:r, k % 2, :], xo[0:r, k, :], rt_n[0:r, 5 + k:6 + k], rs_n[0:r, 5 + k:6 + k], gffn[0:r]
                           ).then_inc(h_ready, 1)
            if i >= 2:
                for half in range(2):
                    split_evac(("h2", i - 2, half), T1h, T1l, T1s, 4 * half, i - 2)
        for half in range(2):
            split_evac(("h2", 4, half), T1h, T1l, T1s, 4 * half, 4)
        dve.wait_ge(convp_in, 16)
        dve.sem_inc(conv_done, 4)
        dve.sem_inc(f_lo, 1)
        with dve.Fori(0, up_loop) as it:
            for q in range(2):
                for j in range(2):
                    t1 = 2 * q + j + 1
                    dve.wait_ge(w_hi, it * 4 + (S_UP + t1 + 2))
                    v.tensor_tensor(wlo[:, j, :], wraw[:, j, :], whi[:, j, :].bitcast(F), ALU.subtract).then_inc(w_lo, 1)
                    tile = it * 2 + (q + FT * j)
                    cp = convp[:].rearrange("p n c -> p (n c)")
                    tap = lambda k: cp[:, bass.ds(tile * 4 + k, 1)]
                    dve.wait_ge(u_evac[j], it * 2 + (q + 2))
                    dve.wait_ge(head_ready, it * 4 + t1)
                    if j == 0:
                        dve.wait_ge(f_lo, it * 2 + (q + 1))
                    v.tensor_scalar(cb[:, j, 0:CW], ub[:, q, j, 2:UW], tap(2), tap(3), ALU.mult, ALU.add).then_inc(conv_tap, 1)
                    dve.wait_ge(conv_tap, it * 8 + (2 * t1 - 1))
                    v.scalar_tensor_tensor(cb[:, j, 0:CW], ub[:, q, j, 1:UW - 1], tap(1), cb[:, j, 0:CW], ALU.mult, ALU.add
                                           ).then_inc(conv_tap, 1)
                    dve.wait_ge(conv_tap, it * 8 + 2 * t1)
                    v.scalar_tensor_tensor(cb[:, j, 0:CW], ub[:, q, j, 0:UW - 2], tap(0), cb[:, j, 0:CW], ALU.mult, ALU.add
                                           ).then_inc(conv_done, 1)
                pair = it * 2 + q
                dve.wait_ge(gelu_done, it * 2 + (q + 1))
                dve.wait_ge(conv_done, it * 4 + (2 * q + 6))
                v.tensor_tensor(cb[:, 0, 0:CW], cb[:, 0, 0:CW], cb[:, 1, 0:CW], ALU.mult).then_inc(f_done, 1)
                dve.wait_ge(f_hi, it * 2 + (q + 1))
                four = lambda t: t.rearrange("p (b t) -> p b t", t=4)
                hi_s = four(fTh[:, bass.ds(pair * NTOK + SEQ, TS)].bitcast(F))
                v.tensor_tensor(fTl[:, bass.ds(pair * NTOK, SEQ)], cb[:, 0, 0:SEQ], fTh[:, bass.ds(pair * NTOK, SEQ)].bitcast(F),
                                ALU.subtract)
                v.tensor_tensor(four(fTl[:, bass.ds(pair * NTOK + SEQ, TS)]), c_sample(cb[:, 0, :]), hi_s, ALU.subtract)
                v.tensor_tensor(four(fTs[:, bass.ds(pair * 64 + 32, TS)]), c_sample(cb[:, 0, :]), hi_s, ALU.subtract
                                ).then_inc(f_lo, 1)
        def conv_rows(j):
            key = ("cv", j)
            b = filled(dve, key)
            if j >= 2:
                dve.wait_ge(cv_out[j % 2], 32 * (j // 2))
            v.tensor_copy(cvrow[0:18, j % 2, :], b[0:18, :]).then_inc(bank_free[USES[key][0]], 1)

        for nb in range(2):
            bi = BLK_DN + nb
            first, n = BLOCKS[bi][:2]
            for s in range(n - 1):
                if first + s + 2 < NSLOT:
                    w_split(first + s + 2)
                if nb == 0:
                    conv_rows(s)
            if nb == 0:
                conv_rows(10)
            sample_sum(bi, fo[0:TS, 4, 512 * nb:512 * nb + 512], ((512, 1.0),), tmp_s3)
            if first + n + 1 < NSLOT:
                w_split(first + n + 1)
        dve.wait_ge(gfin_in, 16)
        for i in range(TILES):
            r = rows(i)
            dve.wait_ge(y_rt, i + 1)
            if i >= 2:
                dve.wait_ge(y_out[i % 2], 16 * (i // 2))
            step(norm_scale(ytmp[0:r, i % 2, :], fo[0:r, i, :], rt_n[0:r, 10 + i:11 + i], rs_n[0:r, 10 + i:11 + i], gfin[0:r]))
            v.tensor_tensor(ytmp[0:r, i % 2, :], ytmp[0:r, i % 2, :], xo[0:r, i, :], ALU.add).then_inc(y_ready, 1)

    ctx.close()


_INS = ("x_prompt", "x_sample", "cache_kv_g0", "cache_kv_g1", "cache_kv_g2", "state_ret", "norm_mix_pre",
        "norm_mix_post", "norm_ffn_pre", "norm_ffn_post")
_OUTS = (("y_prompt", (1, SEQ, D)), ("y_sample", (NB, DT, D)),
         ("p_kv_g0", (1, 1, 128, 2, AH, HD)), ("p_kv_g1", (1, 1, 512, 2, AH, HD)), ("p_kv_g2", (1, 1, 512, 2, AH, HD)),
         ("p_ret", (1, 1, RH, DK, DV)), ("p_conv", (1, 1, 2, 2 * DFF)),
         ("s_kv_g0", (1, NB, 128, 2, AH, HD)), ("s_kv_g1", (1, NB, 512, 2, AH, HD)), ("s_kv_g2", (1, NB, 2048, 2, AH, HD)),
         ("s_ret", (1, NB, RH, DK, DV)), ("s_conv", (1, NB, 2, 2 * DFF)))


def weight_stream(w_in, w_branch_ret, w_branch_attn, w_out, w_ffn_up, w_ffn_down):
    def b_slots(w, per):
        k, n = w.shape
        return w.reshape(k // (128 * per), per, 128, n).transpose(0, 2, 1, 3).reshape(-1, 128, per * n)

    def a_slots(w):
        k, n = w.shape
        return w.reshape(k // 128, 128, n // 128, 128).transpose(2, 1, 0, 3).reshape(n // 128, 128, k)

    rq, rk, rv, rg, aq, ak, av, gr, ga = np.split(w_in, np.cumsum([512, 512, 1024, 1024, 768, 768, 768, 1024])[:8], axis=1)
    ret = np.concatenate([rq, rk, rv], 1)
    att = np.concatenate([aq, ak, av], 1)
    parts = [b_slots(ret[:, 512 * n:512 * n + 512], 2) for n in range(4)]
    parts += [b_slots(att[:, 512 * n:512 * n + 512], 2) for n in range(4)]
    parts.append(b_slots(att[:, 2048:], 4))
    parts += [b_slots(rg[:, 512 * n:512 * n + 512], 2) for n in range(2)]
    parts.append(np.stack([a_slots(gr), a_slots(w_branch_ret)], 1).reshape(-1, 128, SLOT))
    parts.append(a_slots(ga))
    parts.append(np.pad(a_slots(w_branch_attn), ((0, 0), (0, 0), (0, SLOT - BA_W))))
    parts += [b_slots(w_out[:, 512 * n:512 * n + 512], 2) for n in range(2)]
    up = a_slots(w_ffn_up)
    parts.append(np.stack([up[:FT], up[FT:]], 1).reshape(-1, 128, SLOT))
    parts += [b_slots(w_ffn_down[:, 512 * n:512 * n + 512], 2) for n in range(2)]
    return np.concatenate(parts, 0)


def kernel(**inputs):
    import concourse.bacc as bacc
    from concourse.bass_utils import run_bass_kernel_spmd

    inp = {k: np.asarray(x) for k, x in inputs.items()}
    tables, tables_ret = constant_tables()
    arrays = {k: np.ascontiguousarray(inp[k]) for k in _INS}
    arrays["weights"] = weight_stream(*(inp[k][0] for k in ("w_in", "w_branch_ret", "w_branch_attn", "w_out", "w_ffn_up",
                                                            "w_ffn_down")))
    cw = np.concatenate([inp["conv_w"][0], inp["conv_b"]], 0)
    arrays["conv_params"] = np.ascontiguousarray(cw.reshape(4, 2 * FT, 128).transpose(2, 1, 0))
    arrays["conv_state"] = np.ascontiguousarray(
        inp["state_conv"][0].reshape(NB * 2, 2 * FT, 128).transpose(2, 1, 0).reshape(128, -1))
    arrays["tables"], arrays["tables_ret"] = tables, tables_ret

    nc = bacc.Bacc("TRN2", target_bir_lowering=False, num_devices=1)
    f32 = mybir.dt.float32
    a = {k: nc.dram_tensor(f"in_{k}", x.shape, f32, kind="ExternalInput").ap() for k, x in arrays.items()}
    o = {k: nc.dram_tensor(f"out_{k}", shape, f32, kind="ExternalOutput").ap() for k, shape in _OUTS}
    build_layer(nc, a, o)
    r = run_bass_kernel_spmd(nc, [{f"in_{k}": x for k, x in arrays.items()}], core_ids=[0])
    return tuple(r.results[0][f"out_{k}"] for k, _ in _OUTS)
```

```python
import math
from contextlib import ExitStack

import numpy as np
import concourse.bass as bass
from concourse import mybir

D = 1024
KT = D // 128
SEQ = 512
NB = 8
DT = 4
TS = NB * DT
NTOK = SEQ + TS
HALF = NTOK // 2
TILES = 5
PAST = 4096
RH, DK, DV, CHUNK = 4, 128, 256, 128
GROUPS = ((128, 1), (512, 4), (2048, 16))
NG, AH, HD = 3, 4, 64
DFF = 2816
FT = DFF // 128
EPS = 1e-6
SLOT = 1024
NEG = -1e30

S_RET, S_ATT, S_RG, S_GB, S_GA, S_BA = 0, 16, 34, 42, 58, 66
S_OUT = S_BA + 2
S_UP = S_OUT + 8
S_DN = S_UP + 2 * FT
NSLOT = S_DN + FT
BA_W = 256

BLOCKS = ([(S_RET + 4 * n, 4, 2, 512) for n in range(4)] + [(S_ATT + 4 * n, 4, 2, 512) for n in range(4)]
          + [(S_ATT + 16, 2, 4, 256)] + [(S_RG + 4 * n, 4, 2, 512) for n in range(2)]
          + [(S_OUT + 4 * n, 4, 2, 512) for n in range(2)] + [(S_DN + 11 * n, 11, 2, 512) for n in range(2)])
BLK_RQ, BLK_RK, BLK_RV, BLK_AQ, BLK_AQK, BLK_AK, BLK_AV, BLK_AV2, BLK_RG, BLK_OUT, BLK_DN = 0, 1, 2, 4, 5, 6, 7, 8, 9, 11, 13
ROPE_BLOCKS = (BLK_RQ, BLK_RK, BLK_AQ, BLK_AQK, BLK_AK)


def rows(i):
    return 128 if i < 4 else TS


def cols(i):
    return slice(128 * i, 128 * i + rows(i))


def attention_blocks(qb):
    return ([(1, kb) for kb in range(qb + 1)] + [(2, kb) for kb in range(qb + 1)]
            + [(0, kb) for kb in range(max(qb - 1, 0), qb + 1)])


def turns(s):
    return -(-len(attention_blocks(s // 4)) // 4)


def psum_uses():
    order = []
    for i in range(TILES):
        for half in range(2):
            order.append((("x", i, half), 5 + (2 * i + half) % 3))
    turned = lambda b: [(("t", b, i), 5 + i % 3) for i in range(TILES)]
    order += turned(BLK_RQ) + turned(BLK_RK)
    for c in range(4):
        order.append((("S", c), 5))
        if c == 0:
            order.append((("Ss",), 6))
        else:
            order += turned(BLK_AQ + c - 1)
        order += [(("O", c, 0), 6), (("O", c, 1), 7), (("U", c, 0), 5), (("U", c, 1), 5)]
        order += [(("Os", c), 6)] + [(("Us", c, p), (7, 5)[p % 2]) for p in range(4)]
    order += [(("r", 0, i), 5 + i % 3) for i in range(TILES)]
    order += [(("s", 0, g), 4 + g) for g in range(NG)]
    order += [(("r", 1, i), 5 + i % 3) for i in range(TILES)]
    for st in range(17):
        if st:
            order += [(("pt", st - 1, j), 4 + j) for j in range(turns(st - 1))]
            if st % 2 == 0:
                order.append((("o", st // 2 - 1), 7))
        if st < 15:
            order += [(("s", st + 1, g), 4 + g) for g in range(NG)]
    order += [(("st",), 4), (("sn",), 5), (("sp",), 6), (("spn",), 4), (("sv",), 7), (("so",), 5)]
    for i in range(TILES):
        for half in range(2):
            order.append((("h2", i, half), 5 + (2 * i + half) % 3))
    order += [(("cv", j), 5 + j % 3) for j in range(2 * FT // 4)]
    seen, out = {}, {}
    for key, bank in order:
        out[key] = (bank, seen.get(bank, 0))
        seen[bank] = seen.get(bank, 0) + 1
    return out


USES = psum_uses()
SPLIT_KEYS = [k for k in USES if k[0] in ("x", "r", "h2")]
SPLIT_NO = {k: n for n, k in enumerate(SPLIT_KEYS)}


CA_FIELDS = (("ident", 128), ("acos", TILES * 16), ("asin", TILES * 16), ("mask1", 512), ("mask2", 512),
             ("mask0", 256), ("ms0", 128), ("mnew", NG * 32), ("hsel", 4))
CR_FIELDS = (("rcos", TILES * 64), ("rsin", TILES * 128), ("decT", RH * 128), ("qdec", RH * 128), ("kdec", RH),
             ("decTs", RH * 32), ("qdecs", RH * 32), ("kdecs", RH * NB))


def places(fields):
    out, at = {}, 0
    for name, n in fields:
        out[name] = (at, n)
        at += n
    return out, at


CA_AT, CA_N = places(CA_FIELDS)
CR_AT, CR_N = places(CR_FIELDS)


def constant_tables():
    f32 = np.float32
    ca, cr = np.zeros((128, CA_N), f32), np.zeros((128, CR_N), f32)

    def put(a, at, name, v):
        o, n = at[name]
        v = np.asarray(v, np.float64)
        a[:v.shape[0], o:o + n] = v.reshape(v.shape[0], n).astype(f32)

    pos = np.zeros((TILES, 128), f32)
    pos[:4] = np.arange(SEQ).reshape(4, 128)
    pos[4, :TS] = PAST + np.arange(TS) % DT
    af = (np.float64(500000.0) ** (-(np.arange(8, dtype=f32) / f32(8)).astype(np.float64))).astype(f32)
    ang = (pos[:, :, None] * af).astype(f32).astype(np.float64)
    put(ca, CA_AT, "acos", np.concatenate([np.cos(ang), np.cos(ang)], -1).transpose(1, 0, 2))
    put(ca, CA_AT, "asin", np.concatenate([-np.sin(ang), np.sin(ang)], -1).transpose(1, 0, 2))
    rf = (np.float64(10000.0) ** (-(np.arange(64, dtype=f32) * f32(1 / 63)).astype(np.float64))).astype(f32)
    ang = (pos[:, :, None] * rf).astype(f32).astype(np.float64)
    put(cr, CR_AT, "rcos", np.cos(ang).transpose(1, 0, 2))
    put(cr, CR_AT, "rsin", np.concatenate([-np.sin(ang), np.sin(ang)], -1).transpose(1, 0, 2))
    put(ca, CA_AT, "ident", np.eye(128))
    i, j = np.arange(128)[:, None], np.arange(128)[None, :]
    for name, dil in (("mask1", 4), ("mask2", 16)):
        off = np.where((i - j) % dil == 0, 0.0, NEG)
        diag = np.where(((i - j) % dil == 0) & (j <= i), 0.0, NEG)
        put(ca, CA_AT, name, np.concatenate([off, off, off, diag], 1))
    put(ca, CA_AT, "mask0", np.concatenate([np.where(j >= i, 0.0, NEG), np.where(j <= i, 0.0, NEG)], 1))
    p = np.arange(128)
    b, t, h = p // 16, p // 4 % 4, p % 4
    put(ca, CA_AT, "ms0", np.where(j >= t[:, None], 0.0, NEG))
    kb, kt = np.arange(TS)[None] // 4, np.arange(TS)[None] % 4
    same = kb == b[:, None]
    m0 = np.where(same & (kt <= t[:, None]), 0.0, NEG)
    m1 = np.where(same & (kt == t[:, None]), 0.0, NEG)
    put(ca, CA_AT, "mnew", np.stack([m0, m1, m1], 1))
    put(ca, CA_AT, "hsel", (h[:, None] == np.arange(4)[None]).astype(f32))
    lg = log_decay()
    dec = np.where(j[None] >= i[None], np.exp(lg[:, None, None] * np.maximum(j - i, 0)[None]), 0.0)
    put(cr, CR_AT, "decT", dec.transpose(1, 0, 2))
    put(cr, CR_AT, "qdec", np.broadcast_to(np.exp(lg[:, None] * (np.arange(128) + 1.0))[None], (128, 4, 128)))
    put(cr, CR_AT, "kdec", np.exp(lg[None] * (127.0 - np.arange(128))[:, None]))
    sj, si = np.arange(TS)[:, None], np.arange(TS)[None, :]
    ok = (sj // 4 == si // 4) & (sj <= si)
    dec = np.where(ok[None], np.exp(lg[:, None, None] * np.maximum(si - sj, 0)[None]), 0.0)
    put(cr, CR_AT, "decTs", dec.transpose(1, 0, 2))
    put(cr, CR_AT, "qdecs", np.broadcast_to(np.exp(lg[:, None] * (np.arange(TS) % 4 + 1.0))[None], (128, 4, TS)))
    kd = np.exp(lg[None] * (3.0 - np.arange(TS) % 4)[:, None])
    put(cr, CR_AT, "kdecs", kd[:, :, None] * (np.arange(TS)[:, None, None] // 4 == np.arange(NB)[None, None]))
    return ca, cr


def log_decay():
    return np.log1p(-np.exp2(-5.0 - np.arange(RH)))


GAMMA_CHUNK = [float(x) for x in np.exp(log_decay() * CHUNK)]
GAMMA_STEP = [float(x) for x in np.exp(log_decay() * DT)]


def build_layer(nc, a, o):
    F, R = mybir.dt.float32, mybir.dt.float32r
    ALU, ACT, AX = mybir.AluOpType, mybir.ActivationFunctionType, mybir.AxisListType
    ctx = ExitStack()

    base = 16512

    def sb(name, at, shape, dt=F):
        return nc.alloc_sbuf_tensor_at(name, shape, dt, offset=base + 4 * at)

    T1h = sb("T1h", 0, [128, KT, NTOK], R)
    T1l = sb("T1l", 4352, [128, KT, NTOK], R)
    T1s = sb("T1s", 8704, [128, KT, 64], R)
    wraw = sb("wraw", 9216, [128, 2, SLOT])
    whi = sb("whi", 11264, [128, 2, SLOT], R)
    wlo = sb("wlo", 13312, [128, 2, SLOT], R)
    CA0 = 15360
    ca_t = sb("ca", CA0, [128, CA_N])
    CONVP = CA0 + (CA_N + 7) // 8 * 8
    convp = sb("convp", CONVP, [128, 2 * FT, 4])
    STAT = CONVP + 8 * FT
    stat = sb("stat", STAT, [128, 144])
    col = lambda n, w: stat[:, n:n + w]
    ss_x, rt_x, rs_x = (col(5 * k, 5) for k in range(3))
    ss_r, rt_r, rs_r = (col(16 + 20 * k, 20) for k in range(3))
    mx = col(76, 8).rearrange("p (a b) -> p a b", a=2)
    nm, den, rden = col(84, 2), col(86, 2), col(88, 2)
    ss_n, rt_n, rs_n = (col(90 + 15 * k, 15) for k in range(3))
    eps = col(135, 1)
    ss_h = col(136, 5)
    assert CR_N <= 2304
    X = (STAT + 144 + 7) // 8 * 8
    ATT = X + 17168
    SCR = ATT + 10368
    END = (229368 - base) // 4
    assert SCR + 8192 <= END, (SCR, END)
    cr_t = sb("cr", X, [128, CR_N])
    QT = X + 2304
    qT = sb("qT", QT, [128, RH, NTOK])
    kT = sb("kT", QT + 2176, [128, RH, NTOK])
    RBk = sb("rope_k", QT + 4352, [128, TILES, 512])
    V0 = QT + 6912
    vt = sb("v", V0, [128, 4, D])
    vs = sb("v_s", V0 + 4096, [128, D])
    RBq = sb("rope_q", V0 + 5120, [128, TILES, 512])
    assert V0 + 7680 <= ATT
    aqT = sb("aqT", ATT, [128, 6, NTOK])
    akT = sb("akT", ATT + 3264, [128, 6, NTOK])
    av = sb("av", ATT + 6528, [128, 4, 768])
    avs = sb("av_s", ATT + 9600, [128, 768])
    xin = sb("xin", ATT, [128, TILES, D])
    gpre = sb("gpre", ATT + 5120, [128, D])
    xn = sb("xn", ATT + 6144, [128, 2, D])
    junk = sb("junk", ATT + 8192, [128, D])
    at = SCR
    tmp_s = sb("tmp_s", at, [128, 512]); at += 512
    ropet = sb("ropet", at, [128, 2, 512]); at += 1024
    PT = sb("PT", at, [128, RH, 128]); at += 512
    kd = sb("kd", at, [128, 512]); at += 512
    qd = sb("qd", at, [128, RH, 128]); at += 512
    state = sb("state", at, [128, RH, DV]); at += 1024
    S0 = sb("S0", at, [128, 4, 2, DV]); at += 2048
    qm = sb("qm", at, [128, 2, NB, 32]); at += 512
    km = sb("km", at, [128, NB, 128]); at += 1024
    rjunk = sb("rjunk", at, [128, DV]); at += 256
    PTs = sb("PTs", at, [128, RH, 32]); at += 128
    assert at <= END, (at, END)
    rTh = sb("rTh", X, [128, KT, NTOK], R)
    rTl = sb("rTl", X + 4352, [128, KT, NTOK], R)
    rTs = sb("rTs", X + 8704, [128, KT, 64], R)
    assert X + 9216 <= V0
    etmp = sb("etmp", SCR + 512, [128, 2, 512])
    mixr = sb("mixr", V0, [128, KT, NTOK])
    gexp = sb("gexp", V0 + 5120, [128, NTOK])
    at = SCR
    sc = sb("sc", at, [128, 2, 1280]); at += 2560
    pT = sb("pT", at, [128, 1280]); at += 1280
    qpad = sb("qpad", at, [128, 2, NG, 128]); at += 768
    aoh = sb("aoh", at, [128, 2, NTOK], R); at += 2 * NTOK
    aol = sb("aol", at, [128, 2, NTOK], R); at += 2 * NTOK
    qbc = [sb("qbc0", at, [128, 2, 256]), sb("qbc1", at + 512, [128, 2, 256])]; at += 1024
    sTk = sb("sTk", at, [128, NG, 128]); at += 384
    assert at <= END
    kvk = sb("kvk", V0 + 5664, [128, 3, 2, 256])
    prod = sb("prod", V0 + 7200, [128, 512])
    qbc.append(sb("qbc2", V0 + 4352, [128, 2, 256]))
    assert V0 + 7712 <= ATT
    sga = sb("sga", X, [128, KT, NTOK])
    kvv = (sb("kvv0", ATT + 6528, [128, 3, DT, 256]), sb("kvv1", X + 4352, [128, 3, DT, 256]),
           sb("kvv2", V0 + 4352, [128, 3, DT, 256]))
    srow = sb("srow", X + 7808, [128, NG, 160])
    at = SCR
    pad0 = sb("pad0", at, [128, 256]); at += 256
    pad1 = sb("pad1", at, [128, 2, 1024]); at += 2048
    pnew = sb("pnew", at, [128, NG, 128]); at += 384
    qbd = sb("qbd", at, [128, NG, 2, 128]); at += 768
    osel = sb("osel", at, [128, 4, HD]); at += 256
    orow = sb("orow", at, [128, HD]); at += 64
    aosf = sb("aosf", at, [128, 2, 32]); at += 64
    assert at <= SCR + 3840
    MT = ATT
    mTh = sb("mTh", MT, [128, KT, NTOK], R)
    mTl = sb("mTl", MT + 4352, [128, KT, NTOK], R)
    mTs = sb("mTs", MT + 8704, [128, KT, 64], R)
    mtmp = sb("mtmp", SCR, [128, 3, NTOK])
    xo = sb("xo", X, [128, TILES, D])
    xr = sb("xr", X + 5120, [128, TILES, D])
    gpost = sb("gpost", X + 10240, [128, D])
    gffn = sb("gffn", X + 11264, [128, D])
    tmpn = sb("tmpn", SCR + 1200, [128, 2, D])
    hn = sb("hn", SCR + 3248, [128, 2, D])
    njunk = sb("njunk", SCR + 5296, [128, D])
    tmp_s2 = sb("tmp_s2", SCR + 6400, [128, 512])
    fTh = sb("fTh", X + 5120, [128, FT * NTOK], R)
    fTl = sb("fTl", X + 17088, [128, FT * NTOK], R)
    fTs = sb("fTs", X + 29056, [128, FT * 64], R)
    U0 = X + 30464
    UW = 2 + SEQ + NB * 6
    CW = UW - 2
    ub = sb("u", U0, [128, 2, 2, UW])
    cb = sb("c", U0 + 4 * UW, [128, 2, UW])
    cvt = sb("cv_tail", U0 + 3376, [128, 2 * FT * 18])
    cvs = sb("cv_state", U0 + 3376 + 36 * FT, [128, 2 * FT * 16])
    assert U0 + 3376 + 68 * FT <= END
    fo = sb("fo", 0, [128, TILES, D])
    gfin = sb("gfin", 5120, [128, D])
    tmp_s3 = sb("tmp_s3", 8192, [128, 512])
    fjunk = sb("fjunk", U0, [128, D])
    cvrow = sb("cv_row", U0 + 1024, [128, 2, 512])
    assert U0 + 2048 <= U0 + 6 * UW

    def cav(name, *shape):
        off, n = CA_AT[name]
        v = ca_t[:, off:off + n]
        return v.rearrange("p (a b) -> p a b", a=shape[0]) if shape else v

    def crv(name, *shape):
        off, n = CR_AT[name]
        v = cr_t[:, off:off + n]
        return v.rearrange("p (a b) -> p a b", a=shape[0]) if shape else v

    ident = cav("ident")
    P = [ctx.enter_context(nc.psum_tensor(f"bank{n}", [128, 512], F)) for n in range(8)]

    def sem(name):
        return ctx.enter_context(nc.semaphore(name))

    w_raw = [sem(f"w_raw{n}") for n in range(2)]
    w_hi, w_lo, w_used = sem("w_hi"), sem("w_lo"), sem("w_used")
    b_full = sem("b_full")
    b_free = [sem(f"b_free{i}") for i in range(TILES)]
    a_free = [sem(f"a_free{n}") for n in range(2)]
    bank_full = {n: sem(f"bank_full{n}") for n in range(4, 8)}
    bank_free = {n: sem(f"bank_free{n}") for n in range(4, 8)}
    split_hi = sem("split_hi")
    x_in = [sem(f"x_in{i}") for i in range(TILES)]
    x_again = [sem(f"x_again{i}") for i in range(TILES)]
    ident_in = sem("ident_in")
    ca_in, cr_in, gpre_in, convp_in = sem("ca_in"), sem("cr_in"), sem("gpre_in"), sem("convp_in")
    g2_in, gfin_in, cvs_in = sem("g2_in"), sem("gfin_in"), sem("cvs_in")
    act_step, dve_step, pool_step = sem("act_step"), sem("dve_step"), sem("pool_step")
    x_sq, x_rt, x_norm = sem("x_sq"), sem("x_rt"), sem("x_norm")
    tmp_ready = sem("tmp_ready")
    rope_done = sem("rope_done")
    cleared = sem("cleared")
    kd_ready, qd_ready, qm_ready, km_ready = sem("kd_ready"), sem("qd_ready"), sem("qm_ready"), sem("km_ready")
    s0_in = [sem(f"s0_in{n}") for n in range(4)]
    s1_out = [sem(f"s1_out{n}") for n in range(4)]
    on_sq, rt_ready = sem("on_sq"), sem("rt_ready")
    e_ready, r_ready = sem("e_ready"), sem("r_ready")
    k_out, av_out = sem("k_out"), sem("av_out")
    qs_out = sem("qs_out")
    state_out_done = sem("state_out_done")
    windows_moved = sem("windows_moved")
    q_padded, maxed, exped, probs = sem("q_padded"), sem("maxed"), sem("exped"), sem("probs")
    o_hi = sem("o_hi")
    kk_in = [sem(f"kk_in{n}") for n in range(3)]
    kv_in = [sem(f"kv_in{n}") for n in range(9)]
    q_in = [sem(f"q_in{n}") for n in range(3)]
    s_step, pads_ready, qbd_ready, v_used, s_probs = (sem("s_step"), sem("pads_ready"), sem("qbd_ready"),
                                                     sem("v_used"), sem("s_probs"))
    s_max, s_exp, o_row, os_hi, os_lo = (sem(n) for n in ("s_max", "s_exp", "o_row", "os_hi", "os_lo"))
    branch_done = sem("branch_done")
    mix_sum, mix_hi, mix_lo = sem("mix_sum"), sem("mix_hi"), sem("mix_lo")
    n_sq, n_rt, x2_ready, h_ready = sem("n_sq"), sem("n_rt"), sem("x2_ready"), sem("h_ready")
    u_evac = [sem(f"u_evac{n}") for n in range(2)]
    conv_done, tail_done, head_ready, conv_tap = sem("conv_done"), sem("tail_done"), sem("head_ready"), sem("conv_tap")
    gelu_done, f_done, f_hi, f_lo = sem("gelu_done"), sem("f_done"), sem("f_hi"), sem("f_lo")
    half_sq, half_bias, x_scaled = sem("half_sq"), sem("half_bias"), sem("x_scaled")
    y_sq, y_rt, y_ready = sem("y_sq"), sem("y_rt"), sem("y_ready")
    y_scaled, y_half = sem("y_scaled"), sem("y_half")
    y_out = sem("y_out")
    cv_out = [sem(f"cv_out{n}") for n in range(2)]

    def emptied(eng, key):
        bank, n = USES[key]
        eng.wait_ge(bank_free[bank], n + 1)

    def filled(eng, key):
        bank, n = USES[key]
        eng.wait_ge(bank_full[bank], n + 1)
        return P[bank]

    def c_sample(c):
        return c[:, 2 + SEQ:UW].rearrange("p (b t) -> p b t", t=6)[:, :, 0:4]

    w_dram, kv_dram = a["weights"], [a[f"cache_kv_g{g}"] for g in range(NG)]
    qs_dram = nc.dram_tensor("sample_queries", [TS, 768], F).ap()
    new_kv_dram = nc.dram_tensor("sample_keys_values", [TS, 2, 768], F).ap()
    up_loop = 2 * FT // 4

    block = ctx.enter_context(nc.Block())

    @block.sync
    def _(sp):
        def load_x(i):
            sp.dma_start(xin[0:rows(i), i, :], a["x_prompt"][0, 128 * i:128 * i + 128, :] if i < 4 else
                         a["x_sample"].rearrange("b t d -> (b t) d")).then_inc(x_in[i], 16)

        load_x(0)
        sp.dma_start(gpre[:], a["norm_mix_pre"].broadcast_to([128, D])).then_inc(gpre_in, 16)
        sp.dma_start(ca_t[:, 0:128], a["tables"][:, 0:128]).then_inc(ident_in, 16)
        load_x(1)
        sp.dma_start(wraw[:, 0, :], w_dram[0]).then_inc(w_raw[0], 16)
        load_x(2)
        load_x(3)
        load_x(4)
        sp.dma_start(wraw[:, 1, :], w_dram[1]).then_inc(w_raw[1], 16)
        sp.dma_start(ca_t[:, 128:CA_N], a["tables"][:, 128:CA_N]).then_inc(ca_in, 16)
        sp.dma_start(cr_t[:], a["tables_ret"]).then_inc(cr_in, 16)
        sp.dma_start(convp[:], a["conv_params"]).then_inc(convp_in, 16)

        def load(slot):
            for j in range(2):
                sp.wait_ge(w_lo, slot + (j - 1))
                src = w_dram[bass.ds(slot + j, 1)].rearrange("a p n -> p (a n)")
                sp.dma_start(wraw[:, j, :], src).then_inc(w_raw[j], 16)

        def move(g, b, piece, pieces):
            n = (GROUPS[g][0] - DT) * 512 // pieces
            inner = {0: 1, 1: 1, 2: 7}[g]
            flat = lambda t: t[0, bass.ds(b, 1)].rearrange("a w c h d -> (a w c h d)")
            cut = lambda t, at_: flat(t)[at_ + n * piece:at_ + n * piece + n].rearrange("(e r c) -> e r c", e=16, r=inner)
            sp.dma_start(cut(o[f"s_kv_g{g}"], 0), cut(kv_dram[g], DT * 512)).then_inc(windows_moved, 16)

        with sp.Fori(0, NB) as b:
            for e in range(8):
                load(b * 16 + (2 + 2 * e))
                move(2, b, e, 8)
                if e % 4 == 1:
                    move(1, b, e // 4, 2)
                if e == 3:
                    move(0, b, 0, 1)
        with sp.Fori(0, (NSLOT - 130) // 2) as it:
            load(it * 2 + 130)
        sp.wait_ge(k_out, 16 * (NG + 2))
        sp.wait_ge(av_out, 16 * (NG + 1))
        for g in range(NG):
            W = GROUPS[g][0]
            for which in range(2):
                sp.dma_start(o[f"s_kv_g{g}"][0, :, W - DT:W, which].rearrange("b t h d -> b t (h d)"),
                             new_kv_dram[:, which, 256 * g:256 * g + 256].rearrange("(b t) n -> b t n", b=NB)
                             ).then_inc(windows_moved, 16)
        sp.wait_ge(windows_moved, 16 * (NB * (8 + 2 + 1) + 2 * NG))
        for i in range(TILES):
            sp.wait_ge(y_ready, i + 1)
            sp.wait_ge(y_half, i + 1)
            dst = o["y_prompt"][0, 128 * i:128 * i + 128, :] if i < 4 else o["y_sample"].rearrange("b t d -> (b t) d")
            sp.dma_start(dst, fo[0:rows(i), i, :]).then_inc(y_out, 16)
        sp.wait_ge(y_out, 16 * TILES)

    @block.gpsimd
    def _(pool):
        steps = [0]

        def step(ins):
            steps[0] += 1
            ins.then_inc(pool_step, 1)
            pool.wait_ge(pool_step, steps[0])

        nc.gpsimd.memset(ss_r[:], 1.0).then_inc(cleared, 1)
        nc.gpsimd.memset(eps[:], EPS).then_inc(cleared, 1)
        nc.gpsimd.memset(vs[:], 0.0).then_inc(cleared, 1)
        nc.gpsimd.memset(qm[:], 0.0).then_inc(cleared, 1)
        nc.gpsimd.memset(km[:], 0.0).then_inc(cleared, 1)
        for j in range(2):
            pool.wait_ge(w_hi, j + 1)
            nc.gpsimd.tensor_tensor(wlo[:, j, :], wraw[:, j, :], whi[:, j, :].bitcast(F), ALU.subtract).then_inc(w_lo, 1)
        state_in = a["state_ret"]
        state_out = o["s_ret"]

        def load_state(h, p):
            if h:
                pool.wait_ge(s1_out[p], 16 * h)
            pool.dma_start(S0[:, p], state_in[0, 2 * p:2 * p + 2, h].rearrange("b k v -> k b v")
                           ).then_inc(s0_in[p], 16)

        def store_prompt(which, g, prompt, signal):
            dst = o[f"p_kv_g{g}"][0, 0, :, which].rearrange("(n p) h d -> p n (h d)", p=128)
            pool.dma_start(dst, prompt[:, 4 - min(GROUPS[g][0], SEQ) // 128:4]).then_inc(signal, 16)

        pool.wait_ge(w_used, 2)
        for q in range(4):
            load_state(0, q)
        pool.wait_ge(cr_in, 16)
        pool.wait_ge(cleared, 5)
        pool.wait_ge(rope_done, 10)
        for c in range(4):
            if c:
                filled(pool, ("U", c - 1, 1))
            nc.gpsimd.tensor_tensor(kd[:].rearrange("p (h d) -> p h d", h=RH),
                                    RBk[:, c, :].rearrange("p (h d) -> p h d", h=RH),
                                    crv("kdec").unsqueeze(2).broadcast_to([128, RH, 128]), ALU.mult
                                    ).then_inc(kd_ready, 1)
            if c:
                filled(pool, ("Us", c - 1, 3))
            nc.gpsimd.tensor_tensor(km[0:TS], RBk[0:TS, 4, 128 * c:128 * c + 128].unsqueeze(1).broadcast_to([TS, NB, 128]),
                                    crv("kdecs", RH)[0:TS, c, :].unsqueeze(2).broadcast_to([TS, NB, 128]), ALU.mult
                                    ).then_inc(km_ready, 1)
            if c >= 1:
                pool.wait_ge(rope_done, 10 + 5 * c)
                if c == 1:
                    pool.dma_start(qs_dram[:, 0:512], RBq[0:TS, 4, :]).then_inc(qs_out, 16)
                elif c == 2:
                    pool.dma_start(qs_dram[:, 512:768], RBq[0:TS, 4, 0:256]).then_inc(qs_out, 16)
                    store_prompt(0, 0, RBq[:, 0:4, 256:512], k_out)
                    pool.dma_start(new_kv_dram[:, 0, 0:256], RBq[0:TS, 4, 256:512]).then_inc(k_out, 16)
                else:
                    for g in (1, 2):
                        store_prompt(0, g, RBq[:, 0:4, 256 * (g - 1):256 * g], k_out)
                    pool.dma_start(new_kv_dram[:, 0, 256:768], RBq[0:TS, 4, :]).then_inc(k_out, 16)
            for q in range(4):
                emptied(pool, ("Us", c, q))
                pool.dma_start(state_out[0, 2 * q:2 * q + 2, c].rearrange("b k v -> k b v"), S0[:, q]
                               ).then_inc(s1_out[q], 16)
            if c < 3:
                for q in range(4):
                    load_state(c + 1, q)
        pool.dma_start(o["p_ret"][0, 0].rearrange("h k v -> k h v"), state[:]).then_inc(state_out_done, 16)
        for i in range(TILES):
            pool.wait_ge(b_free[i], BLK_AV2 + 1)
        for g in range(NG):
            store_prompt(1, g, av[:, 0:4, 256 * g:256 * g + 256], av_out)
        pool.dma_start(new_kv_dram[:, 1, :], avs[0:TS, :]).then_inc(av_out, 16)
        for q in range(4):
            pool.wait_ge(s1_out[q], 16 * RH)
        emptied(pool, ("r", 0, 4))
        pool.wait_ge(state_out_done, 16)
        step(nc.gpsimd.memset(qpad[:], 0.0))

        def pad_queries(s):
            qb, h = s // 4, s % 4
            par, hp = h % 2, h // 2
            if s >= 2:
                filled(pool, ("s", s - 2, 2))
            for g in range(NG):
                last = nc.gpsimd.tensor_copy(qpad[64 * par:64 * par + 64, par, g, :],
                                             aqT[64 * par:64 * par + 64, 2 * g + hp, 128 * qb:128 * qb + 128])
            last.then_inc(q_padded, 1)

        def load_piece(n):
            b, g, t = n // 6, n // 2 % NG, 2 * (n % 2)
            if n >= 3:
                pool.wait_ge(s_step, n - 2)
            if g == 0:
                pool.dma_start(kvk[:, n % 3, 0, :], kv_dram[0][0, b, :, 0].rearrange("n h d -> n (h d)")
                               ).then_inc(kk_in[n % 3], 16)
            else:
                src = kv_dram[g][0, b].rearrange("(n r) c h d -> n r c (h d)", r=GROUPS[g][1])[:, t:t + 2, 0]
                pool.dma_start(kvk[:, n % 3], src).then_inc(kk_in[n % 3], 16)
            src = qs_dram[4 * b + t:4 * b + t + 2, 256 * g:256 * g + 256].unsqueeze(0).broadcast_to([128, 2, 256])
            pool.dma_start(qbc[n % 3][:], src).then_inc(q_in[n % 3], 16)

        pool.wait_ge(qs_out, 32)
        pool.wait_ge(k_out, 16 * (NG + 2))
        filled(pool, ("t", BLK_AK, 4))
        pad_queries(0)
        pad_queries(1)
        filled(pool, ("r", 1, 4))
        for s in range(16):
            if s < 14:
                pad_queries(s + 2)
            for n in range(3 * s, 3 * s + 3):
                load_piece(n)
        filled(pool, ("o", 7))
        pool.wait_ge(o_hi, 8)
        step(nc.gpsimd.memset(qbd[:], 0.0))
        for g in range(NG):
            for hp in range(2):
                for par in range(2):
                    dst = qbd[64 * par:64 * par + 64, g, hp, :].rearrange("p (n h) -> p n h", h=4)[:, :, 2 * hp + par]
                    last = nc.gpsimd.tensor_copy(dst, aqT[64 * par:64 * par + 64, 2 * g + hp, SEQ:NTOK])
        last.then_inc(qbd_ready, 1)
        pool.wait_ge(av_out, 16 * (NG + 1))
        pool.wait_ge(w_used, S_GA)

        def load_values(n):
            b, g = n // NG, n % NG
            if n >= 9:
                pool.wait_ge(v_used, n - 8)
            elif n == 6:
                pool.wait_ge(s_step, 48)
                pool.wait_ge(a_free[1], 8)
            place = kvv[n % 9 // 3][:, n % 3]
            if g == 0:
                pool.dma_start(place[:, 0, :], kv_dram[0][0, b, :, 1].rearrange("n h d -> n (h d)")
                               ).then_inc(kv_in[n % 9], 16)
            else:
                src = kv_dram[g][0, b].rearrange("(n r) c h d -> n r c (h d)", r=GROUPS[g][1])[:, 0:DT, 1]
                pool.dma_start(place, src).then_inc(kv_in[n % 9], 16)

        for n in range(6):
            load_values(n)
        pool.wait_ge(qbd_ready, 1)
        nc.gpsimd.memset(pad0[:], 0.0).then_inc(pads_ready, 1)
        nc.gpsimd.memset(pad1[:], 0.0).then_inc(pads_ready, 1)
        for n in range(6, 24):
            load_values(n)
        for n in range(KT):
            pool.wait_ge(a_free[n % 2], 13 + n // 2)
            nc.gpsimd.tensor_tensor(mtmp[:, n % 3, :], mtmp[:, n % 3, :], mixr[:, n, :], ALU.add).then_inc(mix_sum, 1)
        pool.wait_ge(mix_lo, KT)
        for i in range(TILES):
            r = rows(i)
            pool.dma_start(xr[0:r, i, :], a["x_prompt"][0, 128 * i:128 * i + 128, :] if i < 4 else
                           a["x_sample"].rearrange("b t d -> (b t) d")).then_inc(x_again[i], 16)
        pool.dma_start(gpost[:], a["norm_mix_post"].broadcast_to([128, D])).then_inc(g2_in, 16)
        pool.dma_start(gffn[:], a["norm_ffn_pre"].broadcast_to([128, D])).then_inc(g2_in, 16)
        for i in range(TILES):
            r = rows(i)
            pool.wait_ge(x_again[i], 16)
            pool.wait_ge(x_scaled, i + 1)
            nc.gpsimd.tensor_tensor(xo[0:r, i, :], tmpn[0:r, i % 2, :], xr[0:r, i, :], ALU.add).then_inc(x2_ready, 1)
        filled(pool, ("h2", 4, 1))
        emptied(pool, ("h2", 4, 1))
        pool.dma_start(cvs[:], a["conv_state"]).then_inc(cvs_in, 16)
        step(nc.gpsimd.memset(ub[:], 0.0))
        pool.wait_ge(cvs_in, 16)
        pool.sem_inc(tail_done, 4)
        with pool.Fori(0, up_loop) as it:
            for q in range(2):
                for j in range(2):
                    tile = it * 2 + (q + FT * j)
                    u_s = ub[:, q, j, 2 + SEQ:].rearrange("p (b t) -> p b t", t=6)
                    pool.wait_ge(conv_done, it * 4 + (2 * q + j + 1))
                    nc.gpsimd.tensor_copy(u_s[:, :, 0:2], cvs[:, bass.ds(tile * 16, 16)].rearrange("p (b t) -> p b t", t=2)
                                          ).then_inc(head_ready, 1)
                    pool.wait_ge(u_evac[j], it * 2 + (q + 2))
                    nc.gpsimd.tensor_copy(cvt[:, bass.ds(tile * 18, 2)], ub[:, q, j, SEQ:SEQ + 2])
                    nc.gpsimd.tensor_copy(cvt[:, bass.ds(tile * 18 + 2, 16)].rearrange("p (b t) -> p b t", t=2),
                                          u_s[:, :, 4:6]).then_inc(tail_done, 1)
        for j in range(2 * FT // 4):
            emptied(pool, ("cv", j))
            pool.dma_start(o["p_conv"][0, 0, :, 512 * j:512 * j + 512], cvrow[0:2, j % 2, :]).then_inc(cv_out[j % 2], 16)
            pool.dma_start(o["s_conv"][0].rearrange("b t n -> (b t) n")[:, 512 * j:512 * j + 512], cvrow[2:18, j % 2, :]
                           ).then_inc(cv_out[j % 2], 16)
        pool.dma_start(gfin[:], a["norm_ffn_post"].broadcast_to([128, D])).then_inc(gfin_in, 16)
        for i in range(TILES):
            pool.wait_ge(y_scaled, i + 1)
            r = rows(i)
            nc.gpsimd.tensor_tensor(fo[0:r, i, 0:512], fo[0:r, i, 0:512], xo[0:r, i, 0:512], ALU.add
                                    ).then_inc(y_half, 1)
        pool.wait_ge(state_out_done, 16)
        pool.wait_ge(k_out, 16 * (NG + 2))
        pool.wait_ge(av_out, 16 * (NG + 1))
        for n in range(2):
            pool.wait_ge(cv_out[n], 32 * (6 - n))

    @block.scalar
    def _(act):
        steps = [0]

        def step(ins):
            steps[0] += 1
            ins.then_inc(act_step, 1)
            act.wait_ge(act_step, steps[0])

        def w_split(s):
            act.wait_ge(w_raw[s % 2], 16 * (s // 2 + 1))
            if s >= 2:
                act.wait_ge(w_used, s - 1)
            nc.scalar.activation(whi[:, s % 2, :], wraw[:, s % 2, :], ACT.Copy).then_inc(w_hi, 1)

        def split_evac(key, Th, Ts, k0, i):
            b = filled(act, key)
            n = rows(i)
            src = b[:, 0:4 * n].rearrange("p (k n) -> p k n", k=4)
            ins = nc.scalar.activation(Th[:, k0:k0 + 4, cols(i)], src, ACT.Copy)
            if i == 4:
                ins = nc.scalar.activation(Ts[:, k0:k0 + 4, 0:32], src, ACT.Copy)
            ins.then_inc(split_hi, 1)

        def tile_end(bi, i):
            if i == 3:
                act.wait_ge(w_used, sum(BLOCKS[bi][:2]))
            else:
                act.wait_ge(b_full, 4 * bi + (2, 3, 4, 0, 1)[i])

        def sample_lo(bi, tmp, width, scales):
            if bi:
                act.wait_ge(b_free[4], bi)
            at_ = 0
            for w, scale in scales:
                ins = nc.scalar.activation(tmp[0:TS, at_:at_ + w], P[4][32:64, at_:at_ + w], ACT.Copy, scale=scale)
                at_ += w
            ins.then_inc(tmp_ready, 1)

        def evac_block(bi, dst, width, scales, tmp=tmp_s):
            tile_end(bi, 4)
            sample_lo(bi, tmp, width, scales)
            for i in range(4):
                tile_end(bi, i)
                at_ = 0
                for w, scale in scales:
                    ins = nc.scalar.activation(dst(i)[:, at_:at_ + w], P[i][:, at_:at_ + w], ACT.Copy, scale=scale)
                    at_ += w
                ins.then_inc(b_free[i], 1)

        def turn_evac(bi):
            for i in range(TILES):
                b = filled(act, ("t", bi, i))
                n = rows(i)
                src = b[:, 0:4 * n].rearrange("p (k n) -> p k n", k=4)
                if bi == BLK_RQ:
                    parts = ((qT, 0, 0, 4),)
                elif bi == BLK_RK:
                    parts = ((kT, 0, 0, 4),)
                elif bi == BLK_AQ:
                    parts = ((aqT, 0, 0, 4),)
                elif bi == BLK_AQK:
                    parts = ((aqT, 4, 0, 2), (akT, 0, 2, 2))
                else:
                    parts = ((akT, 2, 0, 4),)
                for dst, d0, s0, k in parts:
                    ins = nc.scalar.activation(dst[:, d0:d0 + k, cols(i)], src[:, s0:s0 + k, :], ACT.Copy)
                ins.then_inc(bank_free[USES[("t", bi, i)][0]], 1)

        def half_squares(first_bi, x, junk_, base):
            for i in range(TILES):
                r = rows(i)
                if base + i:
                    act.wait_ge(half_sq, base + i)
                act.wait_ge(b_free[i], first_bi + 1)
                nc.scalar.activation(junk_[0:r, 0:512], x[0:r, i, 0:512], ACT.Square, accum_out=ss_h[0:r, i:i + 1]
                                     ).then_inc(half_sq, 1)
            act.wait_ge(half_sq, base + TILES)
            step(nc.scalar.activation(junk_[:, 0:1], eps[:, 0:1], ACT.Sqrt))

        def roots(bi, x, junk_, at_, squared, rooted):
            act.wait_ge(half_bias, (bi - BLK_OUT) // 2 + 1)
            for i in range(TILES):
                r = rows(i)
                if i < 4:
                    tile_end(bi, i)
                    src = P[i][:, :]
                else:
                    act.wait_ge(b_free[4], bi + 1)
                    src = x[0:r, 4, 512:1024]
                nc.scalar.activation(junk_[0:r, 0:512], src, ACT.Square, accum_out=ss_n[0:r, at_ + i:at_ + i + 1]
                                     ).then_inc(squared, 1)
                act.wait_ge(squared, i + 1)
                nc.scalar.activation(rt_n[0:r, at_ + i:at_ + i + 1], ss_n[0:r, at_ + i:at_ + i + 1], ACT.Sqrt, scale=1.0 / D,
                                     bias=ss_h[0:r, i:i + 1]).then_inc(rooted, 1)

        act.wait_ge(cleared, 2)
        step(nc.scalar.activation(rt_x[:, 0:1], eps[:, 0:1], ACT.Sqrt))
        for i in range(TILES + 2):
            if i < TILES:
                r = rows(i)
                act.wait_ge(x_in[i], 16)
                nc.scalar.activation(junk[0:r], xin[0:r, i, :], ACT.Square, accum_out=ss_x[0:r, i:i + 1]).then_inc(x_sq, 1)
                act.wait_ge(x_sq, i + 1)
                nc.scalar.activation(rt_x[0:r, i:i + 1], ss_x[0:r, i:i + 1], ACT.Sqrt, scale=1.0 / D,
                                     bias=eps[0:r, 0:1]).then_inc(x_rt, 1)
            if i >= 2:
                for half in range(2):
                    split_evac(("x", i - 2, half), T1h, T1s, 4 * half, i - 2)
            if i in (1, 2):
                w_split(i - 1)

        dests = {
            BLK_RQ: (lambda i: RBq[:, i, :], ((512, 1.0),)),
            BLK_RK: (lambda i: RBk[:, i, :], ((512, DK ** -0.5),)),
            BLK_RV: (lambda i: vt[:, i, 0:512], ((512, 1.0),)),
            BLK_RV + 1: (lambda i: vt[:, i, 512:1024], ((512, 1.0),)),
            BLK_AQ: (lambda i: RBq[:, i, :], ((512, HD ** -0.5),)),
            BLK_AQK: (lambda i: RBq[:, i, :], ((256, HD ** -0.5), (256, 1.0))),
            BLK_AK: (lambda i: RBq[:, i, :], ((512, 1.0),)),
            BLK_AV: (lambda i: av[:, i, 0:512], ((512, 1.0),)),
            BLK_AV2: (lambda i: av[:, i, 512:768], ((256, 1.0),)),
        }

        def outputs_evac(c):
            filled(act, ("U", c, 1))
            for j in range(2):
                key = ("O", c, j)
                b = filled(act, key)
                nc.scalar.activation(vt[:, c, 512 * j:512 * j + 512], b[:, :], ACT.Copy).then_inc(bank_free[USES[key][0]], 1)
            for h in range(RH):
                if h % 2 == 0:
                    emptied(act, ("O", c, h // 2))
                if 5 * c + h:
                    act.wait_ge(on_sq, 5 * c + h)
                nc.scalar.activation(rjunk[:], vt[:, c, DV * h:DV * h + DV], ACT.Square,
                                     accum_out=ss_r[:, 4 * c + h:4 * c + h + 1]).then_inc(on_sq, 1)

        def sample_outputs_evac(h):
            filled(act, ("Us", h, 3))
            b = filled(act, ("Os", h))
            nc.scalar.activation(vs[0:TS, DV * h:DV * h + DV], b[0:TS, 0:DV], ACT.Copy).then_inc(bank_free[6], 1)
            emptied(act, ("Os", h))
            act.wait_ge(on_sq, 5 * h + 4)
            nc.scalar.activation(rjunk[0:TS], vs[0:TS, DV * h:DV * h + DV], ACT.Square,
                                 accum_out=ss_r[0:TS, 16 + h:17 + h]).then_inc(on_sq, 1)

        for bi in range(BLK_RG):
            first, n = BLOCKS[bi][:2]
            for s in range(n - 1):
                w_split(first + s + 2)
                if s == 1 and bi in (1, 2):
                    turn_evac(bi - 1)
                if s == 1 and bi in (5, 6, 7):
                    turn_evac(bi - 1)
                if s == 2 and 4 <= bi < 8:
                    outputs_evac(bi - 4)
            if bi in (BLK_AQ, BLK_AQK, BLK_AK):
                prev = {BLK_AQ: BLK_RQ, BLK_AQK: BLK_AQ, BLK_AK: BLK_AQK}[bi]
                filled(act, ("t", prev, 4))
            if bi == BLK_AQK:
                act.wait_ge(qs_out, 16)
            if bi == BLK_AK:
                act.wait_ge(qs_out, 32)
                act.wait_ge(k_out, 32)
            if bi == BLK_RV:
                act.wait_ge(cleared, 3)
            dst, scales = dests[bi]
            evac_block(bi, dst, BLOCKS[bi][3], scales)
            w_split(first + n + 1)
            if 4 <= bi < 8:
                sample_outputs_evac(bi - 4)
            if bi == BLK_AV2:
                act.wait_ge(on_sq, 20)
                nc.scalar.activation(rt_r[:], ss_r[:], ACT.Sqrt, scale=1.0 / DV, bias=eps[:, 0:1]).then_inc(rt_ready, 1)
        for g in range(2):
            bi = BLK_RG + g
            first, n = BLOCKS[bi][:2]
            for s in range(n - 1):
                w_split(first + s + 2)
                if g == 1 and s == 2:
                    for i in range(TILES):
                        split_evac(("r", 0, i), rTh, rTs, 0, i)
            tile_end(bi, 4)
            act.wait_ge(b_free[4], bi)
            if g:
                act.wait_ge(r_ready, 5)
            nc.scalar.activation(tmp_s[0:TS, :], P[4][32:64, :], ACT.Copy).then_inc(tmp_ready, 1)
            for j in range(TILES):
                if j == 0:
                    act.wait_ge(b_free[4], bi + 1)
                    dst, src = etmp[0:TS, 0, :], tmp_s[0:TS, :]
                else:
                    tile_end(bi, j - 1)
                    dst, src = etmp[:, j % 2, :], P[j - 1][:, :]
                if j >= 2:
                    act.wait_ge(r_ready, 5 * g + j - 1)
                nc.scalar.activation(dst, src, ACT.Tanh, scale=0.5).then_inc(e_ready, 1)
            w_split(first + n + 1)

        def turned_probs(s):
            nblk = len(attention_blocks(s // 4))
            for j in range(turns(s)):
                key = ("pt", s, j)
                b = filled(act, key)
                k = min(4, nblk - 4 * j)
                nc.scalar.activation(pT[:, 512 * j:512 * j + 128 * k], b[:, 0:128 * k], ACT.Copy
                                     ).then_inc(bank_free[USES[key][0]], 1)

        def attended_hi(pair):
            qb, hp = pair // 2, pair % 2
            b = filled(act, ("o", pair))
            nc.scalar.activation(aoh[:, hp, 128 * qb:128 * qb + 128], b[:, 0:128], ACT.Copy).then_inc(o_hi, 1)

        def exponentials(s):
            w = 128 * len(attention_blocks(s // 4))
            act.wait_ge(maxed, s + 1)
            nc.scalar.activation(sc[:, s % 2, 0:w], sc[:, s % 2, 0:w], ACT.Exp, bias=nm[:, s % 2:s % 2 + 1],
                                 accum_out=den[:, s % 2:s % 2 + 1]).then_inc(exped, 1)

        act.wait_ge(k_out, 16 * (NG + 2))
        for s in range(17):
            if s == 0:
                exponentials(0)
                for i in range(TILES):
                    split_evac(("r", 1, i), rTh, rTs, 4, i)
            else:
                turned_probs(s - 1)
            if s >= 2 and s % 2 == 0:
                attended_hi(s // 2 - 1)
            if s < 15:
                exponentials(s + 1)
            if s < 16:
                w_split(S_GB + s + 2)
                if s % 2 == 0:
                    n = s // 2
                    act.wait_ge(w_used, S_GB + s + 1)
                    if n:
                        act.wait_ge(a_free[1], n)
                    nc.scalar.activation(gexp[:, 0:HALF], P[0][:, 0:HALF], ACT.Tanh, scale=0.5)
                    nc.scalar.activation(gexp[:, HALF:NTOK], P[1][:, 0:HALF], ACT.Tanh, scale=0.5).then_inc(a_free[0], 1)
        def sample_exp():
            act.wait_ge(s_max, 1)
            nc.scalar.activation(srow[:], srow[:], ACT.Exp, bias=nm[:, 0:1], accum_out=den[:, 0:1]).then_inc(s_exp, 1)

        def sample_turned():
            act.wait_ge(pads_ready, 2)
            b = filled(act, ("sp",))
            q4 = b[:, 0:128].rearrange("p (q r) -> p q r", q=4)
            nc.scalar.activation(pad0[:].rearrange("p (q r) -> p q r", q=4)[:, :, 0:16], q4[:, :, 0:16], ACT.Copy)
            nc.scalar.activation(pad0[:].rearrange("p (q r) -> p q r", q=4)[:, :, 48:64], q4[:, :, 16:32], ACT.Copy)
            for g in range(2):
                src = b[:, 128 * (g + 1):128 * (g + 2)].rearrange("p (q j h) -> p q j h", q=4, j=8)
                dst = pad1[:, g, :].rearrange("p (q r) -> p q r", q=4)
                for j in range(8):
                    last = nc.scalar.activation(dst[:, :, 36 * j:36 * j + 4], src[:, :, j, :], ACT.Copy)
            last.then_inc(bank_free[6], 1)
            b = filled(act, ("spn",))
            nc.scalar.activation(pnew[0:TS].rearrange("p g n -> p (g n)"), b[0:TS, 0:384], ACT.Copy).then_inc(bank_free[4], 1)

        def sample_attended():
            b = filled(act, ("so",))
            src = b[0:HD, 0:128].rearrange("p (n h) -> p n h", h=4)
            for h in range(AH):
                last = nc.scalar.activation(aosf[64 * (h % 2):64 * (h % 2) + 64, h // 2, :], src[:, :, h], ACT.Copy)
            last.then_inc(bank_free[USES[("so",)][0]], 1)
            emptied(act, ("so",))
            nc.scalar.activation(aoh[:, :, SEQ:NTOK], aosf[:], ACT.Copy).then_inc(os_hi, 1)

        for n in range(KT):
            w_split(S_GA + n + 2)
            act.wait_ge(w_used, S_GA + n + 1)
            p = n % 2
            nc.scalar.activation(sga[:, n, 0:HALF], P[2 * p][:, 0:HALF], ACT.Tanh, scale=0.5)
            nc.scalar.activation(sga[:, n, HALF:NTOK], P[2 * p + 1][:, 0:HALF], ACT.Tanh, scale=0.5).then_inc(a_free[p], 1)
            if n in (0, 1, 6):
                {0: sample_exp, 1: sample_turned, 6: sample_attended}[n]()
        def mix_high(n):
            act.wait_ge(mix_sum, n + 1)
            nc.scalar.activation(mTh[:, n, :], mtmp[:, n % 3, :], ACT.Copy, scale=0.5)
            nc.scalar.activation(mTs[:, n, 0:32], mtmp[:, n % 3, SEQ:NTOK], ACT.Copy, scale=0.5).then_inc(mix_hi, 1)

        for n in range(KT):
            if n == 4:
                w_split(S_OUT)
            if n:
                mix_high(n - 1)
        w_split(S_OUT + 1)
        mix_high(KT - 1)
        first, n = BLOCKS[BLK_OUT][:2]
        for s in range(2 * n):
            if s == n - 1:
                evac_block(BLK_OUT, lambda i: xo[:, i, 0:512], 512, ((512, 1.0),), tmp_s2)
            if s == n:
                half_squares(BLK_OUT, xo, njunk, 0)
            if s == 2 * n - 1:
                tile_end(BLK_OUT + 1, 4)
                sample_lo(BLK_OUT + 1, tmp_s2, 512, ((512, 1.0),))
            if s < 2 * n - 1:
                w_split(first + s + 2)
        roots(BLK_OUT + 1, xo, njunk, 0, n_sq, n_rt)
        for j in range(2):
            act.sem_inc(u_evac[j], 1)
        for i in range(TILES + 1):
            if i < TILES:
                r = rows(i)
                act.wait_ge(x2_ready, i + 1)
                nc.scalar.activation(njunk[0:r], xo[0:r, i, :], ACT.Square, accum_out=ss_n[0:r, 5 + i:6 + i]).then_inc(n_sq, 1)
                act.wait_ge(n_sq, TILES + i + 1)
                nc.scalar.activation(rt_n[0:r, 5 + i:6 + i], ss_n[0:r, 5 + i:6 + i], ACT.Sqrt, scale=1.0 / D,
                                     bias=eps[0:r, 0:1]).then_inc(n_rt, 1)
            if i:
                for half in range(2):
                    split_evac(("h2", i - 1, half), T1h, T1s, 4 * half, i - 1)
            if i == TILES - 1:
                w_split(S_UP + 1)
        def columns(at, n, j):
            q, t1 = n % 2, 2 * n + j + 1
            act.wait_ge(w_used, at * 2 + (S_UP + t1))
            act.wait_ge(conv_done, at * 2 + t1)
            act.wait_ge(tail_done, at * 2 + t1)
            nc.scalar.activation(ub[:, q, j, 2:2 + HALF], P[2 * j][:, 0:HALF], ACT.Copy)
            nc.scalar.activation(ub[:, q, j, 2 + HALF:2 + SEQ], P[2 * j + 1][:, 0:SEQ - HALF], ACT.Copy)
            u_s = ub[:, q, j, 2 + SEQ:].rearrange("p (b t) -> p b t", t=6)
            nc.scalar.activation(u_s[:, :, 2:6], P[2 * j + 1][:, SEQ - HALF:HALF].rearrange("p (b t) -> p b t", t=4),
                                 ACT.Copy).then_inc(u_evac[j], 1)

        def up_split(at, n, j):
            act.wait_ge(w_raw[j], at * 16 + 16 * ((S_UP + 2 * n + 2 + j) // 2 + 1))
            nc.scalar.activation(whi[:, j, :], wraw[:, j, :], ACT.Copy).then_inc(w_hi, 1)

        def gelu(at, n):
            act.wait_ge(conv_done, at * 2 + (2 * n + 5))
            nc.scalar.activation(cb[:, 0, 0:CW], cb[:, 0, 0:CW], ACT.Gelu_apprx_tanh).then_inc(gelu_done, 1)

        def product_hi(at, n):
            act.wait_ge(f_done, at + (n + 1))
            samp = c_sample(cb[:, 0, :])
            at_f, at_s = (at + n) * NTOK, (at + n) * 64
            place = (lambda x, w: bass.ds(x, w)) if not isinstance(at, int) else (lambda x, w: slice(x, x + w))
            nc.scalar.activation(fTh[:, place(at_f, SEQ)], cb[:, 0, 0:SEQ], ACT.Copy)
            nc.scalar.activation(fTh[:, place(at_f + SEQ, TS)].rearrange("p (b t) -> p b t", t=4), samp, ACT.Copy)
            nc.scalar.activation(fTs[:, place(at_s, TS)].rearrange("p (b t) -> p b t", t=4), samp, ACT.Copy
                                 ).then_inc(f_hi, 1)

        def pair_round(at, n):
            gelu(at, n)
            columns(at, n + 1, 0)
            product_hi(at, n)
            up_split(at, n + 1, 0)
            columns(at, n + 1, 1)
            up_split(at, n + 1, 1)

        for j in range(2):
            columns(0, 0, j)
            up_split(0, 0, j)
        with act.Fori(0, up_loop - 1) as it:
            for q in range(2):
                pair_round(it * 2, q)
        pair_round(0, FT - 2)
        gelu(0, FT - 1)
        product_hi(0, FT - 1)
        first, n = BLOCKS[BLK_DN][:2]
        for s in range(2 * n):
            if s == n - 1:
                evac_block(BLK_DN, lambda i: fo[:, i, 0:512], 512, ((512, 1.0),), tmp_s3)
            if s == n:
                half_squares(BLK_DN, fo, fjunk, TILES)
            if s == 2 * n - 1:
                tile_end(BLK_DN + 1, 4)
                sample_lo(BLK_DN + 1, tmp_s3, 512, ((512, 1.0),))
            if first + s + 2 < NSLOT:
                w_split(first + s + 2)
        roots(BLK_DN + 1, fo, fjunk, 10, y_sq, y_rt)

    @block.tensor
    def _(pe):
        mm = nc.tensor.matmul

        def open_bank(key):
            bank, n = USES[key]
            if n:
                pe.wait_ge(bank_free[bank], n)
            return P[bank], bank_full[bank]

        def turn(key, srcs, n, m=128):
            b, full = open_bank(key)
            for k, src in enumerate(srcs):
                last = nc.tensor.transpose(b[0:m, k * n:(k + 1) * n], src, ident[0:n, 0:n])
            last.then_inc(full, 1)

        def b_block(bi, Th, Tl, Ts, between=None, ready=None, operand=None, tail=1):
            first, n, per, w = BLOCKS[bi]

            def part(i, k, slot, Wh, Wl):
                st, sp_ = k == 0, k == n * per - 1
                if k == 0:
                    if ready:
                        ready(i)
                    if bi:
                        pe.wait_ge(b_free[i], bi)
                if i == 4:
                    mm(P[4][0:64, 0:w], Ts(k), Wh, start=st, stop=False)
                    return mm(P[4][0:64, 0:w], Ts(k), Wl, start=False, stop=sp_)
                xh, xl = Th(k, cols(i)), Tl(k, cols(i))
                mm(P[i][:, 0:w], xh, Wh, start=st, stop=False)
                mm(P[i][:, 0:w], xh, Wl, start=False, stop=False)
                return mm(P[i][:, 0:w], xl, Wh, start=False, stop=sp_)

            W = []
            for s in range(n):
                slot = first + s
                pe.wait_ge(w_lo, slot + 1)
                if operand:
                    operand(s * per + per - 1)
                W += [(s * per + kk, slot, whi[:, slot % 2, kk * w:(kk + 1) * w], wlo[:, slot % 2, kk * w:(kk + 1) * w])
                      for kk in range(per)]
                if tail == 2 and s == n - 2:
                    continue
                if s == 0 and ready:
                    for i in range(TILES):
                        for k in W:
                            last = part(i, *k)
                elif s < n - 1:
                    for k in W:
                        for i in range(TILES):
                            last = part(i, *k)
                else:
                    for i in (4, 0, 1, 2, 3):
                        for k in W:
                            last = part(i, *k)
                        if i != 3:
                            last.then_inc(b_full, 1)
                last.then_inc(w_used, tail if s == n - 1 else 1)
                W = []
                if between:
                    between(s)

        def a_tile(slot, Th, Tl, kt, banks, mid=None, w0=0):
            for half in range(2):
                if half and mid:
                    mid()
                dst = P[banks + half][:, 0:HALF]
                c = slice(HALF * half, HALF * half + HALF)
                for k in range(kt):
                    cut = slice(w0 + 128 * k, w0 + 128 * k + 128)
                    Wh, Wl = whi[:, slot % 2, cut], wlo[:, slot % 2, cut]
                    mm(dst, Wh, Th[:, k, c], start=k == 0, stop=False)
                    mm(dst, Wh, Tl[:, k, c], start=False, stop=False)
                    last = mm(dst, Wl, Th[:, k, c], start=False, stop=k == kt - 1)
            return last

        pe.wait_ge(ident_in, 16)

        def turn_wide(key, src, i):
            for half in range(2):
                turn((key, i, half), [src[0:rows(i), i % 2, 128 * k:128 * k + 128] for k in range(4 * half, 4 * half + 4)],
                     rows(i))

        def turn_input(i):
            pe.wait_ge(x_norm, i + 1)
            turn_wide("x", xn, i)

        T1 = (lambda k, c: T1h[:, k, c], lambda k, c: T1l[:, k, c], lambda k: T1s[:, k, :])

        def turn_block(bi):
            src = RBk if bi == BLK_RK else RBq
            for i in range(TILES):
                pe.wait_ge(rope_done, 5 * ROPE_BLOCKS.index(bi) + i + 1)
                turn(("t", bi, i), [src[0:rows(i), i, 128 * k:128 * k + 128] for k in range(4)], rows(i))

        def scores(c):
            emptied(pe, ("t", BLK_RK, 4))
            emptied(pe, ("t", BLK_RK, 3))
            emptied(pe, ("t", BLK_RK, 2))
            b, full = open_bank(("S", c))
            for h in range(RH):
                last = mm(b[:, 128 * h:128 * h + 128], kT[:, h, cols(c)], qT[:, h, cols(c)], start=True, stop=True)
            last.then_inc(full, 1)
            if c == 0:
                b, full = open_bank(("Ss",))
                for h in range(RH):
                    last = mm(b[0:TS, 32 * h:32 * h + 32], kT[:, h, SEQ:NTOK], qT[:, h, SEQ:NTOK], start=True, stop=True)
                last.then_inc(full, 1)

        def outputs(c):
            emptied(pe, ("S", c))
            if c:
                pe.wait_ge(qd_ready, c)
                emptied(pe, ("U", c - 1, 1))
            for j in range(2):
                b, full = open_bank(("O", c, j))
                for e in range(2):
                    h = 2 * j + e
                    dst = b[:, DV * e:DV * e + DV]
                    last = mm(dst, PT[:, h, :], vt[:, c, DV * h:DV * h + DV], start=True, stop=c == 0)
                    if c:
                        last = mm(dst, qd[:, h, :], state[:, h, :], start=False, stop=True)
                last.then_inc(full, 1)

        def updates(c, j):
            pe.wait_ge(kd_ready, c + 1)
            b, full = open_bank(("U", c, j))
            for e in range(2):
                h = 2 * j + e
                last = mm(b[:, DV * e:DV * e + DV], kd[:, 128 * h:128 * h + 128], vt[:, c, DV * h:DV * h + DV],
                          start=True, stop=True)
            last.then_inc(full, 1)

        def retention_part(c, s):
            if s == 0:
                scores(c)
            elif s == 1:
                if c:
                    turn_block(BLK_AQ + c - 1)
                outputs(c)
                updates(c, 0)
            elif s == 2:
                updates(c, 1)
            else:
                sample_head(c)

        def sample_head(h):
            emptied(pe, ("Ss",))
            ob, ofull = open_bank(("Os", h))
            mm(ob[0:TS, 0:DV], PTs[0:TS, h, :], vs[0:TS, DV * h:DV * h + DV], start=True, stop=False)
            pe.wait_ge(qm_ready, h + 1)
            pe.wait_ge(km_ready, h + 1)
            for p in range(4):
                pe.wait_ge(s0_in[p], 16 * (h + 1))
                for e in range(2):
                    last = mm(ob[0:TS, 0:DV], qm[:, h % 2, 2 * p + e, :], S0[:, p, e, :], start=False,
                              stop=p == 3 and e == 1)
                if p == 3:
                    last.then_inc(ofull, 1)
                b, full = open_bank(("Us", h, p))
                for e in range(2):
                    last = mm(b[:, DV * e:DV * e + DV], km[:, 2 * p + e, :], vs[:, DV * h:DV * h + DV], start=True, stop=True)
                last.then_inc(full, 1)

        turn_input(0)
        turn_input(1)

        def x_ready(i):
            if 1 <= i < 4:
                turn_input(i + 1)
            for half in range(2):
                emptied(pe, ("x", i, half))

        for bi in range(BLK_RG):
            def between(s, bi=bi):
                if bi in (1, 2) and s == 1:
                    turn_block(bi - 1)
                if 4 <= bi < 8:
                    retention_part(bi - 4, s)
            b_block(bi, *T1, between=between, ready=x_ready if bi == 0 else None)

        def turn_gated(g):
            for i in range(TILES):
                pe.wait_ge(r_ready, 5 * g + (i + 2 if i < 4 else 1))
                r = rows(i)
                src = vt[:, i, :] if i < 4 else vs[0:TS, :]
                turn(("r", g, i), [src[:, 128 * (4 * g + k):128 * (4 * g + k) + 128] for k in range(4)], r)

        b_block(BLK_RG, *T1)
        b_block(BLK_RG + 1, *T1, between=lambda s: turn_gated(0) if s == 2 else None)

        def att_scores(s):
            qb, h = s // 4, s % 4
            pe.wait_ge(q_padded, s + 1)
            for g in range(NG):
                gg = (1, 2, 0)[g]
                b, full = open_bank(("s", s, g))
                lo, hi = (0 if gg else 128 * max(qb - 1, 0)), 128 * (qb + 1)
                mm(b[:, 0:hi - lo], qpad[:, h % 2, gg, :], akT[:, 2 * gg + h // 2, lo:hi], start=True, stop=True
                   ).then_inc(full, 1)

        def att_turn(s):
            nblk = len(attention_blocks(s // 4))
            pe.wait_ge(probs, s + 1)
            for j in range(turns(s)):
                ks = range(4 * j, min(4 * j + 4, nblk))
                turn(("pt", s, j), [sc[:, s % 2, 128 * k:128 * k + 128] for k in ks], 128)

        def att_values(s):
            qb, h = s // 4, s % 4
            par = h % 2
            key = ("o", s // 2)
            if par == 0:
                b, full = open_bank(key)
            else:
                b, full = P[7], bank_full[7]
            blocks = attention_blocks(qb)
            for n, (g, kb) in enumerate(blocks):
                if n % 4 == 0:
                    emptied(pe, ("pt", s, n // 4))
                last = mm(b[64 * par:64 * par + 64, 0:128], av[:, kb, 256 * g + 64 * h:256 * g + 64 * h + 64],
                          pT[:, 128 * n:128 * n + 128], start=n == 0, stop=n == len(blocks) - 1)
            if par:
                last.then_inc(full, 1)

        for i in range(TILES):
            pe.wait_ge(b_free[i], BLK_AV2 + 1)
        for i in range(4, -1, -1):
            emptied(pe, ("t", BLK_AK, i))
        for s in range(16):
            slot, n = S_GB + s, s // 2
            if s >= 2:
                att_turn(s - 1)

            def middle(s=s):
                if s < 2:
                    pe.wait_ge(b_free[2 * s + 1], BLK_RG + 2)
                if s == 1:
                    for i in (3, 4):
                        emptied(pe, ("r", 1, i))
                    att_turn(0)
                if s >= 2:
                    att_values(s - 1)
                    if s < 15:
                        att_scores(s + 1)

            if s < 2:
                pe.wait_ge(b_free[2 * s], BLK_RG + 2)
            if s == 1:
                for i in (0, 1, 2):
                    emptied(pe, ("r", 1, i))
            pe.wait_ge(w_lo, slot + 1)
            if n:
                pe.wait_ge(a_free[s % 2], n)
            if s % 2 == 0:
                a_tile(slot, T1h, T1l, KT, 0, middle).then_inc(w_used, 1)
            else:
                a_tile(slot, rTh, rTl, KT, 2, middle).then_inc(w_used, 1)
            if s == 0:
                pe.wait_ge(b_free[4], BLK_RG + 2)
                att_scores(0)
                turn_gated(1)
                att_scores(1)
            elif s == 1:
                att_values(0)
                att_scores(2)
        att_turn(15)
        att_values(15)
        def sample_scores():
            pe.wait_ge(s_step, 48)
            turn(("st",), [sTk[:, g, :] for g in range(NG)], 128)
            pe.wait_ge(qbd_ready, 1)
            b, full = open_bank(("sn",))
            for g in range(NG):
                for hp in range(2):
                    last = mm(b[:, 32 * g:32 * g + 32], qbd[:, g, hp, :], akT[:, 2 * g + hp, SEQ:NTOK], start=hp == 0, stop=hp == 1)
            last.then_inc(full, 1)

        def sample_turn():
            pe.wait_ge(s_probs, 1)
            turn(("sp",), [srow[:, g, 0:128] for g in range(NG)], 128)
            turn(("spn",), [srow[:, g, 128:160] for g in range(NG)], 128, 32)

        def sample_values(batches):
            if 0 in batches:
                emptied(pe, ("sp",))
                emptied(pe, ("spn",))
                open_bank(("sv",))
            b, full = P[7], bank_full[7]
            for bb in batches:
                q = bb // 2
                dst = b[32 * q:32 * q + 32, 0:256]
                for g in range(NG):
                    n = NG * bb + g
                    pe.wait_ge(kv_in[n % 9], 16 * (n // 9 + 1))
                    place = kvv[n % 9 // 3][:, n % 3]
                    if g == 0:
                        last = mm(dst, pad0[:, 32 * bb:32 * bb + 32], place[:, 0, :], start=bb % 2 == 0, stop=False)
                    else:
                        for t in range(DT):
                            last = mm(dst, pad1[:, g - 1, 32 * (4 * bb + t):32 * (4 * bb + t) + 32], place[:, t, :],
                                      start=False, stop=False)
                    last.then_inc(v_used, 1)
                if bb % 2 == 1:
                    for g in range(NG):
                        last = mm(dst, pnew[0:TS, g, 32 * q:32 * q + 32], avs[0:TS, 256 * g:256 * g + 256], start=False,
                                  stop=g == 2)
                if bb == NB - 1:
                    last.then_inc(full, 1)

        for n in range(KT):
            pe.wait_ge(w_lo, S_GA + n + 1)
            pe.wait_ge(a_free[n % 2], 8 + n // 2)
            a_tile(S_GA + n, T1h, T1l, KT, 2 * (n % 2)).then_inc(w_used, 1)
            if n == 0:
                sample_scores()
            elif n == 1:
                sample_turn()
            elif n < 6:
                sample_values(((0,), (1, 2), (3, 4, 5), (6, 7))[n - 2])
            elif n == 6:
                pe.wait_ge(o_row, 1)
                turn(("so",), [orow[:, :]], 128, HD)
        pe.wait_ge(os_lo, 1)
        for n in range(KT):
            pe.wait_ge(w_lo, S_BA + n // 4 + 1)
            pe.wait_ge(a_free[n % 2], 12 + n // 2)
            a_tile(S_BA + n // 4, aoh, aol, 2, 2 * (n % 2), w0=BA_W * (n % 4)
                   ).then_inc(w_used if n % 4 == 3 else branch_done, 1)
        pe.wait_ge(a_free[0], 16)
        pe.wait_ge(a_free[1], 16)
        for nb in range(2):
            b_block(BLK_OUT + nb, lambda k, c: mTh[:, k, c], lambda k, c: mTl[:, k, c], lambda k: mTs[:, k, :],
                    operand=None if nb else lambda k: pe.wait_ge(mix_lo, k + 1))
        def turn_hidden(i):
            pe.wait_ge(h_ready, i + 1)
            turn_wide("h2", hn, i)

        for i in range(TILES):
            turn_hidden(i)
        def rest_ready():
            for i in (3, 4):
                for half in range(2):
                    emptied(pe, ("h2", i, half))

        for i in range(TILES):
            pe.wait_ge(b_free[i], BLK_OUT + 2)
        for i in range(3):
            for half in range(2):
                emptied(pe, ("h2", i, half))
        def up_round(it):
            for q in range(2):
                for j in range(2):
                    pe.wait_ge(w_lo, it * 4 + (S_UP + 2 * q + j + 1))
                    pe.wait_ge(u_evac[j], it * 2 + (q + 1))
                    a_tile(j, T1h, T1l, KT, 2 * j, rest_ready if q == j == 0 else None).then_inc(w_used, 1)

        with pe.Fori(0, up_loop) as it:
            up_round(it)
        pe.wait_ge(u_evac[0], FT + 1)
        pe.wait_ge(u_evac[1], FT + 1)
        pe.wait_ge(tail_done, 2 * FT + 4)
        tile = lambda t: t[:].rearrange("p (k n) -> p k n", k=FT)
        fh, fl, fs = tile(fTh), tile(fTl), tile(fTs)

        def conv_tail(s):
            if s < 11:
                turn18(s)

        def turn18(j):
            b, full = open_bank(("cv", j))
            for k in range(4):
                last = nc.tensor.transpose(b[0:18, 128 * k:128 * k + 128], cvt[:, 18 * (4 * j + k):18 * (4 * j + k) + 18], ident)
            last.then_inc(full, 1)

        b_block(BLK_DN, lambda k, c: fh[:, k, c], lambda k, c: fl[:, k, c], lambda k: fs[:, k, :], between=conv_tail,
                operand=lambda k: pe.wait_ge(f_lo, k + 2))
        b_block(BLK_DN + 1, lambda k, c: fh[:, k, c], lambda k, c: fl[:, k, c], lambda k: fs[:, k, :], tail=2)

    @block.vector
    def _(dve):
        v = nc.vector
        steps = [0]

        def step(ins):
            steps[0] += 1
            ins.then_inc(dve_step, 1)
            dve.wait_ge(dve_step, steps[0])

        def w_split(s):
            dve.wait_ge(w_hi, s + 1)
            v.tensor_tensor(wlo[:, s % 2, :], wraw[:, s % 2, :], whi[:, s % 2, :].bitcast(F), ALU.subtract
                            ).then_inc(w_lo, 1)

        def split_evac(key, Th, Tl, Ts, k0, i):
            b = filled(dve, key)
            n = rows(i)
            dve.wait_ge(split_hi, SPLIT_NO[key] + 1)
            src = b[:, 0:4 * n].rearrange("p (k n) -> p k n", k=4)
            hi = Th[:, k0:k0 + 4, cols(i)].bitcast(F)
            ins = v.tensor_tensor(Tl[:, k0:k0 + 4, cols(i)], src, hi, ALU.subtract)
            if i == 4:
                ins = v.tensor_tensor(Ts[:, k0:k0 + 4, 32:64], src, hi, ALU.subtract)
            ins.then_inc(bank_free[USES[key][0]], 1)

        def norm_scale(out, x, root, rs, gain):
            step(v.reciprocal(rs, root))
            return v.scalar_tensor_tensor(out, x, rs, gain, ALU.mult, ALU.mult)

        def sample_sum(bi, dst, scales, tmp=tmp_s):
            dve.wait_ge(b_full, 4 * bi + 1)
            dve.wait_ge(tmp_ready, bi + 1)
            at_ = 0
            for w, scale in scales:
                ins = v.scalar_tensor_tensor(dst[:, at_:at_ + w], P[4][0:TS, at_:at_ + w], scale, tmp[0:TS, at_:at_ + w],
                                             ALU.mult, ALU.add)
                at_ += w
            ins.then_inc(b_free[4], 1)

        rope_tiles = [0]

        def rope(bi):
            buf = RBk if bi == BLK_RK else RBq
            for i in range(TILES):
                r = rows(i)
                dve.wait_ge(b_free[i], bi + 1)
                if rope_tiles[0]:
                    dve.wait_ge(rope_done, rope_tiles[0])
                rope_tiles[0] += 1
                if bi in (BLK_RQ, BLK_RK):
                    x = buf[0:r, i, :].rearrange("p (h s d) -> p h s d", h=RH, s=2)
                    tn = ropet[0:r, 1, :].rearrange("p (h s d) -> p h s d", h=RH, s=2)
                    cos = crv("rcos", TILES)[0:r, i, :].unsqueeze(1).broadcast_to([r, 8, 64])
                    sin = crv("rsin", TILES)[0:r, i, :].rearrange("p (s d) -> p s d", s=2)
                    v.tensor_tensor(ropet[0:r, 0, :].rearrange("p (k d) -> p k d", k=8),
                                    buf[0:r, i, :].rearrange("p (k d) -> p k d", k=8), cos, ALU.mult)
                    for side in range(2):
                        last = v.tensor_tensor(tn[:, :, side, :], x[:, :, 1 - side, :],
                                               sin[:, side, :].unsqueeze(1).broadcast_to([r, RH, 64]), ALU.mult)
                    step(last)
                    v.tensor_tensor(buf[0:r, i, :], ropet[0:r, 0, :], ropet[0:r, 1, :], ALU.add).then_inc(rope_done, 1)
                else:
                    x = buf[0:r, i, :].rearrange("p (h d) -> p h d", h=8)[:, :, 0:16]
                    tc = ropet[0:r, 0, 0:128].rearrange("p (h d) -> p h d", h=8)
                    tn = ropet[0:r, 1, 0:128].rearrange("p (h d) -> p h d", h=8)
                    cos = cav("acos", TILES)[0:r, i, :].unsqueeze(1).broadcast_to([r, 8, 16])
                    sin = cav("asin", TILES)[0:r, i, :]
                    v.tensor_tensor(tc, x, cos, ALU.mult)
                    for side in range(2):
                        last = v.tensor_tensor(tn[:, :, 8 * side:8 * side + 8], x[:, :, 8 - 8 * side:16 - 8 * side],
                                               sin[:, 8 * side:8 * side + 8].unsqueeze(1).broadcast_to([r, 8, 8]), ALU.mult)
                    step(last)
                    v.tensor_tensor(x, tc, tn, ALU.add).then_inc(rope_done, 1)

        dve.wait_ge(gpre_in, 16)
        for i in range(TILES + 2):
            if i < TILES:
                r = rows(i)
                dve.wait_ge(x_rt, i + 1)
                if i >= 2:
                    filled(dve, ("x", i - 2, 1))
                norm_scale(xn[0:r, i % 2, :], xin[0:r, i, :], rt_x[0:r, i:i + 1], rs_x[0:r, i:i + 1], gpre[0:r]).then_inc(x_norm, 1)
            if i >= 2:
                for half in range(2):
                    split_evac(("x", i - 2, half), T1h, T1l, T1s, 4 * half, i - 2)
        dve.wait_ge(w_lo, 2)
        dve.wait_ge(ca_in, 16)
        dve.wait_ge(cr_in, 16)
        dve.wait_ge(cleared, 4)

        sample_dst = {
            BLK_RQ: (RBq[0:TS, 4, :], ((512, 1.0),)), BLK_RK: (RBk[0:TS, 4, :], ((512, DK ** -0.5),)),
            BLK_RV: (vs[0:TS, 0:512], ((512, 1.0),)), BLK_RV + 1: (vs[0:TS, 512:1024], ((512, 1.0),)),
            BLK_AQ: (RBq[0:TS, 4, :], ((512, HD ** -0.5),)), BLK_AQK: (RBq[0:TS, 4, :], ((256, HD ** -0.5), (256, 1.0))),
            BLK_AK: (RBq[0:TS, 4, :], ((512, 1.0),)), BLK_AV: (avs[0:TS, 0:512], ((512, 1.0),)),
            BLK_AV2: (avs[0:TS, 512:768], ((256, 1.0),)),
        }

        def decayed(c):
            key = ("S", c)
            b = filled(dve, key)
            if c:
                filled(dve, ("O", c - 1, 1))
                v.tensor_tensor(qd[:], qT[:, :, cols(c)], crv("qdec", RH), ALU.mult).then_inc(qd_ready, 1)
            v.tensor_tensor(PT[:], b[:, :].rearrange("p (h n) -> p h n", h=RH), crv("decT", RH), ALU.mult
                            ).then_inc(bank_free[USES[key][0]], 1)
            if c == 0:
                b = filled(dve, ("Ss",))
                v.tensor_tensor(PTs[0:TS], b[0:TS, 0:128].rearrange("p (h n) -> p h n", h=RH), crv("decTs", RH)[0:TS], ALU.mult
                                ).then_inc(bank_free[USES[("Ss",)][0]], 1)
                sample_queries(0)
                sample_queries(1)

        def state_update(c, j):
            key = ("U", c, j)
            b = filled(dve, key)
            for e in range(2):
                h = 2 * j + e
                src = b[:, DV * e:DV * e + DV]
                if c == 0:
                    ins = v.tensor_copy(state[:, h, :], src)
                else:
                    ins = v.scalar_tensor_tensor(state[:, h, :], state[:, h, :], GAMMA_CHUNK[h], src, ALU.mult, ALU.add)
            ins.then_inc(bank_free[USES[key][0]], 1)

        def sample_queries(h):
            if h >= 2:
                filled(dve, ("Os", h - 2))
            dst = bass.AP(qm, (h % 2) * 256, [[512, 128], [36, NB], [1, DT]])
            v.tensor_tensor(dst, qT[:, h, SEQ:NTOK].rearrange("p (b t) -> p b t", t=DT),
                            crv("qdecs", RH)[:, h, :].rearrange("p (b t) -> p b t", t=DT), ALU.mult).then_inc(qm_ready, 1)

        def new_sample_states(h):
            for p in range(4):
                key = ("Us", h, p)
                b = filled(dve, key)
                v.scalar_tensor_tensor(S0[:, p], S0[:, p], GAMMA_STEP[h], b[:, :].rearrange("p (e n) -> p e n", e=2),
                                       ALU.mult, ALU.add).then_inc(bank_free[USES[key][0]], 1)
            if h + 2 < RH:
                sample_queries(h + 2)

        for bi in range(BLK_RG):
            first, n = BLOCKS[bi][:2]
            for s in range(n - 1):
                w_split(first + s + 2)
                if 4 <= bi < 8:
                    if s == 0:
                        decayed(bi - 4)
                    else:
                        state_update(bi - 4, s - 1)
            dst, scales = sample_dst[bi]
            if bi == BLK_AQ:
                filled(dve, ("t", BLK_RQ, 4))
            if bi == BLK_AQK:
                filled(dve, ("t", BLK_AQ, 4))
                dve.wait_ge(qs_out, 16)
            if bi == BLK_AK:
                filled(dve, ("t", BLK_AQK, 4))
                dve.wait_ge(qs_out, 32)
                dve.wait_ge(k_out, 32)
            sample_sum(bi, dst, scales)
            w_split(first + n + 1)
            if 4 <= bi < 8:
                new_sample_states(bi - 4)
            if bi in ROPE_BLOCKS:
                rope(bi)
            if bi == BLK_AV2:
                dve.wait_ge(rt_ready, 1)
                step(v.reciprocal(rs_r[:], rt_r[:]))
                step(v.tensor_scalar(rs_r[:], rs_r[:], 0.5, None, ALU.mult))

        def gate_tile(g, j):
            dve.wait_ge(e_ready, 5 * g + j + 1)
            if j:
                i = j - 1
                t, out, r = etmp[:, j % 2, :], vt[:, i, :], 128
                v.scalar_tensor_tensor(t, t, 1.0, P[i][:, :], ALU.add, ALU.mult).then_inc(b_free[i], 1)
                dve.wait_ge(b_free[i], BLK_RG + g + 1)
            else:
                i = 4
                t, out, r = etmp[0:TS, 0, :], vs[0:TS, :], TS
                step(v.scalar_tensor_tensor(t, t, 1.0, tmp_s[0:TS, :], ALU.add, ALU.mult))
            for hh in range(2):
                h = 2 * g + hh
                o_ = out[:, DV * h:DV * h + DV]
                last = v.scalar_tensor_tensor(o_, o_, rs_r[0:r, 4 * i + h:4 * i + h + 1], t[:, DV * hh:DV * hh + DV],
                                              ALU.mult, ALU.mult)
            last.then_inc(r_ready, 1)

        for g in range(2):
            bi = BLK_RG + g
            first, n = BLOCKS[bi][:2]
            for s in range(n - 1):
                w_split(first + s + 2)
                if g == 1 and s == 2:
                    for i in range(TILES):
                        split_evac(("r", 0, i), rTh, rTl, rTs, 0, i)
            dve.wait_ge(tmp_ready, bi + 1)
            v.tensor_tensor(tmp_s[0:TS, :], P[4][0:TS, :], tmp_s[0:TS, :], ALU.add).then_inc(b_free[4], 1)
            dve.wait_ge(b_free[4], bi + 1)
            for j in range(TILES):
                gate_tile(g, j)
            w_split(first + n + 1)

        masks = {1: cav("mask1"), 2: cav("mask2"), 0: cav("mask0")}

        def score_max(s):
            qb = s // 4
            at_ = 0
            for g in range(NG):
                gg = (1, 2, 0)[g]
                key = ("s", s, g)
                b = filled(dve, key)
                w = 128 * (qb + 1) if gg else 128 * min(qb + 1, 2)
                m = masks[gg]
                full_w = 512 if gg else 256
                last = v.tensor_tensor_reduce(out=sc[:, s % 2, at_:at_ + w], in0=b[:, 0:w], in1=m[:, full_w - w:full_w],
                                              scale=1.0, scalar=NEG, op0=ALU.add, op1=ALU.max,
                                              accum_out=mx[:, s % 2, g:g + 1])
                last.then_inc(bank_free[USES[key][0]], 1)
                at_ += w
            emptied(dve, ("s", s, 0))
            emptied(dve, ("s", s, 1))
            emptied(dve, ("s", s, 2))
            step(v.tensor_reduce(rden[:, s % 2:s % 2 + 1], mx[:, s % 2, 0:3], AX.X, ALU.max))
            v.tensor_scalar(nm[:, s % 2:s % 2 + 1], rden[:, s % 2:s % 2 + 1], -1.0, None, ALU.mult).then_inc(maxed, 1)

        def normalise(s):
            w = 128 * len(attention_blocks(s // 4))
            dve.wait_ge(exped, s + 1)
            step(v.reciprocal(rden[:, s % 2:s % 2 + 1], den[:, s % 2:s % 2 + 1]))
            v.tensor_scalar(sc[:, s % 2, 0:w], sc[:, s % 2, 0:w], rden[:, s % 2:s % 2 + 1], None, ALU.mult
                            ).then_inc(probs, 1)

        def gated(n, gate, src, out, frees):
            for half in range(2):
                c = slice(HALF * half, HALF * half + HALF)
                last = v.scalar_tensor_tensor(out[:, c], gate[:, c], 1.0, P[src + half][:, 0:HALF], ALU.add, ALU.mult)
            last.then_inc(frees, 1)

        def attended_lo(pair):
            qb, hp = pair // 2, pair % 2
            b = filled(dve, ("o", pair))
            dve.wait_ge(o_hi, pair + 1)
            c = slice(128 * qb, 128 * qb + 128)
            v.tensor_tensor(aol[:, hp, c], b[:, 0:128], aoh[:, hp, c].bitcast(F), ALU.subtract).then_inc(bank_free[7], 1)

        def sample_piece(n):
            b, g, t = n // 6, n // 2 % NG, 2 * (n % 2)
            dve.wait_ge(kk_in[n % 3], 16 * (n // 3 + 1))
            dve.wait_ge(q_in[n % 3], 16 * (n // 3 + 1))
            if n:
                dve.wait_ge(s_step, n)
            keys = kvk[:, n % 3, 0, :].unsqueeze(1).broadcast_to([128, 2, 256]) if g == 0 else kvk[:, n % 3]
            step(v.tensor_tensor(prod[:].rearrange("p (t n) -> p t n", t=2), keys, qbc[n % 3][:], ALU.mult))
            v.tensor_reduce(sTk[:, g, 16 * b + 4 * t:16 * b + 4 * t + 8], prod[:].rearrange("p (k d) -> p k d", d=HD), AX.X,
                            ALU.add).then_inc(s_step, 1)

        for s in range(17):
            if s == 0:
                score_max(0)
                for i in range(TILES):
                    split_evac(("r", 1, i), rTh, rTl, rTs, 4, i)
                normalise(0)
            if s < 15:
                if s:
                    sample_piece(3 * s)
                    filled(dve, ("pt", s - 1, turns(s - 1) - 1))
                score_max(s + 1)
                if s:
                    sample_piece(3 * s + 1)
                normalise(s + 1)
                if s == 0:
                    sample_piece(0)
                    sample_piece(1)
            if s >= 2 and s % 2 == 0:
                attended_lo(s // 2 - 1)
            if s < 16:
                w_split(S_GB + s + 2)
                if s % 2:
                    n = s // 2
                    dve.wait_ge(w_used, S_GB + s + 1)
                    dve.wait_ge(a_free[0], n + 1)
                    gated(n, gexp[:], 2, mixr[:, n, :], a_free[1])
                for n in range(3 * s + 2 if s < 15 else 45, 3 * s + 3):
                    sample_piece(n)

        def sample_softmax():
            b = filled(dve, ("st",))
            v.tensor_tensor(srow[:, 0, 0:128], b[:, 0:128], cav("ms0"), ALU.add)
            v.tensor_copy(srow[:, 1:3, 0:128], b[:, 128:384].rearrange("p (g n) -> p g n", g=2)).then_inc(bank_free[4], 1)
            b = filled(dve, ("sn",))
            v.tensor_tensor(srow[:, :, 128:160], b[:, 0:96].rearrange("p (g n) -> p g n", g=NG), cav("mnew", NG), ALU.add
                            ).then_inc(bank_free[5], 1)
            emptied(dve, ("sn",))
            step(v.tensor_reduce(rden[:, 0:1], srow[:], AX.XY, ALU.max))
            v.tensor_scalar(nm[:, 0:1], rden[:, 0:1], -1.0, None, ALU.mult).then_inc(s_max, 1)
            dve.wait_ge(s_exp, 1)
            step(v.reciprocal(rden[:, 1:2], den[:, 0:1]))
            v.tensor_scalar(srow[:], srow[:], rden[:, 1:2], None, ALU.mult).then_inc(s_probs, 1)

        def sample_own_head():
            b = filled(dve, ("sv",))
            v.tensor_tensor(osel[:], b[:, 0:256].rearrange("p (h d) -> p h d", h=AH),
                            cav("hsel").unsqueeze(2).broadcast_to([128, AH, HD]), ALU.mult).then_inc(bank_free[7], 1)
            emptied(dve, ("sv",))
            v.tensor_reduce(orow[:], osel[:].rearrange("p h d -> p d h"), AX.X, ALU.add).then_inc(o_row, 1)

        def sample_attended_lo():
            dve.wait_ge(os_hi, 1)
            v.tensor_tensor(aol[:, :, SEQ:NTOK], aosf[:], aoh[:, :, SEQ:NTOK].bitcast(F), ALU.subtract).then_inc(os_lo, 1)

        for n in range(KT):
            w_split(S_GA + n + 2)
            if n in (0, 5, 6):
                {0: sample_softmax, 5: sample_own_head, 6: sample_attended_lo}[n]()

        def mix_low(n):
            p = n % 3
            dve.wait_ge(mix_hi, n + 1)
            v.scalar_tensor_tensor(mTl[:, n, :], mtmp[:, p, :], 0.5, mTh[:, n, :].bitcast(F), ALU.mult, ALU.subtract)
            v.scalar_tensor_tensor(mTs[:, n, 32:64], mtmp[:, p, SEQ:NTOK], 0.5, mTh[:, n, SEQ:NTOK].bitcast(F), ALU.mult, ALU.subtract
                                   ).then_inc(mix_lo, 1)

        for n in range(KT):
            if n % 4 == 3:
                dve.wait_ge(w_used, S_BA + n // 4 + 1)
            else:
                dve.wait_ge(branch_done, n - n // 4 + 1)
            p = n % 2
            if n >= 3:
                dve.wait_ge(mix_lo, n - 2)
            gated(n, sga[:, n, :], 2 * p, mtmp[:, n % 3, :], a_free[p])
            if n == 4:
                w_split(S_OUT)
            if n:
                mix_low(n - 1)
        w_split(S_OUT + 1)
        mix_low(KT - 1)
        def half_means(count):
            dve.wait_ge(half_sq, count)
            v.tensor_scalar(ss_h[:, 0:4], ss_h[:, 0:4], 1.0 / D, EPS, ALU.mult, ALU.add)
            v.tensor_scalar(ss_h[0:TS, 4:5], ss_h[0:TS, 4:5], 1.0 / D, EPS, ALU.mult, ALU.add).then_inc(half_bias, 1)

        def scaled(out, x, i, at_, gain, signal):
            r = rows(i)
            rs = rs_n[0:r, at_ + i:at_ + i + 1]
            step(v.reciprocal(rs, rt_n[0:r, at_ + i:at_ + i + 1]))
            src = P[i][:, :] if i < 4 else x[0:r, 4, 512:1024]
            ins = v.scalar_tensor_tensor(out[0:r, 512:1024], src, rs, gain[0:r, 512:1024], ALU.mult, ALU.mult)
            if i < 4:
                ins.then_inc(b_free[i], 1)
            v.scalar_tensor_tensor(out[0:r, 0:512], x[0:r, i, 0:512], rs, gain[0:r, 0:512], ALU.mult, ALU.mult
                                   ).then_inc(signal, 1)

        first, n = BLOCKS[BLK_OUT][:2]
        for s in range(2 * n):
            if s == n - 1:
                sample_sum(BLK_OUT, xo[0:TS, 4, 0:512], ((512, 1.0),), tmp_s2)
            if s == 2 * n - 1:
                half_means(TILES)
                sample_sum(BLK_OUT + 1, xo[0:TS, 4, 512:1024], ((512, 1.0),), tmp_s2)
            else:
                w_split(first + s + 2)
        dve.wait_ge(g2_in, 32)
        def mixed(i):
            dve.wait_ge(n_rt, i + 1)
            if i >= 2:
                dve.wait_ge(x2_ready, i - 1)
            scaled(tmpn[:, i % 2, :], xo, i, 0, gpost, x_scaled)

        def hidden(i):
            r = rows(i)
            dve.wait_ge(n_rt, TILES + i + 1)
            if i >= 2:
                filled(dve, ("h2", i - 2, 1))
            norm_scale(hn[0:r, i % 2, :], xo[0:r, i, :], rt_n[0:r, 5 + i:6 + i], rs_n[0:r, 5 + i:6 + i], gffn[0:r]
                       ).then_inc(h_ready, 1)

        def hidden_lo(i):
            for half in range(2):
                split_evac(("h2", i, half), T1h, T1l, T1s, 4 * half, i)

        for stage, i in ((mixed, 0), (mixed, 1), (hidden, 0), (mixed, 2), (hidden, 1), (hidden_lo, 0), (mixed, 3),
                         (hidden, 2), (hidden_lo, 1), (mixed, 4), (hidden, 3), (hidden_lo, 2), (hidden, 4),
                         (hidden_lo, 3)):
            stage(i)
        w_split(S_UP + 1)
        hidden_lo(4)
        dve.wait_ge(convp_in, 16)
        dve.sem_inc(conv_done, 4)
        dve.sem_inc(f_lo, 1)
        with dve.Fori(0, up_loop) as it:
            for q in range(2):
                for j in range(2):
                    t1 = 2 * q + j + 1
                    dve.wait_ge(w_hi, it * 4 + (S_UP + t1 + 2))
                    v.tensor_tensor(wlo[:, j, :], wraw[:, j, :], whi[:, j, :].bitcast(F), ALU.subtract).then_inc(w_lo, 1)
                    tile = it * 2 + (q + FT * j)
                    cp = convp[:].rearrange("p n c -> p (n c)")
                    tap = lambda k: cp[:, bass.ds(tile * 4 + k, 1)]
                    dve.wait_ge(u_evac[j], it * 2 + (q + 2))
                    dve.wait_ge(head_ready, it * 4 + t1)
                    if j == 0:
                        dve.wait_ge(f_lo, it * 2 + (q + 1))
                    v.tensor_scalar(cb[:, j, 0:CW], ub[:, q, j, 2:UW], tap(2), tap(3), ALU.mult, ALU.add).then_inc(conv_tap, 1)
                    dve.wait_ge(conv_tap, it * 8 + (2 * t1 - 1))
                    v.scalar_tensor_tensor(cb[:, j, 0:CW], ub[:, q, j, 1:UW - 1], tap(1), cb[:, j, 0:CW], ALU.mult, ALU.add
                                           ).then_inc(conv_tap, 1)
                    dve.wait_ge(conv_tap, it * 8 + 2 * t1)
                    v.scalar_tensor_tensor(cb[:, j, 0:CW], ub[:, q, j, 0:UW - 2], tap(0), cb[:, j, 0:CW], ALU.mult, ALU.add
                                           ).then_inc(conv_done, 1)
                pair = it * 2 + q
                dve.wait_ge(gelu_done, it * 2 + (q + 1))
                dve.wait_ge(conv_done, it * 4 + (2 * q + 6))
                v.tensor_tensor(cb[:, 0, 0:CW], cb[:, 0, 0:CW], cb[:, 1, 0:CW], ALU.mult).then_inc(f_done, 1)
                dve.wait_ge(f_hi, it * 2 + (q + 1))
                four = lambda t: t.rearrange("p (b t) -> p b t", t=4)
                hi_s = four(fTh[:, bass.ds(pair * NTOK + SEQ, TS)].bitcast(F))
                v.tensor_tensor(fTl[:, bass.ds(pair * NTOK, SEQ)], cb[:, 0, 0:SEQ], fTh[:, bass.ds(pair * NTOK, SEQ)].bitcast(F),
                                ALU.subtract)
                v.tensor_tensor(four(fTl[:, bass.ds(pair * NTOK + SEQ, TS)]), c_sample(cb[:, 0, :]), hi_s, ALU.subtract)
                v.tensor_tensor(four(fTs[:, bass.ds(pair * 64 + 32, TS)]), c_sample(cb[:, 0, :]), hi_s, ALU.subtract
                                ).then_inc(f_lo, 1)
        def conv_rows(j):
            key = ("cv", j)
            b = filled(dve, key)
            if j >= 2:
                dve.wait_ge(cv_out[j % 2], 32 * (j // 2))
            v.tensor_copy(cvrow[0:18, j % 2, :], b[0:18, :]).then_inc(bank_free[USES[key][0]], 1)

        first, n = BLOCKS[BLK_DN][:2]
        for s in range(2 * n):
            if s == n - 1:
                sample_sum(BLK_DN, fo[0:TS, 4, 0:512], ((512, 1.0),), tmp_s3)
            if s == 2 * n - 1:
                half_means(2 * TILES)
                sample_sum(BLK_DN + 1, fo[0:TS, 4, 512:1024], ((512, 1.0),), tmp_s3)
            if first + s + 2 < NSLOT:
                w_split(first + s + 2)
            if s < 11:
                conv_rows(s)
        dve.wait_ge(gfin_in, 16)
        for i in range(TILES):
            r = rows(i)
            dve.wait_ge(y_rt, i + 1)
            scaled(fo[:, i, :], fo, i, 10, gfin, y_scaled)
            dve.wait_ge(y_scaled, i + 1)
            v.tensor_tensor(fo[0:r, i, 512:1024], fo[0:r, i, 512:1024], xo[0:r, i, 512:1024], ALU.add
                            ).then_inc(y_ready, 1)

    ctx.close()


_INS = ("x_prompt", "x_sample", "cache_kv_g0", "cache_kv_g1", "cache_kv_g2", "state_ret", "norm_mix_pre",
        "norm_mix_post", "norm_ffn_pre", "norm_ffn_post")
_OUTS = (("y_prompt", (1, SEQ, D)), ("y_sample", (NB, DT, D)),
         ("p_kv_g0", (1, 1, 128, 2, AH, HD)), ("p_kv_g1", (1, 1, 512, 2, AH, HD)), ("p_kv_g2", (1, 1, 512, 2, AH, HD)),
         ("p_ret", (1, 1, RH, DK, DV)), ("p_conv", (1, 1, 2, 2 * DFF)),
         ("s_kv_g0", (1, NB, 128, 2, AH, HD)), ("s_kv_g1", (1, NB, 512, 2, AH, HD)), ("s_kv_g2", (1, NB, 2048, 2, AH, HD)),
         ("s_ret", (1, NB, RH, DK, DV)), ("s_conv", (1, NB, 2, 2 * DFF)))


def weight_stream(w_in, w_branch_ret, w_branch_attn, w_out, w_ffn_up, w_ffn_down):
    def b_slots(w, per):
        k, n = w.shape
        return w.reshape(k // (128 * per), per, 128, n).transpose(0, 2, 1, 3).reshape(-1, 128, per * n)

    def a_slots(w):
        k, n = w.shape
        return w.reshape(k // 128, 128, n // 128, 128).transpose(2, 1, 0, 3).reshape(n // 128, 128, k)

    rq, rk, rv, rg, aq, ak, av, gr, ga = np.split(w_in, np.cumsum([512, 512, 1024, 1024, 768, 768, 768, 1024])[:8], axis=1)
    ret = np.concatenate([rq, rk, rv], 1)
    att = np.concatenate([aq, ak, av], 1)
    parts = [b_slots(ret[:, 512 * n:512 * n + 512], 2) for n in range(4)]
    parts += [b_slots(att[:, 512 * n:512 * n + 512], 2) for n in range(4)]
    parts.append(b_slots(att[:, 2048:], 4))
    parts += [b_slots(rg[:, 512 * n:512 * n + 512], 2) for n in range(2)]
    parts.append(np.stack([a_slots(gr), a_slots(w_branch_ret)], 1).reshape(-1, 128, SLOT))
    parts.append(a_slots(ga))
    parts.append(a_slots(w_branch_attn).reshape(2, 4, 128, BA_W).transpose(0, 2, 1, 3).reshape(2, 128, SLOT))
    parts += [b_slots(w_out[:, 512 * n:512 * n + 512], 2) for n in range(2)]
    up = a_slots(w_ffn_up)
    parts.append(np.stack([up[:FT], up[FT:]], 1).reshape(-1, 128, SLOT))
    parts += [b_slots(w_ffn_down[:, 512 * n:512 * n + 512], 2) for n in range(2)]
    return np.concatenate(parts, 0)


def kernel(**inputs):
    import concourse.bacc as bacc
    from concourse.bass_utils import run_bass_kernel_spmd

    inp = {k: np.asarray(x) for k, x in inputs.items()}
    tables, tables_ret = constant_tables()
    arrays = {k: np.ascontiguousarray(inp[k]) for k in _INS}
    arrays["weights"] = weight_stream(*(inp[k][0] for k in ("w_in", "w_branch_ret", "w_branch_attn", "w_out", "w_ffn_up",
                                                            "w_ffn_down")))
    cw = np.concatenate([inp["conv_w"][0], inp["conv_b"]], 0)
    arrays["conv_params"] = np.ascontiguousarray(cw.reshape(4, 2 * FT, 128).transpose(2, 1, 0))
    arrays["conv_state"] = np.ascontiguousarray(
        inp["state_conv"][0].reshape(NB * 2, 2 * FT, 128).transpose(2, 1, 0).reshape(128, -1))
    arrays["tables"], arrays["tables_ret"] = tables, tables_ret

    nc = bacc.Bacc("TRN2", target_bir_lowering=False, num_devices=1)
    f32 = mybir.dt.float32
    a = {k: nc.dram_tensor(f"in_{k}", x.shape, f32, kind="ExternalInput").ap() for k, x in arrays.items()}
    o = {k: nc.dram_tensor(f"out_{k}", shape, f32, kind="ExternalOutput").ap() for k, shape in _OUTS}
    build_layer(nc, a, o)
    r = run_bass_kernel_spmd(nc, [{f"in_{k}": x for k, x in arrays.items()}], core_ids=[0])
    return tuple(r.results[0][f"out_{k}"] for k, _ in _OUTS)
```
